# Optimizing a Trainium2 kernel written in Bass

```python
import math
import jax
import jax.numpy as jnp
from jax import lax
import numpy as np

D_MODEL = 1024
BATCH = 1
SEQ = 128
DEPTH = 2
DEC_BATCH = 1
DEC_SEQ = 256
PAST_LEN = 128

GRID_W = 64
N_EVEN = (DEPTH + 1) // 2
N_ODD = DEPTH // 2
EPS = 1e-6
NEG_INF = -1e30
Q_BLOCK = 128
NA_HEADS = 8
HEAD_DIM = 64
D_A = NA_HEADS * HEAD_DIM
WIN_ROWS_MAX = 8
WIN_COLS = 16
D_B = D_MODEL - D_A
HY_ORDER = 2
HY_SHORT = 3
HY_EMB = 33
HY_BANDS = (HY_EMB - 1) // 2
HY_FFN = 64
HY_DECAY_TARGET = 1e-2
HY_FAST_PCT = 0.3
HY_SLOW_PCT = 1.5
D_RNN = D_MODEL
RG_BLOCKS = 16
RG_BLOCK = D_RNN // RG_BLOCKS
RG_CONV = 4
RG_C = 8.0
N_EXPERTS = 16
N_GROUPS = 4
EXPERTS_PER_GROUP = N_EXPERTS // N_GROUPS
TOP_K = 2
D_EXPERT = 512

kernel_name = 'hybrid_natten_hyena_rglru_moe_step'

def rmsnorm(x, g):
    xf = x.astype(jnp.float32)
    y = xf * lax.rsqrt(jnp.mean(xf * xf, axis=-1, keepdims=True) + EPS)
    return (y * g.astype(jnp.float32)).astype(x.dtype)

def dwconv_centred(x, w, b):
    K = w.shape[0]
    L = x.shape[1]
    left = K // 2
    xp = jnp.pad(x, ((0, 0), (left, K - 1 - left), (0, 0)))
    y = xp[:, 0:L, :] * w[0]
    for j in range(1, K):
        y = y + xp[:, j:j + L, :] * w[j]
    return y + b

def context_attention(q, k, v):
    B, Lc, H, Dh = q.shape
    nblk = Lc // Q_BLOCK
    qb = q.reshape(B, nblk, Q_BLOCK, H, Dh).transpose(1, 0, 2, 3, 4)
    scale = Dh ** -0.5

    def block(q_b):
        s = jnp.einsum('bqhd,bkhd->bhqk', q_b, k).astype(jnp.float32) * scale
        p = jax.nn.softmax(s, axis=-1).astype(v.dtype)
        return jnp.einsum('bhqk,bkhd->bqhd', p, v)

    o = lax.map(block, qb)
    return o.transpose(1, 0, 2, 3, 4).reshape(B, Lc, H * Dh)

def neighbourhood_attention(q, k, v, ctx_k, ctx_v, rpb):
    B, L, H, Dh = q.shape
    rows = L // GRID_W
    kr = min(WIN_ROWS_MAX, rows)
    cols = np.arange(GRID_W)
    col_start = np.clip(cols - WIN_COLS // 2, 0, GRID_W - WIN_COLS)
    col_in = (cols[None, :] >= col_start[:, None]) & (cols[None, :] < col_start[:, None] + WIN_COLS)
    dc = np.clip(cols[None, :] - cols[:, None], 1 - WIN_COLS, WIN_COLS - 1) + WIN_COLS - 1
    row_start = jnp.asarray(np.clip(np.arange(rows) - kr // 2, 0, rows - kr), jnp.int32)
    qg = q.reshape(B, rows, GRID_W, H, Dh).transpose(1, 0, 3, 2, 4)
    kg = k.reshape(B, rows, GRID_W, H, Dh)
    vg = v.reshape(B, rows, GRID_W, H, Dh)
    scale = Dh ** -0.5
    n_lat = kr * GRID_W

    def row_block(args):
        r, start, q_r = args
        k_r = lax.dynamic_slice_in_dim(kg, start, kr, axis=1)
        v_r = lax.dynamic_slice_in_dim(vg, start, kr, axis=1)
        dr = start + jnp.arange(kr) - r + WIN_ROWS_MAX - 1
        bias = rpb[:, dr[None, :, None], dc[:, None, :]].astype(jnp.float32)
        s_lat = jnp.einsum('bhqd,bjkhd->bhqjk', q_r, k_r).astype(jnp.float32) * scale + bias
        s_lat = jnp.where(col_in[:, None, :], s_lat, NEG_INF)
        s_ctx = jnp.einsum('bhqd,bhcd->bhqc', q_r, ctx_k).astype(jnp.float32) * scale
        s = jnp.concatenate([s_lat.reshape(B, H, GRID_W, n_lat), s_ctx], axis=-1)
        p = jax.nn.softmax(s, axis=-1).astype(v.dtype)
        p_lat = p[..., :n_lat].reshape(B, H, GRID_W, kr, GRID_W)
        o = jnp.einsum('bhqjk,bjkhd->bqhd', p_lat, v_r)
        return o + jnp.einsum('bhqc,bhcd->bqhd', p[..., n_lat:], ctx_v)

    o = lax.map(row_block, (jnp.arange(rows, dtype=jnp.int32), row_start, qg))
    return o.transpose(1, 0, 2, 3, 4).reshape(B, L, H * Dh)

def hyena_filters(L, w1, b1, w2, b2, w3, freq):
    t = jnp.linspace(0.0, 1.0, L, dtype=jnp.float32)[:, None]
    w = 2.0 * math.pi * jnp.arange(L, dtype=jnp.float32)[:, None] / L
    f = jnp.linspace(1e-4, HY_BANDS - 1, HY_BANDS, dtype=jnp.float32)[None, :]
    z = jnp.concatenate([t, jnp.cos(f * w), -jnp.sin(f * w)], axis=-1)
    h = jnp.sin(freq[0].astype(jnp.float32) * (z @ w1.astype(jnp.float32) + b1.astype(jnp.float32)))
    h = jnp.sin(freq[1].astype(jnp.float32) * (h @ w2.astype(jnp.float32) + b2.astype(jnp.float32)))
    h = h @ w3.astype(jnp.float32)
    max_decay = math.log(HY_DECAY_TARGET) / HY_FAST_PCT
    min_decay = math.log(HY_DECAY_TARGET) / HY_SLOW_PCT
    deltas = jnp.linspace(min_decay, max_decay, D_B, dtype=jnp.float32)
    decay = jnp.exp(-t * jnp.abs(deltas))
    return h.reshape(L, 2 * HY_ORDER, D_B) * decay[:, None, :]

def causal_fft_conv(u, h):
    L = u.shape[1]
    n = 2 * L
    uf = jnp.fft.rfft(u, n=n, axis=1)
    hf = jnp.fft.rfft(h, n=n, axis=0)
    return jnp.fft.irfft(uf * hf, n=n, axis=1)[:, :L]

def bidir_long_conv(u, h_fwd, h_bwd, d):
    y_f = causal_fft_conv(u, h_fwd)
    y_b = jnp.flip(causal_fft_conv(jnp.flip(u, axis=1), h_bwd), axis=1)
    return y_f + y_b + u * d

def hyena_mixer(u, filt, short_w, short_b, bias_d):
    u = dwconv_centred(u, short_w, short_b)
    parts = jnp.split(u, HY_ORDER + 1, axis=-1)
    z = parts[0].astype(jnp.float32)
    for n in range(HY_ORDER):
        z = parts[n + 1].astype(jnp.float32) * bidir_long_conv(
            z, filt[:, 2 * n], filt[:, 2 * n + 1], bias_d[n].astype(jnp.float32))
    return z.astype(u.dtype)

def lin_combine(e1, e2):
    a1, b1 = e1
    a2, b2 = e2
    return a1 * a2, a2 * b1 + b2

def rglru_scan(x, wa, ba, wx, bx, lam, h0, reverse):
    B, L, _ = x.shape
    xf = x.astype(jnp.float32)
    xb = xf.reshape(B, L, RG_BLOCKS, RG_BLOCK)
    r = jax.nn.sigmoid(jnp.einsum('blnd,nde->blne', xb, wa.astype(jnp.float32)).reshape(B, L, D_RNN)
                       + ba.astype(jnp.float32))
    i = jax.nn.sigmoid(jnp.einsum('blnd,nde->blne', xb, wx.astype(jnp.float32)).reshape(B, L, D_RNN)
                       + bx.astype(jnp.float32))
    log_a = -RG_C * r * jax.nn.softplus(-lam.astype(jnp.float32))
    a = jnp.exp(log_a)
    b = jnp.sqrt(jnp.maximum(-jnp.expm1(2.0 * log_a), 0.0)) * (i * xf)
    first = L - 1 if reverse else 0
    b = b.at[:, first].add(a[:, first] * h0.astype(jnp.float32))
    _, h = lax.associative_scan(lin_combine, (a, b), reverse=reverse, axis=1)
    return h

def moe(h, router_w, router_b, w_gate, w_up, w_down):
    B, L, _ = h.shape
    scores = jax.nn.sigmoid((h @ router_w).astype(jnp.float32))
    sel = scores + router_b.astype(jnp.float32)
    group_score = lax.top_k(sel.reshape(B, L, N_GROUPS, EXPERTS_PER_GROUP), TOP_K)[0].sum(-1)
    best = jnp.argmax(group_score, axis=-1)
    in_group = jnp.repeat(best[..., None] == jnp.arange(N_GROUPS), EXPERTS_PER_GROUP, axis=-1)
    _, idx = lax.top_k(jnp.where(in_group, sel, -jnp.inf), TOP_K)
    w = jnp.take_along_axis(scores, idx, axis=-1)
    w = w / jnp.sum(w, axis=-1, keepdims=True)
    gates = jnp.sum(jax.nn.one_hot(idx, N_EXPERTS, dtype=jnp.float32) * w[..., None], axis=-2)
    hid = jnp.einsum('bld,edf->blef', h, w_gate)
    up = jnp.einsum('bld,edf->blef', h, w_up)
    act = jax.nn.silu(hid) * up * gates[..., None].astype(h.dtype)
    return jnp.einsum('blef,efd->bld', act, w_down)

def setup_inputs(seed: int = 0) -> dict:
    key = jax.random.key(seed)
    ks = iter(jax.random.split(key, 48))

    def nrm(shape, s):
        return jax.random.normal(next(ks), shape, jnp.float32) * s

    D = D_MODEL
    x_prompt = nrm((BATCH, SEQ, D), 1.0)
    x_sample = nrm((DEC_BATCH, DEC_SEQ, D), 1.0)
    cache_k = nrm((DEC_BATCH, N_EVEN, NA_HEADS, PAST_LEN, HEAD_DIM), 1.0)
    cache_v = nrm((DEC_BATCH, N_EVEN, NA_HEADS, PAST_LEN, HEAD_DIM), 1.0)
    state_h = nrm((DEC_BATCH, N_ODD, 2, D_RNN), 0.5)
    c = nrm((DEC_BATCH, D), 1.0)
    c_ctx = nrm((D,), 1.0)
    norm_g = 1.0 + nrm((DEPTH, 2, D), 0.1)
    ada_w = nrm((DEPTH, D, 6 * D), 0.5 * D ** -0.5)
    ada_b = nrm((DEPTH, 6 * D), 0.02)
    final_g = 1.0 + nrm((D,), 0.1)
    a_in_w = nrm((N_EVEN, D, 3 * D_A + 3 * D_B), D ** -0.5)
    a_out_w = nrm((N_EVEN, D_A + D_B, D), (D_A + D_B) ** -0.5)
    na_rpb = nrm((N_EVEN, NA_HEADS, 2 * WIN_ROWS_MAX - 1, 2 * WIN_COLS - 1), 0.1)
    hy_short_w = nrm((N_EVEN, HY_SHORT, 3 * D_B), HY_SHORT ** -0.5)
    hy_short_b = nrm((N_EVEN, 3 * D_B), 0.02)
    hy_w1 = nrm((N_EVEN, HY_EMB, HY_FFN), HY_EMB ** -0.5)
    hy_b1 = nrm((N_EVEN, HY_FFN), 0.1)
    hy_w2 = nrm((N_EVEN, HY_FFN, HY_FFN), HY_FFN ** -0.5)
    hy_b2 = nrm((N_EVEN, HY_FFN), 0.1)
    hy_w3 = nrm((N_EVEN, HY_FFN, 2 * HY_ORDER * D_B), 0.1 * HY_FFN ** -0.5)
    hy_freq = 1.0 + nrm((N_EVEN, 2, HY_FFN), 0.1)
    hy_d = nrm((N_EVEN, HY_ORDER, D_B), 0.1)
    c_in_w = nrm((N_ODD, D, 2 * D_RNN), D ** -0.5)
    c_out_w = nrm((N_ODD, D_RNN, D), D_RNN ** -0.5)
    rg_conv_w = nrm((N_ODD, RG_CONV, D_RNN), RG_CONV ** -0.5)
    rg_conv_b = nrm((N_ODD, D_RNN), 0.02)
    rg_wa = nrm((N_ODD, 2, RG_BLOCKS, RG_BLOCK, RG_BLOCK), RG_BLOCK ** -0.5)
    rg_ba = nrm((N_ODD, 2, D_RNN), 0.1)
    rg_wx = nrm((N_ODD, 2, RG_BLOCKS, RG_BLOCK, RG_BLOCK), RG_BLOCK ** -0.5)
    rg_bx = nrm((N_ODD, 2, D_RNN), 0.1)
    a0 = jax.random.uniform(next(ks), (N_ODD, 2, D_RNN), jnp.float32,
                            minval=0.9 ** (1.0 / RG_C), maxval=0.999 ** (1.0 / RG_C))
    rg_lam = jnp.log(a0) - jnp.log1p(-a0)
    router_w = nrm((D, N_EXPERTS), D ** -0.5)
    router_b = nrm((N_EXPERTS,), 0.01)
    moe_w_gate = nrm((DEPTH, N_EXPERTS, D, D_EXPERT), D ** -0.5)
    moe_w_up = nrm((DEPTH, N_EXPERTS, D, D_EXPERT), D ** -0.5)
    moe_w_down = nrm((DEPTH, N_EXPERTS, D_EXPERT, D), D_EXPERT ** -0.5)
    return {'x_prompt': x_prompt, 'x_sample': x_sample, 'cache_k': cache_k, 'cache_v': cache_v,
            'state_h': state_h, 'c': c, 'c_ctx': c_ctx, 'norm_g': norm_g, 'ada_w': ada_w,
            'ada_b': ada_b, 'final_g': final_g, 'a_in_w': a_in_w, 'a_out_w': a_out_w,
            'na_rpb': na_rpb, 'hy_short_w': hy_short_w, 'hy_short_b': hy_short_b,
            'hy_w1': hy_w1, 'hy_b1': hy_b1, 'hy_w2': hy_w2, 'hy_b2': hy_b2, 'hy_w3': hy_w3,
            'hy_freq': hy_freq, 'hy_d': hy_d, 'c_in_w': c_in_w, 'c_out_w': c_out_w,
            'rg_conv_w': rg_conv_w, 'rg_conv_b': rg_conv_b, 'rg_wa': rg_wa, 'rg_ba': rg_ba,
            'rg_wx': rg_wx, 'rg_bx': rg_bx, 'rg_lam': rg_lam, 'router_w': router_w,
            'router_b': router_b, 'moe_w_gate': moe_w_gate, 'moe_w_up': moe_w_up,
            'moe_w_down': moe_w_down}

def reference(x_prompt, x_sample, cache_k, cache_v, state_h, c, c_ctx, norm_g, ada_w, ada_b,
              final_g, a_in_w, a_out_w, na_rpb, hy_short_w, hy_short_b, hy_w1, hy_b1, hy_w2,
              hy_b2, hy_w3, hy_freq, hy_d, c_in_w, c_out_w, rg_conv_w, rg_conv_b, rg_wa, rg_ba,
              rg_wx, rg_bx, rg_lam, router_w, router_b, moe_w_gate, moe_w_up, moe_w_down):

    def modulation(cond, l):
        m = jax.nn.silu(cond) @ ada_w[l] + ada_b[l]
        return [t[:, None, :] for t in jnp.split(m, 6, axis=-1)]

    def even_mixer(h, e, ctx_k, ctx_v):
        B, L, _ = h.shape
        u = h @ a_in_w[e]
        q, k, v, hy_u = jnp.split(u, [D_A, 2 * D_A, 3 * D_A], axis=-1)
        q = q.reshape(B, L, NA_HEADS, HEAD_DIM)
        k = k.reshape(B, L, NA_HEADS, HEAD_DIM)
        v = v.reshape(B, L, NA_HEADS, HEAD_DIM)
        if ctx_k is None:
            attn = context_attention(q, k, v)
            kv = (k.transpose(0, 2, 1, 3), v.transpose(0, 2, 1, 3))
        else:
            attn = neighbourhood_attention(q, k, v, ctx_k, ctx_v, na_rpb[e])
            kv = None
        filt = hyena_filters(L, hy_w1[e], hy_b1[e], hy_w2[e], hy_b2[e], hy_w3[e], hy_freq[e])
        hy = hyena_mixer(hy_u, filt, hy_short_w[e], hy_short_b[e], hy_d[e])
        return jnp.concatenate([attn, hy], axis=-1) @ a_out_w[e], kv

    def odd_mixer(h, o, h0):
        u = h @ c_in_w[o]
        gate_u, xr = jnp.split(u, 2, axis=-1)
        xr = dwconv_centred(xr, rg_conv_w[o], rg_conv_b[o])
        hf = rglru_scan(xr, rg_wa[o, 0], rg_ba[o, 0], rg_wx[o, 0], rg_bx[o, 0], rg_lam[o, 0], h0[:, 0], False)
        hb = rglru_scan(xr, rg_wa[o, 1], rg_ba[o, 1], rg_wx[o, 1], rg_bx[o, 1], rg_lam[o, 1], h0[:, 1], True)
        y = ((hf + hb) * jax.nn.gelu(gate_u.astype(jnp.float32))).astype(h.dtype)
        final = jnp.stack([hf[:, -1], hb[:, 0]], axis=1).astype(h.dtype)
        return y @ c_out_w[o], final

    x = x_prompt
    cond = c_ctx[None, :]
    k_list, v_list, h_list = [], [], []
    for l in range(DEPTH):
        sh1, sc1, g1, sh2, sc2, g2 = modulation(cond, l)
        h = rmsnorm(x, norm_g[l, 0]) * (1 + sc1) + sh1
        if l % 2 == 0:
            out, kv = even_mixer(h, l // 2, None, None)
            k_list.append(kv[0])
            v_list.append(kv[1])
        else:
            h0 = jnp.zeros((x.shape[0], 2, D_RNN), jnp.float32)
            out, fin = odd_mixer(h, l // 2, h0)
            h_list.append(fin)
        x = x + g1 * out
        h = rmsnorm(x, norm_g[l, 1]) * (1 + sc2) + sh2
        x = x + g2 * moe(h, router_w, router_b, moe_w_gate[l], moe_w_up[l], moe_w_down[l])
    y_prompt = rmsnorm(x, final_g)
    new_k = jnp.stack(k_list, axis=1)
    new_v = jnp.stack(v_list, axis=1)
    new_h = jnp.stack(h_list, axis=1)

    x = x_sample
    for l in range(DEPTH):
        sh1, sc1, g1, sh2, sc2, g2 = modulation(c, l)
        h = rmsnorm(x, norm_g[l, 0]) * (1 + sc1) + sh1
        if l % 2 == 0:
            out, _ = even_mixer(h, l // 2, cache_k[:, l // 2], cache_v[:, l // 2])
        else:
            out, _ = odd_mixer(h, l // 2, state_h[:, l // 2])
        x = x + g1 * out
        h = rmsnorm(x, norm_g[l, 1]) * (1 + sc2) + sh2
        x = x + g2 * moe(h, router_w, router_b, moe_w_gate[l], moe_w_up[l], moe_w_down[l])
    y_sample = rmsnorm(x, final_g)
    return (y_prompt, y_sample, new_k, new_v, new_h)


_drawn_inputs = setup_inputs


def setup_inputs(seed=0):
    import zlib

    import numpy as np

    out = dict(_drawn_inputs(seed))
    spreads = {}
    factors = {'na_rpb': 8.0, 'hy_short_b': 8.0, 'hy_freq': 3.121, 'rg_ba': 3.509}
    for name, (base, spread) in spreads.items():
        noise = np.random.default_rng([zlib.crc32(name.encode()), seed]).standard_normal(out[name].shape)
        drawn = base * np.exp(spread * noise) if base else spread * noise
        out[name] = jnp.asarray(drawn.astype(out[name].dtype))
    for name, factor in factors.items():
        out[name] = (out[name] * factor).astype(out[name].dtype)
    return out
```

```python
import math
from contextlib import ExitStack

import numpy as np
import concourse.bass as bass
from concourse import mybir

FP = mybir.dt.float32
ALU = mybir.AluOpType
ACT = mybir.ActivationFunctionType
AX = mybir.AxisListType

P = 128
D = 1024
KD = D // P
LP, LS = 128, 256
T = LP + LS
TC = T // P
DEPTH = 2
H, DH = 8, 64
DA = H * DH
DB = D - DA
GRID_W, ROWS = 64, 4
WIN_COLS, WIN_ROWS = 16, 8
RPB_C = 2 * WIN_COLS - 1
RPB_R = 2 * WIN_ROWS - 1
EMB, FFN = 33, 64
NE, NG, EPG = 16, 4, 4
F = 512
KF = F // P
EPS = 1e-6
BIG = 1e30
SCALE = DH ** -0.5
TWO_PI = 2 * math.pi
PI1 = 6.28125
PI2 = float(np.float32(TWO_PI - PI1))
ROUND = 12582912.0
SEGS = ((0, LP), (LP, T))
SUBS = ((0, 0, 1), (1, 1, 3))
N_SLICE = 6 * D // 512


def shape_constants():
    c = {}
    ident = np.eye(P, dtype=np.float32)
    sel = np.zeros((P, 2, P), np.float32)
    for j in range(4):
        for k in range(2):
            sel[32 * j + k, k, :] = 1.0
    cols = np.arange(GRID_W)
    start = np.clip(cols - WIN_COLS // 2, 0, GRID_W - WIN_COLS)
    inside = (cols[None, :] >= start[:, None]) & (cols[None, :] < start[:, None] + WIN_COLS)
    mask = np.where(inside, 0.0, -BIG).astype(np.float32)[:, ::-1]
    c["k_const"] = np.concatenate([ident, sel.reshape(P, 2 * P), np.concatenate([mask, mask])], axis=1)
    zs, decs = [], []
    for L in (LP, LS):
        t = np.linspace(0.0, 1.0, L, dtype=np.float32)[:, None]
        w = (2.0 * math.pi * np.arange(L, dtype=np.float32)[:, None] / L).astype(np.float32)
        f = np.linspace(1e-4, 15, 16, dtype=np.float32)[None, :]
        zs.append(np.concatenate([t, np.cos(f * w), -np.sin(f * w)], axis=-1))
        lo, hi = math.log(1e-2) / 1.5, math.log(1e-2) / 0.3
        deltas = np.linspace(lo, hi, DB, dtype=np.float32)
        decs.append(np.exp(-t * np.abs(deltas)))
    c["k_z"] = np.ascontiguousarray(np.concatenate(zs).T.astype(np.float32))
    c["k_decay"] = np.concatenate(decs).astype(np.float32)
    for tag, L in (("p", LP), ("s", LS)):
        n = 2 * L
        t, k = np.arange(L)[:, None], np.arange(L)[None, :]
        ang = 2 * np.pi * ((t * k) % n) / n
        re, im = np.cos(ang), -np.sin(ang)
        im[:, 0] = (-1.0) ** np.arange(L)
        c["k_dft_" + tag] = np.concatenate([re, im], axis=1).astype(np.float32)
        wt = np.full((L, 1), 2.0 / n)
        wt[0] = 1.0 / n
        c["k_idft_" + tag] = np.concatenate([re.T * wt, im.T * wt], axis=0).astype(np.float32)
    return c


SEM_NAMES = """consts_ld x_ld tables_ld hyp_ld w3_ld decay_ld hyrow_ld params_ld rw_ld
silu_c silu_ct par_tr par_ev
f1_mm f1_arg f1_sin f2_mm f2_arg f2_sin filt_mm filt_dec filt_sd filt_d
spec_mm spec_ev spec_fix
ada_ld0 ada_ld1 ada_aux ada_mm ada_row ada_bc ada_mod
norm_ss norm_h norm_h2 norm_rs tr_mm tr_act tr_dve
in_ld0 in_ld1 in_mm in_act in_dve
tok_mm tok_ev
cache_ld bias_ld bias_ok cv_mm cv_ev
u_mm spec_y inv_mm inv_ev
sc_mm sc_ev at_max at_exp at_nrm pt_mm pt_ev pv_mm pv_ev
out_ld out_mm out_ev out_x
rt_mm rt_sig rt_gates
gu_ld0 gu_ld1 dn_ld0 dn_ld1 gu_used0 gu_used1 dn_used0 dn_used1
moe_mm moe_silu moe_act moe_tr moe_actT moe_dn moe_acc moe_zero moe_x
kout_mm kout_ev kv_out
odd_ld0 odd_ld1 odd_mm odd_act odd_dve bd_zero bd_ld rg_mm rg_sig rg_a rg_th rg_b rg_scan sp_e sp_ln rg_lamok
fin_mm fin_ev fin_out odd_y
norm_gl y_ready y_out""".split()


def build(nc, io):
    ctx = ExitStack()
    with ctx:
        def sb(name, cols, rows=P):
            return ctx.enter_context(nc.sbuf_tensor(name, [rows, cols], FP))

        s = {n: ctx.enter_context(nc.semaphore(n)) for n in SEM_NAMES}
        ada_ld, in_ld, odd_ld = (s["ada_ld0"], s["ada_ld1"]), (s["in_ld0"], s["in_ld1"]), (s["odd_ld0"], s["odd_ld1"])
        gu_ld, dn_ld = (s["gu_ld0"], s["gu_ld1"]), (s["dn_ld0"], s["dn_ld1"])
        gu_used, dn_used = (s["gu_used0"], s["gu_used1"]), (s["dn_used0"], s["dn_used1"])

        const = sb("const", 128 + 256 + 64)
        ident, sel, cmask = const[:, 0:128], const[:, 128:384], const[:, 384:448]
        sel = sel.rearrange("p (c m) -> p c m", c=2)
        x = sb("x", TC * D)[:, :].rearrange("p (c d) -> p c d", c=TC)
        h_t = sb("h", TC * D)
        h = h_t[:, :].rearrange("p (c d) -> p c d", c=TC)
        hT_t = sb("hT", KD * T)
        hT = hT_t[:, :].rearrange("p (k t) -> p k t", k=KD)
        catT = hT
        mods_t = sb("mods", 2 * 6 * D)
        mods = mods_t[:, :].rearrange("p (c v d) -> p c v d", c=2, v=6)
        W = sb("W", 24576)
        E = sb("E", 3584)
        c0 = sb("c0", 2048, 1)[:, :].rearrange("p (n s f) -> p n s f", n=2, s=2)
        parH = sb("parH", 48)
        parR = sb("parR", 104)
        scT = sb("scT", 16)
        rw = sb("rw", KD * NE)[:, :].rearrange("p (k e) -> p k e", k=KD)
        small = sb("small", 64)
        hyp = sb("hyp", 4, FFN)
        ss, rstd = small[:, 0:3], small[:, 3:6]
        eps_c = small[:, 6:7]
        s_rg = small[:, 8:24]
        gates = sb("gates", TC * NE)[:, :].rearrange("p (c e) -> p c e", c=TC)
        ps = ctx.enter_context(nc.psum_tensor("ps", [P, 8, 512], FP))

        rows_h, rows_r, rows_c = mods_t[0:48, 0:128], mods_t[0:104, 128:256], mods_t[0:16, 256:384]
        rows_s = mods_t[0:16, 384:512]
        ftmp = mods_t[:, 1024:5120].rearrange("p (b f n) -> p b f n", b=2, f=4)
        d_row = mods_t[0:1, 5120:6144].rearrange("p (n f) -> p n f", n=2)
        hid = mods_t[0:FFN, 6144:6144 + 6 * T].rearrange("p (b t) -> p b t", b=6)
        filt_s = h_t[:, :].rearrange("p (c n f) -> p c n f", c=TC, n=2)
        filt_d = hT_t[:, :].rearrange("p (c n f) -> p c n f", c=TC, n=2)
        w3 = E[0:FFN, 0:2048]
        decay = E[:, 2048:3584].rearrange("p (c f) -> p c f", c=TC)
        ada_w = W[:, 0:12288].rearrange("p (b n) -> p b n", b=2)
        mrow = W[:, 12288:13824].rearrange("p (b n) -> p b n", b=3)
        adab = W[:, 13824:15360].rearrange("p (b n) -> p b n", b=3)
        gt = W[:, 15360:15872]
        z_sb = E[0:EMB, 0:T]
        wblk = W[:, 0:8192].rearrange("p (b k n) -> p b k n", b=2, k=KD)
        qkT = W[:, 8192:11264].rearrange("p (m t) -> p m t", m=8)
        v_tok = W[:, 11264:12800].rearrange("p (c n) -> p c n", c=TC)
        hy2T = W[:, 12800:14336].rearrange("p (m t) -> p m t", m=4)
        ck = W[:, 14336:14848]
        cv = W[:, 14848:15360]
        ckT = W[:, 15360:15872].rearrange("p (m t) -> p m t", m=4)
        dft_s = W[:, 15872:16896].rearrange("p (k f) -> p k f", k=2)
        idft_s = W[:, 16896:17920].rearrange("p (k t) -> p k t", k=4)
        dft_p = W[:, 17920:18176]
        idft_p = W[:, 18176:18432].rearrange("p (k t) -> p k t", k=2)
        spec = W[:, 18432:24576].rearrange("p (n a c f) -> p n a c f", n=2, a=2, c=TC)
        hy01T = [mods_t[:, 6144 * b:6144 * b + 4 * T].rearrange("p (m t) -> p m t", m=4) for b in range(2)]
        hy_tok = h_t[:, :].rearrange("p (c a n) -> p c a n", c=TC, a=2)
        prod = W[:, 0:3072].rearrange("p (a c n) -> p a c n", a=2, c=TC)
        ptmp = W[:, 3072:6144].rearrange("p (a c n) -> p a c n", a=2, c=TC)
        bias = E[:, :].rearrange("p (h r k) -> p h r k", h=H, r=7)
        sc_p = W[:, 15872:16896].rearrange("p (h k) -> p h k", h=H)
        sc_s = W[:, 16896:23040].rearrange("p (q h k) -> p q h k", q=2, h=H)
        ptT = W[:, 0:7168].rearrange("p (j k) -> p j k", k=512)
        amax = W[:, 23040:23064].rearrange("p (q h) -> p q h", q=3)
        asum = W[:, 23064:23088].rearrange("p (q h) -> p q h", q=3)
        arcp = W[:, 23088:23112].rearrange("p (q h) -> p q h", q=3)
        k_tok = W[:, 7168:7680]
        wout = W[:, 0:8192].rearrange("p (k n) -> p k n", k=KD)
        otmp = W[:, 8192:11264].rearrange("p (c d) -> p c d", c=TC)
        geluT = W[:, 8192:11264].rearrange("p (m t) -> p m t", m=8)
        xrT = W[:, 11264:14336].rearrange("p (m t) -> p m t", m=8)
        rr = h_t[:, :].rearrange("p (m t) -> p m t", m=8)
        ri = W[:, 14336:17408].rearrange("p (m t) -> p m t", m=8)
        ra = W[:, 17408:20480].rearrange("p (m t) -> p m t", m=8)
        rt = W[:, 20480:23552].rearrange("p (m t) -> p m t", m=8)
        bd = [mods_t[:, 6144 * d:6144 * d + 2048].rearrange("p (g m n) -> p g m n", g=2, m=8) for d in range(2)]
        spt = W[:, 23552:23552 + 128].rearrange("p (a m) -> p a m", a=8)
        fin_col = W[:, 23680:23696].rearrange("p (d m) -> p d m", d=2)
        fin_row = W[0:16, 23712:23840]
        wg = [W[:, 12288 * b:12288 * b + 4096].rearrange("p (k f) -> p k f", k=KD) for b in range(2)]
        wu = [W[:, 12288 * b + 4096:12288 * b + 8192].rearrange("p (k f) -> p k f", k=KD) for b in range(2)]
        wd = [W[:, 12288 * b + 8192:12288 * b + 12288].rearrange("p (k d) -> p k d", k=KF) for b in range(2)]
        acc = mods[:, 0, 0:3, :]
        mt = mods_t[:, 6144:6144 + 3072].rearrange("p (a b n) -> p a b n", a=3, b=2)
        silu_b, act_b, actT_b = mt[:, 0], mt[:, 1], mt[:, 2]
        R = {n: E[:, 48 * i:48 * i + 48].rearrange("p (c e) -> p c e", c=TC)
                   for i, n in enumerate(["sc", "sel", "msk", "eq", "w", "t1", "t2", "m2", "sm"])}
        pr6 = E[:, 512:512 + 72].rearrange("p (c g o) -> p c g o", c=TC, g=NG)
        gsc, geq, gw, gin = (E[:, 600 + 16 * i:612 + 16 * i].rearrange("p (c g) -> p c g", c=TC) for i in range(4))
        r1, r2 = (E[:, 680 + 8 * i:683 + 8 * i].rearrange("p (c o) -> p c o", c=TC) for i in range(2))
        rbias = E[:, 704:720]
        rank16 = E[:, 720:736]
        fing = mods[:, 0, 5, :]

        block = ctx.enter_context(nc.Block())
        w_in = io["a_in_w"][0].rearrange("(k p) n -> p k n", p=P)
        w_cin = io["c_in_w"][0].rearrange("(k p) n -> p k n", p=P)
        w_aout = io["a_out_w"][0].rearrange("(k p) n -> p k n", p=P)
        w_cout = io["c_out_w"][0].rearrange("(k p) n -> p k n", p=P)
        wg_d = io["moe_w_gate"].rearrange("l e (k p) f -> (l e) p k f", p=P)
        wu_d = io["moe_w_up"].rearrange("l e (k p) f -> (l e) p k f", p=P)
        wd_d = io["moe_w_down"].rearrange("l e (k p) d -> (l e) p k d", p=P)
        IN_ORDER = (3, 4, 5, 0, 1, 2)
        ODD_ORDER = (2, 3, 0, 1)
        NBODY = NE // 2
        BT = 2 * TC

        @block.sync
        def _(sp):
            sp.dma_start(const[:, :], io["k_const"]).then_inc(s["consts_ld"], 16)
            sp.dma_start(rows_c[0:8, :], io["c_ctx"].rearrange("(k p) -> k p", p=P)).then_inc(s["params_ld"], 16)
            sp.dma_start(rows_c[8:16, :], io["c"][0].rearrange("(k p) -> k p", p=P)).then_inc(s["params_ld"], 16)
            sp.dma_start(rows_h[0:36, :], io["hy_short_w"][0].rearrange("j (c p) -> (j c) p", p=P)).then_inc(s["params_ld"], 16)
            sp.dma_start(rows_h[36:48, :], io["hy_short_b"][0].rearrange("(c p) -> c p", p=P)).then_inc(s["params_ld"], 16)
            sp.dma_start(rows_r[0:32, :], io["rg_conv_w"][0].rearrange("j (c p) -> (j c) p", p=P)).then_inc(s["params_ld"], 16)
            sp.dma_start(rows_r[32:40, :], io["rg_conv_b"][0].rearrange("(c p) -> c p", p=P)).then_inc(s["params_ld"], 16)
            for i, n in enumerate(("rg_ba", "rg_bx", "rg_lam", "state_h")):
                sp.dma_start(rows_r[40 + 16 * i:56 + 16 * i, :],
                             io[n][0].rearrange("d (c p) -> (d c) p", p=P) if n != "state_h"
                             else io[n][0, 0].rearrange("d (c p) -> (d c) p", p=P)).then_inc(s["params_ld"], 16)
            sp.dma_start(x[:, 0, :], io["x_prompt"][0]).then_inc(s["x_ld"], 16)
            sp.dma_start(x[:, 1:3, :], io["x_sample"][0].rearrange("(c p) d -> p c d", p=P)).then_inc(s["x_ld"], 16)

            def ada(l):
                if l == 1:
                    sp.wait_ge(s["moe_dn"], NBODY * BT + 2)
                for k in range(KD):
                    if k >= 2:
                        sp.wait_ge(s["ada_mm"], KD * l + k - 1)
                    sp.dma_start(ada_w[:, k % 2, :], io["ada_w"][l, k * P:(k + 1) * P, :]).then_inc(ada_ld[k % 2], 16)

            def in_blocks(src, order, sems, mm, per):
                for i, nb in enumerate(order):
                    if i >= 2:
                        sp.wait_ge(mm, per[i - 2])
                    sp.dma_start(wblk[:, i % 2], src[:, :, nb * 512:(nb + 1) * 512]).then_inc(sems[i % 2], 16)

            def experts(l):
                sp.wait_ge(s["out_mm"], 6 * (l + 1))
                sp.wait_ge(s["out_x"], l + 1)
                if l == 1:
                    sp.wait_ge(s["fin_out"], 16)
                with sp.Fori(0, NBODY) as i:
                    for b in range(2):
                        e = i * 2 + (NE * l + b)
                        sp.wait_ge(gu_used[b], i + (NBODY * l + 1))
                        sp.dma_start(wg[b], wg_d[e]).then_inc(gu_ld[b], 16)
                        sp.dma_start(wu[b], wu_d[e]).then_inc(gu_ld[b], 16)
                        sp.wait_ge(dn_used[b], i + (NBODY * l + 1))
                        sp.dma_start(wd[b], wd_d[e]).then_inc(dn_ld[b], 16)

            ada(0)
            sp.wait_ge(s["ada_mm"], KD)
            in_blocks(w_in, IN_ORDER, in_ld, s["in_mm"], (4, 8, 12, 16, 20, 23))
            sp.wait_ge(s["pv_mm"], 24)
            sp.wait_ge(s["kv_out"], 32)
            for k in range(2):
                sp.dma_start(wout[:, 4 * k:4 * k + 4, :], w_aout[:, 4 * k:4 * k + 4, :]).then_inc(s["out_ld"], 16)
            experts(0)
            ada(1)
            sp.wait_ge(s["ada_mm"], 2 * KD)
            in_blocks(w_cin, ODD_ORDER, odd_ld, s["odd_mm"], (4, 8, 12, 16))
            sp.wait_ge(s["odd_mm"], 16)
            for k in range(2):
                sp.dma_start(wout[:, 4 * k:4 * k + 4, :], w_cout[:, 4 * k:4 * k + 4, :]).then_inc(s["out_ld"], 16)
            experts(1)
            sp.wait_ge(s["y_ready"], 3)
            sp.dma_start(io["y_prompt"][0], h[:, 0, :]).then_inc(s["y_out"], 16)
            sp.dma_start(io["y_sample"][0].rearrange("(c p) d -> p c d", p=P), h[:, 1:3, :]).then_inc(s["y_out"], 16)
            sp.wait_ge(s["y_out"], 32)
            sp.wait_ge(s["kv_out"], 32)
            sp.wait_ge(s["fin_out"], 16)

        @block.gpsimd
        def _(pool):
            gp = nc.gpsimd
            pool.dma_start(z_sb, io["k_z"]).then_inc(s["hyp_ld"], 16)
            for i, src in enumerate((io["hy_b1"][0], io["hy_b2"][0], io["hy_freq"][0, 0], io["hy_freq"][0, 1])):
                pool.dma_start(hyp[:, i:i + 1], src.rearrange("(p o) -> p o", o=1)).then_inc(s["hyp_ld"], 16)
            pool.dma_start(hid[0:EMB, 5, 0:FFN], io["hy_w1"][0]).then_inc(s["hyp_ld"], 16)
            pool.dma_start(hid[:, 5, 64:128], io["hy_w2"][0]).then_inc(s["hyp_ld"], 16)
            pool.dma_start(d_row, io["hy_d"][0:1]).then_inc(s["hyrow_ld"], 16)
            pool.dma_start(decay, io["k_decay"].rearrange("(c p) f -> p c f", p=P)).then_inc(s["decay_ld"], 16)
            pool.dma_start(dft_s, io["k_dft_s"].rearrange("(k p) f -> p k f", p=P)).then_inc(s["tables_ld"], 16)
            pool.dma_start(dft_p, io["k_dft_p"]).then_inc(s["tables_ld"], 16)
            pool.dma_start(idft_s, io["k_idft_s"].rearrange("(k p) f -> p k f", p=P)).then_inc(s["tables_ld"], 16)
            pool.dma_start(idft_p, io["k_idft_p"].rearrange("(k p) f -> p k f", p=P)).then_inc(s["tables_ld"], 16)
            pool.dma_start(rw, io["router_w"].rearrange("(k p) e -> p k e", p=P)).then_inc(s["rw_ld"], 16)

            def ada_aux(l):
                for c in range(2):
                    for j in range(4):
                        pool.dma_start(adab[32 * j + c:32 * j + c + 1], io["ada_b"][l:l + 1].rearrange(
                            "o (b j n) -> o j b n", b=3, j=4)[:, j]).then_inc(s["ada_aux"], 16)
                    for j, (v, half) in enumerate(((1, 0), (1, 1), (0, 0), (0, 1))):
                        pool.dma_start(gt[32 * j + c:32 * j + c + 1, :],
                                       io["norm_g"][l, v:v + 1, half * 512:half * 512 + 512]).then_inc(s["ada_aux"], 16)

            ada_aux(0)
            pool.wait_ge(s["f1_mm"], 1)
            pool.dma_start(w3, io["hy_w3"][0]).then_inc(s["w3_ld"], 16)
            for c in range(TC):
                pool.wait_ge(s["filt_dec"], 4 * c + 4)
                for n in range(2):
                    f0, f1 = ftmp[:, c % 2, 2 * n, :], ftmp[:, c % 2, 2 * n + 1, :]
                    gp.tensor_tensor(filt_s[:, c, n, :], f0, f1, ALU.add)
                    gp.tensor_tensor(filt_d[:, c, n, :], f0, f1, ALU.subtract).then_inc(s["filt_sd"], 1)
            pool.wait_ge(s["hyrow_ld"], 16)
            pool.wait_ge(s["filt_sd"], 6)
            for c in range(2):
                gp.tensor_tensor(filt_s[0:1, c, :, :], filt_s[0:1, c, :, :], d_row, ALU.add).then_inc(s["filt_d"], 1)
            pool.wait_ge(s["spec_ev"], 16)
            for n in range(2):
                gp.memset(spec[0:1, n, 1, 0:2, :], 0.0).then_inc(s["spec_fix"], 1)

            pool.wait_ge(s["filt_dec"], 12)
            rpb = io["na_rpb"]
            for up in range(2):
                for hh in range(H):
                    off = hh * RPB_R * RPB_C + (WIN_ROWS - 4 - up) * RPB_C + WIN_COLS - GRID_W
                    src = bass.AP(tensor=rpb.tensor, offset=off, ap=[[1, GRID_W], [RPB_C, 7], [1, GRID_W]])
                    pool.dma_start(bias[64 * up:64 * up + 64, hh], src).then_inc(s["bias_ld"], 16)
            pool.wait_ge(s["ada_row"], 3)
            pool.wait_ge(s["ada_bc"], N_SLICE * 2)
            pool.dma_start(ck.rearrange("p (h d) -> p h d", h=H), io["cache_k"][0, 0].rearrange("h t d -> t h d")).then_inc(s["cache_ld"], 16)
            pool.dma_start(cv.rearrange("p (h d) -> p h d", h=H), io["cache_v"][0, 0].rearrange("h t d -> t h d")).then_inc(s["cache_ld"], 16)
            pool.wait_ge(s["bias_ld"], 16 * 16)
            for hh in range(H):
                b3 = bias[:, hh]
                gp.tensor_tensor(b3, b3, cmask[:, None, :].broadcast_to([P, 7, GRID_W]), ALU.add).then_inc(s["bias_ok"], 1)

            def shift(i, lo):
                for n, (cond, c0_, c1_) in enumerate(SUBS):
                    for c in range(c0_, c1_):
                        pool.wait_ge(s["norm_h"], 3 * i + c + 1)
                        gp.tensor_tensor(h[:, c, :], h[:, c, :], mods[:, cond, lo, :], ALU.add).then_inc(s["norm_h2"], 1)

            def residual(n_done, sem_in, done):
                for c in range(TC):
                    pool.wait_ge(sem_in, n_done + 2 * c + 2)
                    gp.tensor_tensor(x[:, c, :], x[:, c, :], otmp[:, c, :], ALU.add)
                pool.drain().then_inc(done, 1)

            def moe_pool(l):
                pool.dma_start(rbias, io["router_b"].rearrange("(o e) -> o e", o=1).broadcast_to([P, NE])).then_inc(s["rw_ld"], 16)
                for e in range(NE):
                    gp.memset(rank16[:, e:e + 1], float(NE - e))
                gp.memset(acc, 0.0)
                pool.drain().then_inc(s["moe_zero"], 1)

            shift(0, 0)
            residual(0, s["out_ev"], s["out_x"])
            shift(1, 3)
            moe_pool(0)
            pool.wait_ge(s["moe_x"], 1)
            ada_aux(1)
            pool.wait_ge(s["ada_mod"], N_SLICE * 4)
            shift(2, 0)
            pool.wait_ge(s["tr_mm"], 6 * 3)
            for d in range(2):
                gp.memset(bd[d], 0.0).then_inc(s["bd_zero"], 1)
            pool.wait_ge(s["bd_zero"], 2)
            for d in range(2):
                for g, n in enumerate(("rg_wa", "rg_wx")):
                    src = io[n][0, d].rearrange("(m u) i j -> u i m j", u=2)
                    for u in range(2):
                        pool.dma_start(bd[d][64 * u:64 * u + 64, g, :, 64 * u:64 * u + 64], src[u]).then_inc(s["bd_ld"], 16)
            residual(6, s["out_ev"], s["out_x"])
            shift(3, 3)
            moe_pool(1)
            pool.wait_ge(s["moe_x"], 2)
            pool.dma_start(fing, io["final_g"].rearrange("(o d) -> o d", o=1).broadcast_to([P, D])).then_inc(s["norm_gl"], 16)

        @block.tensor
        def _(pe):
            def mm(out, pairs):
                for i, (a, b) in enumerate(pairs):
                    last = nc.tensor.matmul(out, a, b, start=(i == 0), stop=(i == len(pairs) - 1))
                return last

            pe.wait_ge(s["consts_ld"], 16)
            pe.wait_ge(s["params_ld"], 10 * 16)
            nc.tensor.transpose(ps[:, 0, 0:48], rows_h, ident[0:48, 0:48])
            nc.tensor.transpose(ps[:, 0, 64:168], rows_r, ident[0:104, 0:104])
            pe.wait_ge(s["silu_c"], 1)
            nc.tensor.transpose(ps[:, 0, 192:208], rows_s, ident[0:16, 0:16]).then_inc(s["par_tr"], 1)
            pe.wait_ge(s["hyp_ld"], 7 * 16)
            nc.tensor.matmul(ps[0:FFN, 1, 0:T], hid[0:EMB, 5, 0:FFN], z_sb, start=True, stop=True).then_inc(s["f1_mm"], 1)
            pe.wait_ge(s["f1_sin"], 1)
            nc.tensor.matmul(ps[0:FFN, 2, 0:T], hid[:, 5, 64:128], hid[:, 3, :], start=True, stop=True).then_inc(s["f2_mm"], 1)
            pe.wait_ge(s["f2_sin"], 1)
            pe.wait_ge(s["w3_ld"], 16)
            pe.wait_ge(s["par_ev"], 1)
            for c in range(TC):
                for f in range(4):
                    t = 4 * c + f
                    if t >= 8:
                        pe.wait_ge(s["filt_dec"], t - 7)
                    mm(ps[:, t % 8, :], [(hid[:, 4, c * P:(c + 1) * P], w3[:, f * 512:(f + 1) * 512])]).then_inc(s["filt_mm"], 1)
            pe.wait_ge(s["tables_ld"], 4 * 16)
            pe.wait_ge(s["filt_dec"], 12)
            pe.wait_ge(s["filt_d"], 2)
            t = 0
            for n in range(2):
                for src, col, c in ((0, 0, 1), (0, 128, 2), (0, 0, 0), (1, 256, 1), (1, 384, 2), (1, 128, 0), (2, 256, 1), (2, 128, 0)):
                    filt = filt_d if src == 1 else filt_s
                    m = 1 if src == 2 else P
                    if t >= 8:
                        pe.wait_ge(s["spec_ev"], t - 7)
                    pairs = ([(dft_p[:, col:col + m], filt[:, 0, n, :])] if c == 0 else
                             [(dft_s[:, k, col:col + m], filt[:, 1 + k, n, :]) for k in range(2)])
                    mm(ps[0:m, t % 8, :], pairs).then_inc(s["spec_mm"], 1)
                    t += 1

            def ada(l):
                for k in range(KD):
                    pe.wait_ge(ada_ld[k % 2], 16 * (l * KD // 2 + k // 2 + 1))
                    lhs = scT[:, :].rearrange("p (c k) -> p k c", c=2)[:, k, :]
                    for n in range(N_SLICE):
                        b, j = divmod(n, 4)
                        last = nc.tensor.matmul(ps[32 * j:32 * j + 2, b, :], lhs, ada_w[:, k % 2, n * 512:(n + 1) * 512],
                                                start=(k == 0), stop=(k == KD - 1))
                    last.then_inc(s["ada_mm"], 1)
                pe.wait_ge(s["ada_row"], 3 * l + 3)
                t = 0
                for c in range(2):
                    for n in range(N_SLICE):
                        b, j = divmod(n, 4)
                        if t >= 5:
                            pe.wait_ge(s["ada_mod"], 2 * N_SLICE * l + t - 4)
                        nc.tensor.matmul(ps[:, 3 + t % 5, :], sel[32 * j:32 * j + 2, c, :], mrow[32 * j:32 * j + 2, b, :],
                                         start=True, stop=True).then_inc(s["ada_bc"], 1)
                        t += 1

            def transposes(i):
                for c in range(TC):
                    pe.wait_ge(s["norm_h2"], 3 * i + c + 1)
                    for half in range(2):
                        for k in range(4):
                            last = nc.tensor.transpose(ps[:, 2 * c + half, k * P:(k + 1) * P],
                                                       h[:, c, (4 * half + k) * P:(4 * half + k + 1) * P], ident)
                        last.then_inc(s["tr_mm"], 1)
                pe.wait_ge(s["tr_act"], 3 * i + 3)
                pe.wait_ge(s["tr_dve"], 3 * i + 3)

            def out_proj(l):
                pe.wait_ge(s["out_ld"], 32 * (l + 1))
                for t in range(6):
                    c, half = divmod(t, 2)
                    mm(ps[:, t, :], [(catT[:, k, c * P:(c + 1) * P], wout[:, k, half * 512:(half + 1) * 512])
                                     for k in range(KD)]).then_inc(s["out_mm"], 1)

            def moe(l):
                pe.wait_ge(s["rw_ld"], 16 * (l + 2))
                for c in range(TC):
                    m_ = mm(ps[:, c, 0:NE], [(hT[:, k, c * P:(c + 1) * P], rw[:, k, :]) for k in range(KD)])
                m_.then_inc(s["rt_mm"], 1)
                pe.wait_ge(s["rt_sig"], l + 1)
                with pe.Fori(0, NBODY) as i:
                    base = i * BT + (NBODY * BT * l)

                    def gate_up(t):
                        b, c = divmod(t, TC)
                        if c == 0:
                            pe.wait_ge(gu_ld[b], i * 32 + (32 * (NBODY * l + 1)))
                        pe.wait_ge(s["moe_act"], base + (t + 1))
                        for w, bank in ((wg[b], 2 * (t % 2)), (wu[b], 2 * (t % 2) + 1)):
                            last = mm(ps[:, bank, :], [(hT[:, k, c * P:(c + 1) * P], w[:, k, :]) for k in range(KD)])
                        last.then_inc(s["moe_mm"], 1)
                        if c == TC - 1:
                            pe.drain().then_inc(gu_used[b], 1)

                    def down(t):
                        b, c = divmod(t, TC)
                        pe.wait_ge(s["moe_act"], base + (t + 3))
                        pe.wait_ge(s["moe_actT"], base + (t + 1))
                        for k in range(KF):
                            last = nc.tensor.transpose(ps[:, 4 + t % 2, k * P:(k + 1) * P],
                                                       act_b[:, t % 2, k * P:(k + 1) * P], ident)
                        last.then_inc(s["moe_tr"], 1)
                        if c == 0:
                            pe.wait_ge(dn_ld[b], i * 16 + (16 * (NBODY * l + 1)))
                        pe.wait_ge(s["moe_actT"], base + (t + 3))
                        pe.wait_ge(s["moe_acc"], base + (t + 1))
                        for half in range(2):
                            last = mm(ps[:, 6 + half, :], [(actT_b[:, t % 2, k * P:(k + 1) * P],
                                                            wd[b][:, k, half * 512:(half + 1) * 512]) for k in range(KF)])
                        last.then_inc(s["moe_dn"], 1)
                        if c == TC - 1:
                            pe.drain().then_inc(dn_used[b], 1)

                    for t in range(BT):
                        gate_up(t)
                        if t:
                            down(t - 1)
                    down(BT - 1)

            for b in range(2):
                pe.sem_inc(gu_used[b], 1)
                pe.sem_inc(dn_used[b], 1)
            pe.sem_inc(s["moe_tr"], 2)
            pe.sem_inc(s["moe_dn"], 2)

            pe.wait_ge(s["spec_ev"], 16)
            ada(0)
            pe.wait_ge(s["ada_mod"], 2 * N_SLICE)
            transposes(0)
            t = 0
            for i, nb in enumerate(IN_ORDER):
                pe.wait_ge(in_ld[i % 2], 16 * (i // 2 + 1))
                for m in range(3 if nb == 2 else 4):
                    if t >= 8:
                        u = t - 8
                        if u < 12:
                            pe.wait_ge(s["in_dve"], u + 1)
                        else:
                            pe.wait_ge(s["in_act"], u + 1)
                    if nb == 2:
                        mm(ps[:, t % 8, :], [(hT[:, k, m * P:(m + 1) * P], wblk[:, i % 2, k, :]) for k in range(KD)]).then_inc(s["in_mm"], 1)
                    else:
                        mm(ps[:, t % 8, 0:T], [(wblk[:, i % 2, k, m * P:(m + 1) * P], hT[:, k, :]) for k in range(KD)]).then_inc(s["in_mm"], 1)
                    t += 1
            pe.wait_ge(s["in_act"], 23)
            for c in range(TC):
                for a in range(2):
                    for m in range(4):
                        last = nc.tensor.transpose(ps[:, 2 * c + a, m * P:(m + 1) * P], hy01T[a][:, m, c * P:(c + 1) * P], ident)
                    last.then_inc(s["tok_mm"], 1)
            pe.wait_ge(s["cache_ld"], 32)
            for m in range(4):
                last = nc.tensor.transpose(ps[:, 6, m * P:(m + 1) * P], ck[:, m * P:(m + 1) * P], ident)
            last.then_inc(s["cv_mm"], 1)
            for m in range(4):
                last = nc.tensor.transpose(ps[:, 7, m * P:(m + 1) * P], qkT[:, 4 + m, 0:P], ident)
            last.then_inc(s["cv_mm"], 1)
            pe.wait_ge(s["tok_ev"], 6)
            pe.wait_ge(s["cv_ev"], 2)
            pe.wait_ge(s["spec_fix"], 2)
            for n in range(2):
                if n == 1:
                    pe.wait_ge(s["inv_ev"], 3)
                for a in range(2):
                    for c in range(TC):
                        if c == 0:
                            pairs = [(dft_p[:, a * 128:a * 128 + 128], hy_tok[:, 0, 0, :])]
                        else:
                            col = 256 * a + 128 * (c - 1)
                            pairs = [(dft_s[:, k, col:col + 128], hy_tok[:, 1 + k, 0, :]) for k in range(2)]
                        mm(ps[:, 3 * a + c, :], pairs).then_inc(s["u_mm"], 1)
                pe.wait_ge(s["spec_y"], n + 1)
                if n == 0:
                    for c in range(TC):
                        if c == 0:
                            pairs = [(idft_p[:, a, :], prod[:, a, 0, :]) for a in range(2)]
                        else:
                            pairs = [(idft_s[:, 2 * a + k, (c - 1) * P:c * P], prod[:, a, 1 + k, :])
                                     for a in range(2) for k in range(2)]
                        mm(ps[:, c, :], pairs).then_inc(s["inv_mm"], 1)
                else:
                    for m in range(4):
                        ch = slice(m * P, (m + 1) * P)
                        mm(ps[:, m, 0:LP], [(prod[:, a, 0, ch], idft_p[:, a, :]) for a in range(2)])
                        mm(ps[:, m, LP:T], [(prod[:, a, 1 + k, ch], idft_s[:, 2 * a + k, :])
                                            for a in range(2) for k in range(2)]).then_inc(s["inv_mm"], 1)
            pe.wait_ge(s["inv_ev"], 7)
            for hh in range(H):
                r0 = 64 * (hh % 2)
                rows = slice(r0, r0 + 64)
                for q in range(3):
                    t = 3 * hh + q
                    if t >= 8:
                        pe.wait_ge(s["sc_ev"], t - 7)
                    lhs = qkT[rows, hh // 2, q * P:(q + 1) * P]
                    if q == 0:
                        last = mm(ps[:, t % 8, 0:P], [(lhs, qkT[rows, 4 + hh // 2, 0:P])])
                    else:
                        mm(ps[:, t % 8, 0:LS], [(lhs, qkT[rows, 4 + hh // 2, LP:T])])
                        last = mm(ps[:, t % 8, LS:T], [(lhs, ckT[rows, hh // 2, :])])
                    last.then_inc(s["sc_mm"], 1)
            pe.wait_ge(s["sc_ev"], 24)
            pe.wait_ge(s["at_nrm"], 3)
            for j in range(14):
                if j >= 8:
                    pe.wait_ge(s["pt_ev"], j - 7)
                for k in range(4):
                    hh, i = divmod(4 * j + k, 7)
                    src = (sc_p[:, hh, :] if i == 0 else
                           sc_s[:, (i - 1) // 3, hh, ((i - 1) % 3) * P:((i - 1) % 3 + 1) * P])
                    last = nc.tensor.transpose(ps[:, j % 8, k * P:(k + 1) * P], src, ident)
                last.then_inc(s["pt_mm"], 1)
            pe.wait_ge(s["pt_ev"], 14)

            def pt(hh, i):
                j, k = divmod(7 * hh + i, 4)
                return ptT[:, j, k * P:(k + 1) * P]

            for hh in range(H):
                r0 = 64 * (hh % 2)
                cols = slice(hh * DH, (hh + 1) * DH)
                for q in range(3):
                    t = 3 * hh + q
                    if t >= 8:
                        pe.wait_ge(s["pv_ev"], t - 7)
                    if q == 0:
                        pairs = [(v_tok[:, 0, cols], pt(hh, 0))]
                    else:
                        pairs = [(v_tok[:, 1, cols], pt(hh, 3 * q - 2)), (v_tok[:, 2, cols], pt(hh, 3 * q - 1)),
                                 (cv[:, cols], pt(hh, 3 * q))]
                    mm(ps[r0:r0 + 64, t % 8, 0:P], pairs).then_inc(s["pv_mm"], 1)
            pe.wait_ge(s["pv_ev"], 24)
            out_proj(0)
            pe.wait_ge(s["out_ev"], 6)
            transposes(1)
            moe(0)
            pe.wait_ge(s["moe_x"], 1)
            ada(1)
            pe.wait_ge(s["ada_mod"], 4 * N_SLICE)
            transposes(2)
            t = 0
            for i, nb in enumerate(ODD_ORDER):
                pe.wait_ge(odd_ld[i % 2], 16 * (i // 2 + 1))
                for m in range(4):
                    if t >= 8:
                        pe.wait_ge(s["odd_dve"], t - 7)
                    mm(ps[:, t % 8, 0:T], [(wblk[:, i % 2, k, m * P:(m + 1) * P], hT[:, k, :]) for k in range(KD)]).then_inc(s["odd_mm"], 1)
                    t += 1
            pe.wait_ge(s["odd_act"], 16)
            pe.wait_ge(s["bd_ld"], 8 * 16)
            t = 0
            for d in range(2):
                for g in range(2):
                    for m in range(8):
                        if t >= 8:
                            pe.wait_ge(s["rg_sig"], t - 7)
                        mm(ps[:, t % 8, 0:T], [(bd[d][:, g, m, :], xrT[:, m, :])]).then_inc(s["rg_mm"], 1)
                        t += 1
            pe.wait_ge(s["rg_sig"], 32)
            pe.wait_ge(s["odd_y"], 1)
            nc.tensor.transpose(ps[0:16, 6, 0:P], fin_col.rearrange("p d m -> p (d m)"), ident).then_inc(s["fin_mm"], 1)
            out_proj(1)
            pe.wait_ge(s["out_ev"], 12)
            transposes(3)
            moe(1)

        @block.scalar
        def _(act):
            A = nc.scalar.activation
            act.wait_ge(s["params_ld"], 10 * 16)
            A(rows_s, rows_c, ACT.Silu).then_inc(s["silu_c"], 1)
            act.wait_ge(s["f1_arg"], 1)
            A(hid[:, 3, :], hid[:, 0, :], ACT.Sin).then_inc(s["f1_sin"], 1)
            act.wait_ge(s["f2_arg"], 1)
            A(hid[:, 4, :], hid[:, 0, :], ACT.Sin).then_inc(s["f2_sin"], 1)
            t = 0
            for n in range(2):
                for dst in (spec[:, n, 0, 1, :], spec[:, n, 0, 2, :], spec[:, n, 0, 0, :],
                            spec[:, n, 1, 1, :], spec[:, n, 1, 2, :], spec[:, n, 1, 0, :],
                            c0[:, n, 1, :], c0[:, n, 0, :]):
                    act.wait_ge(s["spec_mm"], t + 1)
                    A(dst, ps[0:dst.shape[0], t % 8, :], ACT.Copy).then_inc(s["spec_ev"], 1)
                    t += 1

            def modulation(l):
                t = 0
                for c in range(2):
                    for n in range(N_SLICE):
                        act.wait_ge(s["ada_bc"], 2 * N_SLICE * l + t + 1)
                        A(mods_t[:, c * 6 * D + n * 512:c * 6 * D + (n + 1) * 512], ps[:, 3 + t % 5, :], ACT.Copy).then_inc(s["ada_mod"], 1)
                        t += 1

            def sumsq(i):
                for c in range(TC):
                    A(h[:, c, :], x[:, c, :], ACT.Square, accum_out=ss[:, c:c + 1])
                act.drain()
                A(rstd, ss, ACT.Sqrt, bias=eps_c, scale=1.0 / D).then_inc(s["norm_ss"], 1)

            def transposed(i):
                for c in range(TC):
                    act.wait_ge(s["tr_mm"], 6 * i + 2 * c + 1)
                    A(hT[:, 0:4, c * P:(c + 1) * P], ps[:, 2 * c, :].rearrange("p (k t) -> p k t", k=4), ACT.Copy).then_inc(s["tr_act"], 1)

            def moe(l):
                act.wait_ge(s["rt_mm"], l + 1)
                A(R["sc"], ps[:, 0:TC, 0:NE], ACT.Sigmoid).then_inc(s["rt_sig"], 1)
                with act.Fori(0, NBODY) as i:
                    base = i * BT + (NBODY * BT * l)

                    def silu(t):
                        act.wait_ge(s["moe_mm"], base + (t + 1))
                        act.wait_ge(s["moe_act"], base + (t + 1))
                        A(silu_b[:, t % 2, :], ps[:, 2 * (t % 2), :], ACT.Silu).then_inc(s["moe_silu"], 1)

                    def down(t):
                        act.wait_ge(s["moe_tr"], base + (t + 3))
                        act.wait_ge(s["moe_dn"], base + (t + 1))
                        A(actT_b[:, t % 2, :], ps[:, 4 + t % 2, :], ACT.Copy).then_inc(s["moe_actT"], 1)

                    for t in range(BT):
                        silu(t)
                        if t:
                            down(t - 1)
                    down(BT - 1)

            act.sem_inc(s["moe_actT"], 2)
            modulation(0)
            act.wait_ge(s["x_ld"], 32)
            act.wait_ge(s["spec_mm"], 16)
            act.wait_ge(s["par_ev"], 2)
            sumsq(0)
            transposed(0)
            for t in range(23):
                act.wait_ge(s["in_mm"], t + 1)
                if t < 12:
                    dst = hy01T[t // 4][:, t % 4, :] if t < 8 else hy2T[:, t - 8, :]
                    A(dst, ps[:, t % 8, 0:T], ACT.Identity, bias=parH[:, 36 + t:37 + t], scale=parH[:, 12 + t:13 + t]).then_inc(s["in_act"], 1)
                elif t < 20:
                    A(qkT[:, t - 12, :], ps[:, t % 8, 0:T], ACT.Copy).then_inc(s["in_act"], 1)
                else:
                    A(v_tok[:, t - 20, :], ps[:, t % 8, :], ACT.Copy).then_inc(s["in_act"], 1)
            act.wait_ge(s["in_act"], 23)
            act.dma_start(io["new_v"][0, 0].rearrange("h t d -> t h d"), v_tok[:, 0, :].rearrange("p (h d) -> p h d", h=H)).then_inc(s["kv_out"], 16)
            act.wait_ge(s["cv_mm"], 1)
            A(ckT, ps[:, 6, :].rearrange("p (m t) -> p m t", m=4), ACT.Copy).then_inc(s["cv_ev"], 1)
            act.wait_ge(s["cv_mm"], 2)
            A(k_tok, ps[:, 7, :], ACT.Copy).then_inc(s["cv_ev"], 1)
            act.wait_ge(s["cv_ev"], 2)
            act.dma_start(io["new_k"][0, 0].rearrange("h t d -> t h d"), k_tok.rearrange("p (h d) -> p h d", h=H)).then_inc(s["kv_out"], 16)
            for q in range(3):
                act.wait_ge(s["at_max"], q + 1)
                for hh in range(H):
                    buf = sc_p[:, hh, :] if q == 0 else sc_s[:, q - 1, hh, :]
                    last = A(buf, buf, ACT.Exp, bias=amax[:, q, hh:hh + 1], accum_out=asum[:, q, hh:hh + 1])
                act.drain().then_inc(s["at_exp"], 1)
            for j in range(14):
                act.wait_ge(s["pt_mm"], j + 1)
                A(ptT[:, j, :], ps[:, j % 8, :], ACT.Copy).then_inc(s["pt_ev"], 1)
            act.wait_ge(s["out_x"], 1)
            sumsq(1)
            transposed(1)
            moe(0)
            modulation(1)
            act.wait_ge(s["moe_x"], 1)
            sumsq(2)
            transposed(2)
            act.wait_ge(s["rg_lamok"], 1)
            A(spt[:, 1, :], spt[:, 0, :], ACT.Exp, scale=-1.0).then_inc(s["sp_e"], 1)
            act.wait_ge(s["rg_lamok"], 2)
            A(spt[:, 3, :], spt[:, 2, :], ACT.Ln).then_inc(s["sp_ln"], 1)
            for t in range(16):
                act.wait_ge(s["odd_mm"], t + 1)
                if t < 8:
                    A(xrT[:, t, :], ps[:, t % 8, 0:T], ACT.Identity, bias=parR[:, 32 + t:33 + t], scale=parR[:, 16 + t:17 + t]).then_inc(s["odd_act"], 1)
                else:
                    A(geluT[:, t - 8, :], ps[:, t % 8, 0:T], ACT.Gelu_apprx_tanh).then_inc(s["odd_act"], 1)
            for d in range(2):
                for g in range(2):
                    for m in range(8):
                        t = (2 * d + g) * 8 + m
                        act.wait_ge(s["rg_mm"], t + 1)
                        if d == 1 and m == 0 and g == 0:
                            act.wait_ge(s["rg_th"], 1)
                            act.wait_ge(s["rg_scan"], 1)
                        dst = (rr if g == 0 else ri)[:, m, :]
                        A(dst, ps[:, t % 8, 0:T], ACT.Sigmoid, bias=parR[:, 40 + 16 * g + 8 * d + m:41 + 16 * g + 8 * d + m]).then_inc(s["rg_sig"], 1)
                act.wait_ge(s["rg_lamok"], 3)
                act.wait_ge(s["rg_sig"], 16 * d + 16)
                for m in range(8):
                    A(ra[:, m, :], rr[:, m, :], ACT.Exp, scale=s_rg[:, 8 * d + m:8 * d + m + 1]).then_inc(s["rg_a"], 1)
                for m in range(8):
                    A(rt[:, m, :], rr[:, m, :], ACT.Tanh, scale=s_rg[:, 8 * d + m:8 * d + m + 1]).then_inc(s["rg_th"], 1)
                act.wait_ge(s["rg_b"], 2 * d + 1)
                A(rt, rt, ACT.Sqrt).then_inc(s["rg_th"], 1)
            act.wait_ge(s["fin_mm"], 1)
            A(fin_row, ps[0:16, 6, 0:P], ACT.Copy).then_inc(s["fin_ev"], 1)
            act.wait_ge(s["fin_ev"], 1)
            act.dma_start(io["new_h"][0, 0].rearrange("d (m p) -> (d m) p", p=P), fin_row).then_inc(s["fin_out"], 16)
            act.wait_ge(s["out_x"], 2)
            sumsq(3)
            transposed(3)
            act.wait_ge(s["fin_out"], 16)
            moe(1)
            act.wait_ge(s["moe_x"], 2)
            sumsq(4)

        @block.vector
        def _(v):
            V = nc.vector
            V.memset(eps_c, EPS)
            v.sem_inc(s["moe_act"], 2)
            v.sem_inc(s["moe_acc"], 1)
            v.wait_ge(s["par_tr"], 1)
            V.tensor_copy(parH[:, :], ps[:, 0, 0:48])
            V.tensor_copy(parR[:, :], ps[:, 0, 64:168])
            V.tensor_copy(scT[:, :], ps[:, 0, 192:208]).then_inc(s["par_ev"], 2)
            v.wait_ge(s["hyp_ld"], 7 * 16)
            for i, (mm_, done, bank) in enumerate(((s["f1_mm"], s["f1_arg"], 1), (s["f2_mm"], s["f2_arg"], 2))):
                v.wait_ge(mm_, 1)
                a, b, k = hid[:, 0, :], hid[:, 1, :], hid[:, 2, :]
                if i == 1:
                    v.wait_ge(s["f1_sin"], 1)
                V.tensor_scalar(a, ps[0:FFN, bank, 0:T], hyp[:, i:i + 1], hyp[:, 2 + i:3 + i], ALU.add, ALU.mult)
                v.drain()
                V.tensor_scalar(b, a, 1.0 / TWO_PI, ROUND, ALU.mult, ALU.add)
                v.drain()
                V.tensor_scalar(k, b, ROUND, None, ALU.subtract)
                v.drain()
                V.scalar_tensor_tensor(b, k, -PI1, a, ALU.mult, ALU.add)
                v.drain()
                V.scalar_tensor_tensor(a, k, -PI2, b, ALU.mult, ALU.add)
                v.drain()
                V.tensor_scalar(a, a, 3.1415925, -3.1415925, ALU.min, ALU.max).then_inc(done, 1)
            v.wait_ge(s["decay_ld"], 16)
            for c in range(TC):
                if c == 2:
                    v.wait_ge(s["filt_sd"], 2)
                for f in range(4):
                    t = 4 * c + f
                    v.wait_ge(s["filt_mm"], t + 1)
                    V.tensor_tensor(ftmp[:, c % 2, f, :], ps[:, t % 8, :], decay[:, c, :], ALU.mult).then_inc(s["filt_dec"], 1)

            def ada_rows(l):
                v.wait_ge(s["ada_aux"], 256 * (l + 1))
                v.wait_ge(s["ada_mm"], KD * (l + 1))
                for j in range(4):
                    r = slice(32 * j, 32 * j + 2)
                    last = V.tensor_tensor(mrow[r], ps[r, 0:3, :], adab[r], ALU.add)
                last.then_inc(s["ada_row"], 1)
                v.drain()
                for j, b in ((2, 0), (3, 0), (0, 2), (1, 2)):
                    r = slice(32 * j, 32 * j + 2)
                    last = V.scalar_tensor_tensor(mrow[r, b, :], mrow[r, b, :], 1.0, gt[r, :], ALU.add, ALU.mult)
                last.then_inc(s["ada_row"], 2)

            def norm(i, row):
                v.wait_ge(s["norm_ss"], i + 1)
                V.reciprocal(rstd, rstd)
                v.drain()
                for cond, c0_, c1_ in SUBS:
                    for c in range(c0_, c1_):
                        V.scalar_tensor_tensor(h[:, c, :], x[:, c, :], rstd[:, c:c + 1], mods[:, cond, row, :],
                                               ALU.mult, ALU.mult).then_inc(s["norm_h"], 1)

            def transposed(i):
                for c in range(TC):
                    v.wait_ge(s["tr_mm"], 6 * i + 2 * c + 2)
                    V.tensor_copy(hT[:, 4:8, c * P:(c + 1) * P], ps[:, 2 * c + 1, :].rearrange("p (k t) -> p k t", k=4)).then_inc(s["tr_dve"], 1)

            def gated(l):
                for t in range(6):
                    c, half = divmod(t, 2)
                    v.wait_ge(s["out_mm"], 6 * l + t + 1)
                    V.tensor_tensor(otmp[:, c, half * 512:(half + 1) * 512], ps[:, t, :],
                                    mods[:, min(c, 1), 2, half * 512:(half + 1) * 512], ALU.mult).then_inc(s["out_ev"], 1)

            def first_max(dst, vals, mx, rank, n):
                V.tensor_reduce(mx, vals, AX.X, ALU.max)
                v.drain()
                V.tensor_tensor(dst, vals, mx.broadcast_to([P, TC, n]), ALU.is_equal)
                v.drain()
                V.tensor_tensor(dst, dst, rank, ALU.mult)
                v.drain()
                V.tensor_reduce(mx, dst, AX.X, ALU.max)
                v.drain()
                V.tensor_tensor(dst, dst, mx.broadcast_to([P, TC, n]), ALU.is_equal)
                v.drain()

            def router(l):
                v.wait_ge(s["rt_sig"], l + 1)
                v.wait_ge(s["moe_zero"], l + 1)
                rk = rank16[:, None, :].broadcast_to([P, TC, NE])
                V.tensor_tensor(R["sel"], R["sc"], rbias[:, None, :].broadcast_to([P, TC, NE]), ALU.add)
                v.drain()
                g4 = R["sel"].rearrange("p c (g o) -> p c g o", g=NG)
                for i, (a, b) in enumerate(((0, 1), (0, 2), (0, 3), (1, 2), (1, 3), (2, 3))):
                    V.tensor_tensor(pr6[:, :, :, i], g4[:, :, :, a], g4[:, :, :, b], ALU.add)
                v.drain()
                V.tensor_reduce(gsc, pr6, AX.X, ALU.max)
                v.drain()
                first_max(gin, gsc, r1, rk[:, :, 0:NG], NG)
                V.tensor_scalar(geq, gin, 1.0, BIG, ALU.subtract, ALU.mult)
                v.drain()
                m4 = R["msk"].rearrange("p c (g o) -> p c g o", g=NG)
                for o in range(EPG):
                    V.tensor_tensor(m4[:, :, :, o], g4[:, :, :, o], gin, ALU.mult)
                v.drain()
                for o in range(EPG):
                    V.tensor_tensor(m4[:, :, :, o], m4[:, :, :, o], geq, ALU.add)
                v.drain()
                first_max(R["t1"], R["msk"], r1, rk, NE)
                V.scalar_tensor_tensor(R["m2"], R["t1"], -2 * BIG, R["msk"], ALU.mult, ALU.add)
                v.drain()
                first_max(R["t2"], R["m2"], r1, rk, NE)
                V.tensor_tensor(R["t1"], R["t1"], R["t2"], ALU.add)
                v.drain()
                V.tensor_tensor(R["sm"], R["t1"], R["sc"], ALU.mult)
                v.drain()
                V.tensor_reduce(r2, R["sm"], AX.X, ALU.add)
                v.drain()
                V.reciprocal(r2, r2)
                v.drain()
                V.tensor_tensor(gates, R["sm"], r2.broadcast_to([P, TC, NE]), ALU.mult).then_inc(s["rt_gates"], 1)
                v.drain()

            def moe(l):
                router(l)
                gates_e = gates.rearrange("p c e -> p (c e)")
                with v.Fori(0, NBODY) as i:
                    base = i * BT + (NBODY * BT * l)

                    def act_(t):
                        b, c = divmod(t, TC)
                        v.wait_ge(s["moe_silu"], base + (t + 1))
                        v.wait_ge(s["moe_tr"], base + (t + 1))
                        V.scalar_tensor_tensor(act_b[:, t % 2, :], silu_b[:, t % 2, :], gates_e[:, bass.ds(i * 2 + (NE * c + b), 1)],
                                               ps[:, 2 * (t % 2) + 1, :], ALU.mult, ALU.mult).then_inc(s["moe_act"], 1)

                    def sum_(t):
                        c = t % TC
                        v.wait_ge(s["moe_dn"], base + (t + 3))
                        a = acc[:, c, :].rearrange("p (a n) -> p a n", a=2)
                        V.tensor_tensor(a, a, ps[:, 6:8, :], ALU.add).then_inc(s["moe_acc"], 1)

                    for t in range(BT):
                        act_(t)
                        if t:
                            sum_(t - 1)
                    sum_(BT - 1)
                v.drain()
                for c in range(TC):
                    V.tensor_tensor(acc[:, c, :], acc[:, c, :], mods[:, min(c, 1), 5, :], ALU.mult)
                v.drain()
                V.tensor_tensor(x, x, acc, ALU.add).then_inc(s["moe_x"], 1)

            ada_rows(0)
            v.wait_ge(s["ada_mod"], 2 * N_SLICE)
            norm(0, 1)
            transposed(0)
            for t in range(12):
                dst = hy01T[t // 4][:, t % 4, :] if t < 8 else hy2T[:, t - 8, :]
                v.wait_ge(s["in_act"], t + 1)
                for lo, hi in SEGS:
                    V.scalar_tensor_tensor(dst[:, lo + 1:hi], ps[:, t % 8, lo:hi - 1], parH[:, t:t + 1],
                                           dst[:, lo + 1:hi], ALU.mult, ALU.add)
                v.drain()
                for lo, hi in SEGS:
                    last = V.scalar_tensor_tensor(dst[:, lo:hi - 1], ps[:, t % 8, lo + 1:hi], parH[:, 24 + t:25 + t],
                                                  dst[:, lo:hi - 1], ALU.mult, ALU.add)
                last.then_inc(s["in_dve"], 1)
            for t in range(6):
                v.wait_ge(s["tok_mm"], t + 1)
                V.tensor_copy(hy_tok[:, t // 2, t % 2, :], ps[:, t, :]).then_inc(s["tok_ev"], 1)
            for n in range(2):
                v.wait_ge(s["u_mm"], 6 * n + 6)
                v.wait_ge(s["spec_fix"], 2)
                Ur, Ui = ps[:, 0:3, :], ps[:, 3:6, :]
                A_, B_ = spec[:, n, 0], spec[:, n, 1]
                V.tensor_tensor(ptmp[:, 0], Ur, A_, ALU.mult)
                V.tensor_tensor(ptmp[:, 1], Ui, B_, ALU.mult)
                v.drain()
                V.tensor_tensor(prod[:, 0], ptmp[:, 0], ptmp[:, 1], ALU.subtract)
                v.drain()
                V.tensor_tensor(ptmp[:, 0], Ur, B_, ALU.mult)
                V.tensor_tensor(ptmp[:, 1], Ui, A_, ALU.mult)
                v.drain()
                V.tensor_tensor(prod[:, 1], ptmp[:, 0], ptmp[:, 1], ALU.add)
                v.drain()
                V.tensor_tensor(prod[0:1, 1, 0:2, :], ps[0:1, 3:5, :], c0[:, n], ALU.mult).then_inc(s["spec_y"], 1)
                if n == 0:
                    for c in range(TC):
                        v.wait_ge(s["inv_mm"], c + 1)
                        V.tensor_tensor(hy_tok[:, c, 0, :], ps[:, c, :], hy_tok[:, c, 1, :], ALU.mult).then_inc(s["inv_ev"], 1)
                else:
                    for m in range(4):
                        v.wait_ge(s["inv_mm"], 4 + m)
                        V.tensor_tensor(catT[:, 4 + m, :], ps[:, m, 0:T], hy2T[:, m, :], ALU.mult).then_inc(s["inv_ev"], 1)
            v.wait_ge(s["bias_ok"], H)
            for hh in range(H):
                for q in range(3):
                    t = 3 * hh + q
                    v.wait_ge(s["sc_mm"], t + 1)
                    if q == 0:
                        V.tensor_scalar(sc_p[:, hh, :], ps[:, t % 8, 0:P], SCALE, None, ALU.mult).then_inc(s["sc_ev"], 1)
                    else:
                        b0 = 3 - 2 * (q - 1)
                        V.scalar_tensor_tensor(sc_s[:, q - 1, hh, 0:LS].rearrange("p (r k) -> p r k", r=4),
                                               ps[:, t % 8, 0:LS].rearrange("p (r k) -> p r k", r=4), SCALE,
                                               bias[:, hh, b0:b0 + 4, ::-1], ALU.mult, ALU.add)
                        V.tensor_scalar(sc_s[:, q - 1, hh, LS:T], ps[:, t % 8, LS:T], SCALE, None, ALU.mult).then_inc(s["sc_ev"], 1)
            v.drain()
            for q in range(3):
                V.tensor_reduce(amax[:, q, :], sc_p if q == 0 else sc_s[:, q - 1], AX.X, ALU.max)
                v.drain()
                V.tensor_scalar(amax[:, q, :], amax[:, q, :], -1.0, None, ALU.mult).then_inc(s["at_max"], 1)
            for q in range(3):
                v.wait_ge(s["at_exp"], q + 1)
                V.reciprocal(arcp[:, q, :], asum[:, q, :])
                v.drain()
                buf = sc_p if q == 0 else sc_s[:, q - 1]
                V.tensor_tensor(buf, buf, arcp[:, q, :, None].broadcast_to([P, H, P if q == 0 else T]), ALU.mult).then_inc(s["at_nrm"], 1)
            for hh in range(H):
                r0 = 64 * (hh % 2)
                for q in range(3):
                    t = 3 * hh + q
                    v.wait_ge(s["pv_mm"], t + 1)
                    V.tensor_copy(catT[r0:r0 + 64, hh // 2, q * P:(q + 1) * P], ps[r0:r0 + 64, t % 8, 0:P]).then_inc(s["pv_ev"], 1)
            gated(0)
            norm(1, 4)
            transposed(1)
            moe(0)
            ada_rows(1)
            v.wait_ge(s["ada_mod"], 4 * N_SLICE)
            norm(2, 1)
            transposed(2)
            lam = parR[:, 72:88]
            V.tensor_scalar(spt[:, 4, :], lam, -1.0, None, ALU.mult)
            v.drain()
            V.tensor_tensor(spt[:, 0, :], lam, spt[:, 4, :], ALU.max).then_inc(s["rg_lamok"], 1)
            v.wait_ge(s["sp_e"], 1)
            V.tensor_scalar(spt[:, 2, :], spt[:, 1, :], 1.0, None, ALU.add).then_inc(s["rg_lamok"], 1)
            for t in range(8):
                dst = xrT[:, t, :]
                v.wait_ge(s["odd_act"], t + 1)
                for tap, sh in ((0, -2), (1, -1), (3, 1)):
                    for lo, hi in SEGS:
                        a, b = max(lo, lo - sh), min(hi, hi - sh)
                        last = V.scalar_tensor_tensor(dst[:, a:b], ps[:, t % 8, a + sh:b + sh], parR[:, 8 * tap + t:8 * tap + t + 1],
                                                      dst[:, a:b], ALU.mult, ALU.add)
                    if tap != 3:
                        v.drain()
                last.then_inc(s["odd_dve"], 1)
            v.wait_ge(s["sp_ln"], 1)
            V.tensor_scalar(spt[:, 5, :], spt[:, 2, :], -1.0, 1e-30, ALU.add, ALU.max)
            v.drain()
            V.reciprocal(spt[:, 6, :], spt[:, 5, :])
            V.tensor_tensor(spt[:, 3, :], spt[:, 3, :], spt[:, 1, :], ALU.mult)
            v.drain()
            V.tensor_tensor(spt[:, 3, :], spt[:, 3, :], spt[:, 6, :], ALU.mult)
            V.tensor_scalar(spt[:, 7, :], spt[:, 2, :], 1.0, None, ALU.is_equal)
            v.drain()
            V.tensor_tensor(spt[:, 7, :], spt[:, 7, :], spt[:, 1, :], ALU.mult)
            v.drain()
            V.tensor_tensor(spt[:, 3, :], spt[:, 3, :], spt[:, 7, :], ALU.add)
            V.tensor_scalar(spt[:, 4, :], spt[:, 4, :], 0.0, None, ALU.max)
            v.drain()
            V.tensor_tensor(spt[:, 3, :], spt[:, 3, :], spt[:, 4, :], ALU.add)
            v.drain()
            V.tensor_scalar(s_rg, spt[:, 3, :], -8.0, None, ALU.mult).then_inc(s["rg_lamok"], 1)
            for d in range(2):
                v.wait_ge(s["rg_sig"], 16 * d + 16)
                V.tensor_tensor(ri, ri, xrT, ALU.mult)
                v.wait_ge(s["rg_a"], 8 * d + 8)
                v.wait_ge(s["rg_th"], 9 * d + 8)
                V.tensor_tensor(rr, ra, ra, ALU.mult)
                v.drain()
                V.scalar_tensor_tensor(rt, rr, 1.0, rt, ALU.add, ALU.mult)
                v.drain()
                V.tensor_scalar(rt, rt, -1.0, 0.0, ALU.mult, ALU.max).then_inc(s["rg_b"], 1)
                v.wait_ge(s["rg_th"], 9 * d + 9)
                V.tensor_tensor(ri, ri, rt, ALU.mult).then_inc(s["rg_b"], 1)
                v.drain()
                out = catT if d == 0 else rr
                for m in range(8):
                    for lo, hi in SEGS:
                        init = 0.0 if lo == 0 else parR[:, 88 + 8 * d + m:89 + 8 * d + m]
                        o_, a_, b_ = out[:, m, lo:hi], ra[:, m, lo:hi], ri[:, m, lo:hi]
                        if d == 1:
                            o_, a_, b_ = o_[:, ::-1], a_[:, ::-1], b_[:, ::-1]
                        V.tensor_tensor_scan(o_, a_, b_, init, ALU.mult, ALU.add)
                v.drain()
                V.tensor_copy(fin_col[:, d, :], out[:, :, LP - 1] if d == 0 else out[:, :, 0])
                v.drain().then_inc(s["rg_scan"], 1)
            v.wait_ge(s["odd_act"], 16)
            V.tensor_tensor(catT, catT, rr, ALU.add)
            v.drain()
            V.tensor_tensor(catT, catT, geluT, ALU.mult)
            v.drain().then_inc(s["odd_y"], 1)
            gated(1)
            norm(3, 4)
            transposed(3)
            moe(1)
            v.wait_ge(s["norm_ss"], 5)
            V.reciprocal(rstd, rstd)
            v.drain()
            v.wait_ge(s["norm_gl"], 16)
            for c in range(TC):
                V.scalar_tensor_tensor(h[:, c, :], x[:, c, :], rstd[:, c:c + 1], fing, ALU.mult, ALU.mult).then_inc(s["y_ready"], 1)


_INS = ["x_prompt", "x_sample", "cache_k", "cache_v", "state_h", "c", "c_ctx", "norm_g", "ada_w", "ada_b",
        "final_g", "a_in_w", "a_out_w", "na_rpb", "hy_short_w", "hy_short_b", "hy_w1", "hy_b1", "hy_w2",
        "hy_b2", "hy_w3", "hy_freq", "hy_d", "c_in_w", "c_out_w", "rg_conv_w", "rg_conv_b", "rg_wa", "rg_ba",
        "rg_wx", "rg_bx", "rg_lam", "router_w", "router_b", "moe_w_gate", "moe_w_up", "moe_w_down"]
_OUTS = [("y_prompt", (1, LP, D)), ("y_sample", (1, LS, D)), ("new_k", (1, 1, H, LP, DH)),
         ("new_v", (1, 1, H, LP, DH)), ("new_h", (1, 1, 2, D))]


def kernel(**inputs):
    import concourse.bacc as bacc
    from concourse.bass_utils import run_bass_kernel_spmd

    nc = bacc.Bacc("TRN2", target_bir_lowering=False, num_devices=1)
    arrays, io = {}, {}
    for name in _INS:
        a = np.asarray(inputs[name])
        if name == "na_rpb":
            a = a[..., ::-1]
        a = np.ascontiguousarray(a)
        arrays["in_" + name] = a
        io[name] = nc.dram_tensor("in_" + name, a.shape, mybir.dt.from_np(a.dtype), kind="ExternalInput").ap()
    for name, a in shape_constants().items():
        a = np.ascontiguousarray(a)
        arrays[name] = a
        io[name] = nc.dram_tensor(name, a.shape, FP, kind="ExternalInput").ap()
    for name, shape in _OUTS:
        io[name] = nc.dram_tensor("out_" + name, shape, FP, kind="ExternalOutput").ap()
    build(nc, io)
    r = run_bass_kernel_spmd(nc, [arrays], core_ids=[0])
    return tuple(r.results[0]["out_" + name] for name, _ in _OUTS)
```

```python
import math
from contextlib import ExitStack

import numpy as np
import concourse.bass as bass
from concourse import mybir

FP = mybir.dt.float32
ALU = mybir.AluOpType
ACT = mybir.ActivationFunctionType
AX = mybir.AxisListType

P = 128
D = 1024
KD = D // P
LP, LS = 128, 256
T = LP + LS
TC = T // P
DEPTH = 2
H, DH = 8, 64
DA = H * DH
DB = D - DA
GRID_W, ROWS = 64, 4
WIN_COLS, WIN_ROWS = 16, 8
RPB_C = 2 * WIN_COLS - 1
RPB_R = 2 * WIN_ROWS - 1
EMB, FFN = 33, 64
NE, NG, EPG = 16, 4, 4
F = 512
KF = F // P
CAP = 64
EPS = 1e-6
BIG = 1e30
SCALE = DH ** -0.5
TWO_PI = 2 * math.pi
PI1 = 6.28125
PI2 = float(np.float32(TWO_PI - PI1))
ROUND = 12582912.0
SEGS = ((0, LP), (LP, T))
SUBS = ((0, 0, 1), (1, 1, 3))
N_SLICE = 6 * D // 512


def shape_constants():
    c = {}
    ident = np.eye(P, dtype=np.float32)
    sel = np.zeros((P, 2, P), np.float32)
    for j in range(4):
        for k in range(2):
            sel[32 * j + k, k, :] = 1.0
    cols = np.arange(GRID_W)
    start = np.clip(cols - WIN_COLS // 2, 0, GRID_W - WIN_COLS)
    inside = (cols[None, :] >= start[:, None]) & (cols[None, :] < start[:, None] + WIN_COLS)
    mask = np.where(inside, 0.0, -BIG).astype(np.float32)[:, ::-1]
    c["k_const"] = np.concatenate([ident, sel.reshape(P, 2 * P), np.concatenate([mask, mask]),
                                   np.triu(np.ones((P, P), np.float32)), np.ones((P, P), np.float32),
                                   np.tile(np.arange(P, dtype=np.float32), (P, 1)),
                                   (np.arange(P, dtype=np.float32) % CAP)[:, None],
                                   (np.arange(P, dtype=np.float32) % CAP + CAP)[:, None]], axis=1)
    zs, decs = [], []
    for L in (LP, LS):
        t = np.linspace(0.0, 1.0, L, dtype=np.float32)[:, None]
        w = (2.0 * math.pi * np.arange(L, dtype=np.float32)[:, None] / L).astype(np.float32)
        f = np.linspace(1e-4, 15, 16, dtype=np.float32)[None, :]
        zs.append(np.concatenate([t, np.cos(f * w), -np.sin(f * w)], axis=-1))
        lo, hi = math.log(1e-2) / 1.5, math.log(1e-2) / 0.3
        deltas = np.linspace(lo, hi, DB, dtype=np.float32)
        decs.append(np.exp(-t * np.abs(deltas)))
    c["k_z"] = np.ascontiguousarray(np.concatenate(zs).T.astype(np.float32))
    c["k_decay"] = np.concatenate(decs).astype(np.float32)
    for tag, L in (("p", LP), ("s", LS)):
        n = 2 * L
        t, k = np.arange(L)[:, None], np.arange(L)[None, :]
        ang = 2 * np.pi * ((t * k) % n) / n
        re, im = np.cos(ang), -np.sin(ang)
        im[:, 0] = (-1.0) ** np.arange(L)
        c["k_dft_" + tag] = np.concatenate([re, im], axis=1).astype(np.float32)
        wt = np.full((L, 1), 2.0 / n)
        wt[0] = 1.0 / n
        c["k_idft_" + tag] = np.concatenate([re.T * wt, im.T * wt], axis=0).astype(np.float32)
    return c


SEM_NAMES = """consts_ld x_ld tables_ld hyp_ld w3_ld decay_ld hyrow_ld params_ld rw_ld
silu_c silu_ct par_tr par_ev
f1_mm f1_arg f1_sin f2_mm f2_arg f2_sin filt_mm filt_dec filt_sd filt_d
spec_mm spec_ev spec_fix
ada_ld0 ada_ld1 ada_aux ada_mm ada_row ada_bc ada_mod
norm_ss norm_h norm_h2 norm_rs tr_mm tr_act tr_dve
in_ld0 in_ld1 in_mm in_act in_dve
tok_mm tok_ev
cache_ld bias_ld bias_ok cv_mm cv_ev
u_mm spec_y inv_mm inv_ev
sc_mm sc_ev at_max at_exp at_nrm pt_mm pt_ev pv_mm pv_ev
out_ld out_mm out_ev out_x
rt_mm rt_sig rt_gates
gu_ld0 gu_ld1 dn_ld0 dn_ld1 gu_used0 gu_used1 dn_used0 dn_used1
moe_zero moe_x pos_mm pos_ready rows_mm rows_ev rows_st
kout_mm kout_ev kv_out
odd_ld0 odd_ld1 odd_mm odd_act odd_dve bd_zero bd_ld rg_mm rg_sig rg_a rg_th rg_b rg_scan sp_e sp_ln rg_lamok
fin_mm fin_ev fin_out odd_y
norm_gl y_ready y_out""".split()
LAYER_SEMS = """de_mm de_silu de_act de_tr de_actT de_dn de_acc
g_mm g_ev p_ready gu_mm silu_ev act_ready tr_mm tr_ev dn_mm y_ev pt_ready sc_mm acc_done bc_ld""".split()


def build(nc, io):
    ctx = ExitStack()
    with ctx:
        def sb(name, cols, rows=P):
            return ctx.enter_context(nc.sbuf_tensor(name, [rows, cols], FP))

        s = {n: ctx.enter_context(nc.semaphore(n)) for n in SEM_NAMES}
        layer_s = [{n: ctx.enter_context(nc.semaphore(f"{n}_l{l}")) for n in LAYER_SEMS} for l in range(DEPTH)]
        ada_ld, in_ld, odd_ld = (s["ada_ld0"], s["ada_ld1"]), (s["in_ld0"], s["in_ld1"]), (s["odd_ld0"], s["odd_ld1"])
        gu_ld, dn_ld = (s["gu_ld0"], s["gu_ld1"]), (s["dn_ld0"], s["dn_ld1"])
        gu_used, dn_used = (s["gu_used0"], s["gu_used1"]), (s["dn_used0"], s["dn_used1"])

        const = sb("const", 128 + 256 + 64 + 3 * 128 + 2)
        tri, ones = const[:, 448:576], const[:, 576:704]
        slot_row, slot_col = const[:, 704:832], const[:, 832:834]
        ident, sel, cmask = const[:, 0:128], const[:, 128:384], const[:, 384:448]
        sel = sel.rearrange("p (c m) -> p c m", c=2)
        x = sb("x", TC * D)[:, :].rearrange("p (c d) -> p c d", c=TC)
        h_t = sb("h", TC * D)
        h = h_t[:, :].rearrange("p (c d) -> p c d", c=TC)
        hT_t = sb("hT", KD * T)
        hT = hT_t[:, :].rearrange("p (k t) -> p k t", k=KD)
        catT = hT
        mods_t = sb("mods", 2 * 6 * D)
        mods = mods_t[:, :].rearrange("p (c v d) -> p c v d", c=2, v=6)
        W = sb("W", 24576)
        E = sb("E", 3584)
        c0 = sb("c0", 2048, 1)[:, :].rearrange("p (n s f) -> p n s f", n=2, s=2)
        parH = sb("parH", 48)
        parR = sb("parR", 104)
        scT = sb("scT", 16)
        rw = sb("rw", KD * NE)[:, :].rearrange("p (k e) -> p k e", k=KD)
        small = sb("small", 64)
        hyp = sb("hyp", 4, FFN)
        ss, rstd = small[:, 0:3], small[:, 3:6]
        eps_c = small[:, 6:7]
        s_rg = small[:, 8:24]
        gates = sb("gates", TC * NE)[:, :].rearrange("p (c e) -> p c e", c=TC)
        ps = ctx.enter_context(nc.psum_tensor("ps", [P, 8, 512], FP))

        rows_h, rows_r, rows_c = mods_t[0:48, 0:128], mods_t[0:104, 128:256], mods_t[0:16, 256:384]
        rows_s = mods_t[0:16, 384:512]
        ftmp = mods_t[:, 1024:5120].rearrange("p (b f n) -> p b f n", b=2, f=4)
        d_row = mods_t[0:1, 5120:6144].rearrange("p (n f) -> p n f", n=2)
        hid = mods_t[0:FFN, 6144:6144 + 6 * T].rearrange("p (b t) -> p b t", b=6)
        filt_s = h_t[:, :].rearrange("p (c n f) -> p c n f", c=TC, n=2)
        filt_d = hT_t[:, :].rearrange("p (c n f) -> p c n f", c=TC, n=2)
        w3 = E[0:FFN, 0:2048]
        decay = E[:, 2048:3584].rearrange("p (c f) -> p c f", c=TC)
        ada_w = W[:, 0:12288].rearrange("p (b n) -> p b n", b=2)
        mrow = W[:, 12288:13824].rearrange("p (b n) -> p b n", b=3)
        adab = W[:, 13824:15360].rearrange("p (b n) -> p b n", b=3)
        gt = W[:, 15360:15872]
        z_sb = E[0:EMB, 0:T]
        wblk = W[:, 0:8192].rearrange("p (b k n) -> p b k n", b=2, k=KD)
        qkT = W[:, 8192:11264].rearrange("p (m t) -> p m t", m=8)
        v_tok = W[:, 11264:12800].rearrange("p (c n) -> p c n", c=TC)
        hy2T = W[:, 12800:14336].rearrange("p (m t) -> p m t", m=4)
        ck = W[:, 14336:14848]
        cv = W[:, 14848:15360]
        ckT = W[:, 15360:15872].rearrange("p (m t) -> p m t", m=4)
        dft_s = W[:, 15872:16896].rearrange("p (k f) -> p k f", k=2)
        idft_s = W[:, 16896:17920].rearrange("p (k t) -> p k t", k=4)
        dft_p = W[:, 17920:18176]
        idft_p = W[:, 18176:18432].rearrange("p (k t) -> p k t", k=2)
        spec = W[:, 18432:24576].rearrange("p (n a c f) -> p n a c f", n=2, a=2, c=TC)
        hy01T = [mods_t[:, 6144 * b:6144 * b + 4 * T].rearrange("p (m t) -> p m t", m=4) for b in range(2)]
        hy_tok = h_t[:, :].rearrange("p (c a n) -> p c a n", c=TC, a=2)
        prod = W[:, 0:3072].rearrange("p (a c n) -> p a c n", a=2, c=TC)
        ptmp = W[:, 3072:6144].rearrange("p (a c n) -> p a c n", a=2, c=TC)
        bias = E[:, :].rearrange("p (h r k) -> p h r k", h=H, r=7)
        sc_p = W[:, 15872:16896].rearrange("p (h k) -> p h k", h=H)
        sc_s = W[:, 16896:23040].rearrange("p (q h k) -> p q h k", q=2, h=H)
        ptT = W[:, 0:7168].rearrange("p (j k) -> p j k", k=512)
        amax = W[:, 23040:23064].rearrange("p (q h) -> p q h", q=3)
        asum = W[:, 23064:23088].rearrange("p (q h) -> p q h", q=3)
        arcp = W[:, 23088:23112].rearrange("p (q h) -> p q h", q=3)
        k_tok = W[:, 7168:7680]
        wout = W[:, 0:8192].rearrange("p (k n) -> p k n", k=KD)
        otmp = W[:, 8192:11264].rearrange("p (c d) -> p c d", c=TC)
        geluT = W[:, 8192:11264].rearrange("p (m t) -> p m t", m=8)
        xrT = W[:, 11264:14336].rearrange("p (m t) -> p m t", m=8)
        rr = h_t[:, :].rearrange("p (m t) -> p m t", m=8)
        ri = W[:, 14336:17408].rearrange("p (m t) -> p m t", m=8)
        ra = W[:, 17408:20480].rearrange("p (m t) -> p m t", m=8)
        rt = W[:, 20480:23552].rearrange("p (m t) -> p m t", m=8)
        bd = [mods_t[:, 6144 * d:6144 * d + 2048].rearrange("p (g m n) -> p g m n", g=2, m=8) for d in range(2)]
        spt = W[:, 23552:23552 + 128].rearrange("p (a m) -> p a m", a=8)
        fin_col = W[:, 23680:23696].rearrange("p (d m) -> p d m", d=2)
        fin_row = W[0:16, 23712:23840]
        wg = [W[:, 12288 * b:12288 * b + 4096].rearrange("p (k f) -> p k f", k=KD) for b in range(2)]
        wu = [W[:, 12288 * b + 4096:12288 * b + 8192].rearrange("p (k f) -> p k f", k=KD) for b in range(2)]
        wd = [W[:, 12288 * b + 8192:12288 * b + 12288].rearrange("p (k d) -> p k d", k=KF) for b in range(2)]
        acc = mods[:, 0, 0:3, :]
        mr = mods_t[:, 6144:6144 + 3072]
        silu_h, act_h = (mr[:, 512 * i:512 * i + 512].rearrange("p (r n) -> p r n", r=2) for i in range(2))
        actT_h = mr[:, 1024:1536].rearrange("p (r j n) -> p r j n", r=2, j=2)
        y_h = mr[:, 1536:2560].rearrange("p (r n) -> p r n", r=2)
        hTg = mods_t[:, 3072:4096].rearrange("p (r k n) -> p r k n", r=2, k=KD)
        row_bc = mods_t[:, 4096:4864].rearrange("p (a t) -> p a t", a=2)
        place_T = mods_t[:, 9216:9216 + 1536].rearrange("p (b r t) -> p b r t", b=2, r=2)
        place = E[:, 1024:1792].rearrange("p (b c n) -> p b c n", b=2, c=TC)
        rows_T = E[0:NE, 1792:2560].rearrange("p (a t) -> p a t", a=2)
        posm = E[:, 2560:2608].rearrange("p (c e) -> p c e", c=TC)
        counts = ctx.enter_context(nc.sbuf_tensor("counts", [1, NE + 1], mybir.dt.int32))
        cnt_f = E[0:1, 2608:2608 + NE + 1]
        rows_d = [nc.dram_tensor(f"place_rows_{l}", (NE, 2, T), FP, kind="Internal").ap() for l in range(DEPTH)]
        B_G, B_GU, B_TR, B_DN, B_SC = (0, 1), (2, 3), 4, (5, 3), 6
        mt = mods_t[:, 6144:6144 + 3072].rearrange("p (a b n) -> p a b n", a=3, b=2)
        silu_b, act_b, actT_b = mt[:, 0], mt[:, 1], mt[:, 2]
        R = {n: E[:, 48 * i:48 * i + 48].rearrange("p (c e) -> p c e", c=TC)
                   for i, n in enumerate(["sc", "sel", "msk", "eq", "w", "t1", "t2", "m2", "sm"])}
        pr6 = E[:, 512:512 + 72].rearrange("p (c g o) -> p c g o", c=TC, g=NG)
        gsc, geq, gw, gin = (E[:, 600 + 16 * i:612 + 16 * i].rearrange("p (c g) -> p c g", c=TC) for i in range(4))
        r1, r2 = (E[:, 680 + 8 * i:683 + 8 * i].rearrange("p (c o) -> p c o", c=TC) for i in range(2))
        rbias = E[:, 704:720]
        rank16 = E[:, 720:736]
        fing = mods[:, 0, 5, :]

        block = ctx.enter_context(nc.Block())
        w_in = io["a_in_w"][0].rearrange("(k p) n -> p k n", p=P)
        w_cin = io["c_in_w"][0].rearrange("(k p) n -> p k n", p=P)
        w_aout = io["a_out_w"][0].rearrange("(k p) n -> p k n", p=P)
        w_cout = io["c_out_w"][0].rearrange("(k p) n -> p k n", p=P)
        wg_d = io["moe_w_gate"].rearrange("l e (k p) f -> (l e) p k f", p=P)
        wu_d = io["moe_w_up"].rearrange("l e (k p) f -> (l e) p k f", p=P)
        wd_d = io["moe_w_down"].rearrange("l e (k p) d -> (l e) p k d", p=P)
        IN_ORDER = (3, 4, 5, 0, 1, 2)
        ODD_ORDER = (2, 3, 0, 1)
        NBODY = NE // 2
        BT = 2 * TC

        @block.sync
        def _(sp):
            sp.dma_start(const[:, :], io["k_const"]).then_inc(s["consts_ld"], 16)
            sp.dma_start(rows_c[0:8, :], io["c_ctx"].rearrange("(k p) -> k p", p=P)).then_inc(s["params_ld"], 16)
            sp.dma_start(rows_c[8:16, :], io["c"][0].rearrange("(k p) -> k p", p=P)).then_inc(s["params_ld"], 16)
            sp.dma_start(rows_h[0:36, :], io["hy_short_w"][0].rearrange("j (c p) -> (j c) p", p=P)).then_inc(s["params_ld"], 16)
            sp.dma_start(rows_h[36:48, :], io["hy_short_b"][0].rearrange("(c p) -> c p", p=P)).then_inc(s["params_ld"], 16)
            sp.dma_start(rows_r[0:32, :], io["rg_conv_w"][0].rearrange("j (c p) -> (j c) p", p=P)).then_inc(s["params_ld"], 16)
            sp.dma_start(rows_r[32:40, :], io["rg_conv_b"][0].rearrange("(c p) -> c p", p=P)).then_inc(s["params_ld"], 16)
            for i, n in enumerate(("rg_ba", "rg_bx", "rg_lam", "state_h")):
                sp.dma_start(rows_r[40 + 16 * i:56 + 16 * i, :],
                             io[n][0].rearrange("d (c p) -> (d c) p", p=P) if n != "state_h"
                             else io[n][0, 0].rearrange("d (c p) -> (d c) p", p=P)).then_inc(s["params_ld"], 16)
            sp.dma_start(x[:, 0, :], io["x_prompt"][0]).then_inc(s["x_ld"], 16)
            sp.dma_start(x[:, 1:3, :], io["x_sample"][0].rearrange("(c p) d -> p c d", p=P)).then_inc(s["x_ld"], 16)

            def ada(l):
                if l == 1:
                    for b in range(2):
                        sp.wait_ge(gu_used[b], NBODY + 1)
                        sp.wait_ge(dn_used[b], NBODY + 1)
                for k in range(KD):
                    if k >= 2:
                        sp.wait_ge(s["ada_mm"], KD * l + k - 1)
                    sp.dma_start(ada_w[:, k % 2, :], io["ada_w"][l, k * P:(k + 1) * P, :]).then_inc(ada_ld[k % 2], 16)

            def in_blocks(src, order, sems, mm, per):
                for i, nb in enumerate(order):
                    if i >= 2:
                        sp.wait_ge(mm, per[i - 2])
                    sp.dma_start(wblk[:, i % 2], src[:, :, nb * 512:(nb + 1) * 512]).then_inc(sems[i % 2], 16)

            def experts(l):
                sp.wait_ge(s["out_mm"], 6 * (l + 1))
                sp.wait_ge(s["out_x"], l + 1)
                if l == 1:
                    sp.wait_ge(s["fin_out"], 16)
                with sp.Fori(0, NBODY) as i:
                    for b in range(2):
                        e = i * 2 + (NE * l + b)
                        sp.wait_ge(gu_used[b], i + (NBODY * l + 1))
                        sp.dma_start(wg[b], wg_d[e]).then_inc(gu_ld[b], 16)
                        sp.dma_start(wu[b], wu_d[e]).then_inc(gu_ld[b], 16)
                        sp.wait_ge(dn_used[b], i + (NBODY * l + 1))
                        sp.dma_start(wd[b], wd_d[e]).then_inc(dn_ld[b], 16)

            ada(0)
            sp.wait_ge(s["ada_mm"], KD)
            in_blocks(w_in, IN_ORDER, in_ld, s["in_mm"], (4, 8, 12, 16, 20, 23))
            sp.wait_ge(s["pv_mm"], 24)
            sp.wait_ge(s["kv_out"], 32)
            for k in range(2):
                sp.dma_start(wout[:, 4 * k:4 * k + 4, :], w_aout[:, 4 * k:4 * k + 4, :]).then_inc(s["out_ld"], 16)
            experts(0)
            ada(1)
            sp.wait_ge(s["ada_mm"], 2 * KD)
            in_blocks(w_cin, ODD_ORDER, odd_ld, s["odd_mm"], (4, 8, 12, 16))
            sp.wait_ge(s["odd_mm"], 16)
            for k in range(2):
                sp.dma_start(wout[:, 4 * k:4 * k + 4, :], w_cout[:, 4 * k:4 * k + 4, :]).then_inc(s["out_ld"], 16)
            experts(1)
            sp.wait_ge(s["y_ready"], 3)
            sp.dma_start(io["y_prompt"][0], h[:, 0, :]).then_inc(s["y_out"], 16)
            sp.dma_start(io["y_sample"][0].rearrange("(c p) d -> p c d", p=P), h[:, 1:3, :]).then_inc(s["y_out"], 16)
            sp.wait_ge(s["y_out"], 32)
            sp.wait_ge(s["kv_out"], 32)
            sp.wait_ge(s["fin_out"], 16)

        @block.gpsimd
        def _(pool):
            gp = nc.gpsimd
            pool.dma_start(z_sb, io["k_z"]).then_inc(s["hyp_ld"], 16)
            for i, src in enumerate((io["hy_b1"][0], io["hy_b2"][0], io["hy_freq"][0, 0], io["hy_freq"][0, 1])):
                pool.dma_start(hyp[:, i:i + 1], src.rearrange("(p o) -> p o", o=1)).then_inc(s["hyp_ld"], 16)
            pool.dma_start(hid[0:EMB, 5, 0:FFN], io["hy_w1"][0]).then_inc(s["hyp_ld"], 16)
            pool.dma_start(hid[:, 5, 64:128], io["hy_w2"][0]).then_inc(s["hyp_ld"], 16)
            pool.dma_start(d_row, io["hy_d"][0:1]).then_inc(s["hyrow_ld"], 16)
            pool.dma_start(decay, io["k_decay"].rearrange("(c p) f -> p c f", p=P)).then_inc(s["decay_ld"], 16)
            pool.dma_start(dft_s, io["k_dft_s"].rearrange("(k p) f -> p k f", p=P)).then_inc(s["tables_ld"], 16)
            pool.dma_start(dft_p, io["k_dft_p"]).then_inc(s["tables_ld"], 16)
            pool.dma_start(idft_s, io["k_idft_s"].rearrange("(k p) f -> p k f", p=P)).then_inc(s["tables_ld"], 16)
            pool.dma_start(idft_p, io["k_idft_p"].rearrange("(k p) f -> p k f", p=P)).then_inc(s["tables_ld"], 16)
            pool.dma_start(rw, io["router_w"].rearrange("(k p) e -> p k e", p=P)).then_inc(s["rw_ld"], 16)

            def ada_aux(l):
                for c in range(2):
                    for j in range(4):
                        pool.dma_start(adab[32 * j + c:32 * j + c + 1], io["ada_b"][l:l + 1].rearrange(
                            "o (b j n) -> o j b n", b=3, j=4)[:, j]).then_inc(s["ada_aux"], 16)
                    for j, (v, half) in enumerate(((1, 0), (1, 1), (0, 0), (0, 1))):
                        pool.dma_start(gt[32 * j + c:32 * j + c + 1, :],
                                       io["norm_g"][l, v:v + 1, half * 512:half * 512 + 512]).then_inc(s["ada_aux"], 16)

            ada_aux(0)
            pool.wait_ge(s["f1_mm"], 1)
            pool.dma_start(w3, io["hy_w3"][0]).then_inc(s["w3_ld"], 16)
            for c in range(TC):
                pool.wait_ge(s["filt_dec"], 4 * c + 4)
                for n in range(2):
                    f0, f1 = ftmp[:, c % 2, 2 * n, :], ftmp[:, c % 2, 2 * n + 1, :]
                    gp.tensor_tensor(filt_s[:, c, n, :], f0, f1, ALU.add)
                    gp.tensor_tensor(filt_d[:, c, n, :], f0, f1, ALU.subtract).then_inc(s["filt_sd"], 1)
            pool.wait_ge(s["hyrow_ld"], 16)
            pool.wait_ge(s["filt_sd"], 6)
            for c in range(2):
                gp.tensor_tensor(filt_s[0:1, c, :, :], filt_s[0:1, c, :, :], d_row, ALU.add).then_inc(s["filt_d"], 1)
            pool.wait_ge(s["spec_ev"], 16)
            for n in range(2):
                gp.memset(spec[0:1, n, 1, 0:2, :], 0.0).then_inc(s["spec_fix"], 1)

            pool.wait_ge(s["filt_dec"], 12)
            rpb = io["na_rpb"]
            for up in range(2):
                for hh in range(H):
                    off = hh * RPB_R * RPB_C + (WIN_ROWS - 4 - up) * RPB_C + WIN_COLS - GRID_W
                    src = bass.AP(tensor=rpb.tensor, offset=off, ap=[[1, GRID_W], [RPB_C, 7], [1, GRID_W]])
                    pool.dma_start(bias[64 * up:64 * up + 64, hh], src).then_inc(s["bias_ld"], 16)
            pool.wait_ge(s["ada_row"], 3)
            pool.wait_ge(s["ada_bc"], N_SLICE * 2)
            pool.dma_start(ck.rearrange("p (h d) -> p h d", h=H), io["cache_k"][0, 0].rearrange("h t d -> t h d")).then_inc(s["cache_ld"], 16)
            pool.dma_start(cv.rearrange("p (h d) -> p h d", h=H), io["cache_v"][0, 0].rearrange("h t d -> t h d")).then_inc(s["cache_ld"], 16)
            pool.wait_ge(s["bias_ld"], 16 * 16)
            for hh in range(H):
                b3 = bias[:, hh]
                gp.tensor_tensor(b3, b3, cmask[:, None, :].broadcast_to([P, 7, GRID_W]), ALU.add).then_inc(s["bias_ok"], 1)

            def shift(i, lo):
                for n, (cond, c0_, c1_) in enumerate(SUBS):
                    for c in range(c0_, c1_):
                        pool.wait_ge(s["norm_h"], 3 * i + c + 1)
                        gp.tensor_tensor(h[:, c, :], h[:, c, :], mods[:, cond, lo, :], ALU.add).then_inc(s["norm_h2"], 1)

            def residual(n_done, sem_in, done):
                for c in range(TC):
                    pool.wait_ge(sem_in, n_done + 2 * c + 2)
                    gp.tensor_tensor(x[:, c, :], x[:, c, :], otmp[:, c, :], ALU.add)
                pool.drain().then_inc(done, 1)

            def moe_pool(l):
                pool.dma_start(rbias, io["router_b"].rearrange("(o e) -> o e", o=1).broadcast_to([P, NE])).then_inc(s["rw_ld"], 16)
                for e in range(NE):
                    gp.memset(rank16[:, e:e + 1], float(NE - e))
                gp.memset(acc, 0.0)
                pool.drain().then_inc(s["moe_zero"], 1)
                q = layer_s[l]
                pool.wait_ge(s["rows_ev"], 2 * l + 2)
                for a in range(2):
                    pool.dma_start(rows_d[l][:, a, :], rows_T[:, a, :]).then_inc(s["rows_st"], 16)
                pool.wait_ge(s["rows_st"], 32 * l + 32)
                with pool.If(pool.value_load(counts[0:1, NE:NE + 1]) <= 2 * CAP):
                    with pool.Fori(0, NE) as e:
                        pool.wait_ge(q["pt_ready"], e + 1)
                        pool.dma_start(row_bc, rows_d[l][bass.ds(e, 1)].broadcast_to([P, 2, T])).then_inc(q["bc_ld"], 16)

            shift(0, 0)
            residual(0, s["out_ev"], s["out_x"])
            shift(1, 3)
            moe_pool(0)
            pool.wait_ge(s["moe_x"], 1)
            ada_aux(1)
            pool.wait_ge(s["ada_mod"], N_SLICE * 4)
            shift(2, 0)
            pool.wait_ge(s["tr_mm"], 6 * 3)
            for d in range(2):
                gp.memset(bd[d], 0.0).then_inc(s["bd_zero"], 1)
            pool.wait_ge(s["bd_zero"], 2)
            for d in range(2):
                for g, n in enumerate(("rg_wa", "rg_wx")):
                    src = io[n][0, d].rearrange("(m u) i j -> u i m j", u=2)
                    for u in range(2):
                        pool.dma_start(bd[d][64 * u:64 * u + 64, g, :, 64 * u:64 * u + 64], src[u]).then_inc(s["bd_ld"], 16)
            residual(6, s["out_ev"], s["out_x"])
            shift(3, 3)
            moe_pool(1)
            pool.wait_ge(s["moe_x"], 2)
            pool.dma_start(fing, io["final_g"].rearrange("(o d) -> o d", o=1).broadcast_to([P, D])).then_inc(s["norm_gl"], 16)

        @block.tensor
        def _(pe):
            def mm(out, pairs):
                for i, (a, b) in enumerate(pairs):
                    last = nc.tensor.matmul(out, a, b, start=(i == 0), stop=(i == len(pairs) - 1))
                return last

            pe.wait_ge(s["consts_ld"], 16)
            pe.wait_ge(s["params_ld"], 10 * 16)
            nc.tensor.transpose(ps[:, 0, 0:48], rows_h, ident[0:48, 0:48])
            nc.tensor.transpose(ps[:, 0, 64:168], rows_r, ident[0:104, 0:104])
            pe.wait_ge(s["silu_c"], 1)
            nc.tensor.transpose(ps[:, 0, 192:208], rows_s, ident[0:16, 0:16]).then_inc(s["par_tr"], 1)
            pe.wait_ge(s["hyp_ld"], 7 * 16)
            nc.tensor.matmul(ps[0:FFN, 1, 0:T], hid[0:EMB, 5, 0:FFN], z_sb, start=True, stop=True).then_inc(s["f1_mm"], 1)
            pe.wait_ge(s["f1_sin"], 1)
            nc.tensor.matmul(ps[0:FFN, 2, 0:T], hid[:, 5, 64:128], hid[:, 3, :], start=True, stop=True).then_inc(s["f2_mm"], 1)
            pe.wait_ge(s["f2_sin"], 1)
            pe.wait_ge(s["w3_ld"], 16)
            pe.wait_ge(s["par_ev"], 1)
            for c in range(TC):
                for f in range(4):
                    t = 4 * c + f
                    if t >= 8:
                        pe.wait_ge(s["filt_dec"], t - 7)
                    mm(ps[:, t % 8, :], [(hid[:, 4, c * P:(c + 1) * P], w3[:, f * 512:(f + 1) * 512])]).then_inc(s["filt_mm"], 1)
            pe.wait_ge(s["tables_ld"], 4 * 16)
            pe.wait_ge(s["filt_dec"], 12)
            pe.wait_ge(s["filt_d"], 2)
            t = 0
            for n in range(2):
                for src, col, c in ((0, 0, 1), (0, 128, 2), (0, 0, 0), (1, 256, 1), (1, 384, 2), (1, 128, 0), (2, 256, 1), (2, 128, 0)):
                    filt = filt_d if src == 1 else filt_s
                    m = 1 if src == 2 else P
                    if t >= 8:
                        pe.wait_ge(s["spec_ev"], t - 7)
                    pairs = ([(dft_p[:, col:col + m], filt[:, 0, n, :])] if c == 0 else
                             [(dft_s[:, k, col:col + m], filt[:, 1 + k, n, :]) for k in range(2)])
                    mm(ps[0:m, t % 8, :], pairs).then_inc(s["spec_mm"], 1)
                    t += 1

            def ada(l):
                for k in range(KD):
                    pe.wait_ge(ada_ld[k % 2], 16 * (l * KD // 2 + k // 2 + 1))
                    lhs = scT[:, :].rearrange("p (c k) -> p k c", c=2)[:, k, :]
                    for n in range(N_SLICE):
                        b, j = divmod(n, 4)
                        last = nc.tensor.matmul(ps[32 * j:32 * j + 2, b, :], lhs, ada_w[:, k % 2, n * 512:(n + 1) * 512],
                                                start=(k == 0), stop=(k == KD - 1))
                    last.then_inc(s["ada_mm"], 1)
                pe.wait_ge(s["ada_row"], 3 * l + 3)
                t = 0
                for c in range(2):
                    for n in range(N_SLICE):
                        b, j = divmod(n, 4)
                        if t >= 5:
                            pe.wait_ge(s["ada_mod"], 2 * N_SLICE * l + t - 4)
                        nc.tensor.matmul(ps[:, 3 + t % 5, :], sel[32 * j:32 * j + 2, c, :], mrow[32 * j:32 * j + 2, b, :],
                                         start=True, stop=True).then_inc(s["ada_bc"], 1)
                        t += 1

            def transposes(i):
                for c in range(TC):
                    pe.wait_ge(s["norm_h2"], 3 * i + c + 1)
                    for half in range(2):
                        for k in range(4):
                            last = nc.tensor.transpose(ps[:, 2 * c + half, k * P:(k + 1) * P],
                                                       h[:, c, (4 * half + k) * P:(4 * half + k + 1) * P], ident)
                        last.then_inc(s["tr_mm"], 1)
                pe.wait_ge(s["tr_act"], 3 * i + 3)
                pe.wait_ge(s["tr_dve"], 3 * i + 3)

            def out_proj(l):
                pe.wait_ge(s["out_ld"], 32 * (l + 1))
                for t in range(6):
                    c, half = divmod(t, 2)
                    mm(ps[:, t, :], [(catT[:, k, c * P:(c + 1) * P], wout[:, k, half * 512:(half + 1) * 512])
                                     for k in range(KD)]).then_inc(s["out_mm"], 1)

            def moe(l):
                pe.wait_ge(s["rw_ld"], 16 * (l + 2))
                for c in range(TC):
                    m_ = mm(ps[:, c, 0:NE], [(hT[:, k, c * P:(c + 1) * P], rw[:, k, :]) for k in range(KD)])
                m_.then_inc(s["rt_mm"], 1)
                pe.wait_ge(s["rt_sig"], l + 1)
                q = layer_s[l]
                pe.wait_ge(s["rt_gates"], l + 1)
                for c in range(TC):
                    mm(ps[:, c, 0:NE], [(ones, R["t1"][:, a, :]) for a in range(c)] + [(tri, R["t1"][:, c, :])])
                mm(ps[0:1, 3, 0:NE], [(ones[:, 0:1], R["t1"][:, a, :]) for a in range(TC)]).then_inc(s["pos_mm"], 1)
                pe.wait_ge(s["pos_ready"], l + 1)
                for a, src in enumerate((posm, gates)):
                    for c in range(TC):
                        last = nc.tensor.transpose(ps[0:NE, 4 + a, c * P:(c + 1) * P], src[:, c, :], ident)
                    last.then_inc(s["rows_mm"], 1)
                pe.wait_ge(s["rows_ev"], 2 * l + 2)
                with pe.If(pe.value_load(counts[0:1, NE:NE + 1]) > 2 * CAP):
                    with pe.Fori(0, NBODY) as i:
                        base = i * BT

                        def gate_up(t):
                            b, c = divmod(t, TC)
                            if c == 0:
                                pe.wait_ge(gu_ld[b], i * 32 + (32 * (NBODY * l + 1)))
                            pe.wait_ge(q["de_act"], base + (t + 1))
                            for w, bank in ((wg[b], 2 * (t % 2)), (wu[b], 2 * (t % 2) + 1)):
                                last = mm(ps[:, bank, :], [(hT[:, k, c * P:(c + 1) * P], w[:, k, :]) for k in range(KD)])
                            last.then_inc(q["de_mm"], 1)
                            if c == TC - 1:
                                pe.drain().then_inc(gu_used[b], 1)

                        def down(t):
                            b, c = divmod(t, TC)
                            pe.wait_ge(q["de_act"], base + (t + 3))
                            pe.wait_ge(q["de_actT"], base + (t + 1))
                            for k in range(KF):
                                last = nc.tensor.transpose(ps[:, 4 + t % 2, k * P:(k + 1) * P],
                                                           act_b[:, t % 2, k * P:(k + 1) * P], ident)
                            last.then_inc(q["de_tr"], 1)
                            if c == 0:
                                pe.wait_ge(dn_ld[b], i * 16 + (16 * (NBODY * l + 1)))
                            pe.wait_ge(q["de_actT"], base + (t + 3))
                            pe.wait_ge(q["de_acc"], base + (t + 1))
                            for half in range(2):
                                last = mm(ps[:, 6 + half, :], [(actT_b[:, t % 2, k * P:(k + 1) * P],
                                                                wd[b][:, k, half * 512:(half + 1) * 512]) for k in range(KF)])
                            last.then_inc(q["de_dn"], 1)
                            if c == TC - 1:
                                pe.drain().then_inc(dn_used[b], 1)

                        for t in range(BT):
                            gate_up(t)
                            if t:
                                down(t - 1)
                        down(BT - 1)

                with pe.Else():
                    def count(e):
                        return pe.value_load(counts[0:1, bass.ds(e, 1)])

                    def gather(e, b):
                        n = count(e)
                        pe.wait_ge(q["p_ready"], e + 1)
                        pe.wait_ge(q["g_ev"], e + 1)

                        def half(r):
                            for k in range(KD):
                                last = mm(ps[:, B_G[r], k * CAP:(k + 1) * CAP],
                                          [(h[:, c, k * P:(k + 1) * P], place[:, b, c, r * CAP:(r + 1) * CAP]) for c in range(TC)])
                            return last
                        with pe.If(n > CAP):
                            half(1)
                        half(0).then_inc(q["g_mm"], 1)

                    def gate_up(i, b):
                        e = i * 2 + b
                        n = count(e)
                        pe.wait_ge(gu_ld[b], i * 32 + (32 * (NBODY * l + 1)))
                        pe.wait_ge(q["g_ev"], e + 2)
                        pe.wait_ge(q["act_ready"], e + 1)

                        def half(r):
                            for w, col in ((wg[b], 0), (wu[b], 256)):
                                for k in range(KD):
                                    for fh in range(2):
                                        last = nc.tensor.matmul(ps[64 * fh:64 * fh + 64, B_GU[r], col:col + 256], hTg[:, r, k, :],
                                                                w[:, k, 256 * fh:256 * fh + 256], start=(k == 0), stop=(k == KD - 1))
                            return last
                        with pe.If(n > CAP):
                            pe.wait_ge(q["y_ev"], e + 1)
                            half(1)
                        half(0).then_inc(q["gu_mm"], 1)
                        pe.drain().then_inc(gu_used[b], 1)

                    def act_transposes(e):
                        n = count(e)
                        pe.wait_ge(q["act_ready"], e + 2)
                        pe.wait_ge(q["tr_ev"], e + 1)

                        def half(r):
                            for j in range(2):
                                last = nc.tensor.transpose(ps[:, B_TR, 256 * r + 128 * j:256 * r + 128 * j + 128],
                                                           act_h[:, r, 128 * j:128 * j + 128], ident)
                            return last
                        with pe.If(n > CAP):
                            half(1)
                        half(0).then_inc(q["tr_mm"], 1)

                    def down(i, b):
                        e = i * 2 + b
                        n = count(e)
                        pe.wait_ge(dn_ld[b], i * 16 + (16 * (NBODY * l + 1)))
                        pe.wait_ge(q["tr_ev"], e + 2)
                        pe.wait_ge(q["y_ev"], e + 1)

                        def half(r):
                            for k in range(KF):
                                for dh in range(2):
                                    last = nc.tensor.matmul(ps[64 * dh:64 * dh + 64, B_DN[r], :],
                                                            actT_h[:, r, k % 2, 64 * (k // 2):64 * (k // 2) + 64],
                                                            wd[b][:, k, 512 * dh:512 * dh + 512], start=(k == 0), stop=(k == KF - 1))
                            return last
                        with pe.If(n > CAP):
                            half(1)
                        half(0).then_inc(q["dn_mm"], 1)
                        pe.drain().then_inc(dn_used[b], 1)

                    def scatter(e, b, c):
                        n = count(e)
                        pe.wait_ge(q["y_ev"], e + 2)
                        pe.wait_ge(q["pt_ready"], e + 2)
                        pe.wait_ge(q["acc_done"], e * 3 + (c + 1))

                        def part(r, start, stop):
                            for dh in range(2):
                                rows = slice(64 * dh, 64 * dh + 64)
                                last = nc.tensor.matmul(ps[:, B_SC + dh, :], place_T[rows, b, r, c * P:(c + 1) * P], y_h[rows, r, :],
                                                        start=start, stop=stop)
                            return last
                        with pe.If(n > CAP):
                            part(1, True, False)
                            part(0, False, True).then_inc(q["sc_mm"], 1)
                        with pe.Else():
                            part(0, True, True).then_inc(q["sc_mm"], 1)

                    def body(i, first=False, last=False):
                        for b in range(2):
                            e = i * 2 + b
                            prev = not (first and b == 0)
                            gate_up(i, b)
                            if prev:
                                scatter(e - 1, 1 - b, 0)
                            if not (last and b == 1):
                                gather(e + 1, 1 - b)
                            if prev:
                                scatter(e - 1, 1 - b, 1)
                            act_transposes(e)
                            if prev:
                                scatter(e - 1, 1 - b, 2)
                            down(i, b)

                    gather(0, 0)
                    body(0, first=True)
                    with pe.Fori(1, NBODY - 1) as i:
                        body(i)
                    body(NBODY - 1, last=True)
                    for c in range(TC):
                        scatter(NE - 1, 1, c)

            for b in range(2):
                pe.sem_inc(gu_used[b], 1)
                pe.sem_inc(dn_used[b], 1)
            for q in layer_s:
                pe.sem_inc(q["de_tr"], 2)
                pe.sem_inc(q["de_dn"], 2)
                pe.sem_inc(q["g_mm"], 2)
                pe.sem_inc(q["gu_mm"], 1)
                pe.sem_inc(q["tr_mm"], 1)
                pe.sem_inc(q["dn_mm"], 1)
                pe.sem_inc(q["sc_mm"], 4)

            pe.wait_ge(s["spec_ev"], 16)
            ada(0)
            pe.wait_ge(s["ada_mod"], 2 * N_SLICE)
            transposes(0)
            t = 0
            for i, nb in enumerate(IN_ORDER):
                pe.wait_ge(in_ld[i % 2], 16 * (i // 2 + 1))
                for m in range(3 if nb == 2 else 4):
                    if t >= 8:
                        u = t - 8
                        if u < 12:
                            pe.wait_ge(s["in_dve"], u + 1)
                        else:
                            pe.wait_ge(s["in_act"], u + 1)
                    if nb == 2:
                        mm(ps[:, t % 8, :], [(hT[:, k, m * P:(m + 1) * P], wblk[:, i % 2, k, :]) for k in range(KD)]).then_inc(s["in_mm"], 1)
                    else:
                        mm(ps[:, t % 8, 0:T], [(wblk[:, i % 2, k, m * P:(m + 1) * P], hT[:, k, :]) for k in range(KD)]).then_inc(s["in_mm"], 1)
                    t += 1
            pe.wait_ge(s["in_act"], 23)
            for c in range(TC):
                for a in range(2):
                    for m in range(4):
                        last = nc.tensor.transpose(ps[:, 2 * c + a, m * P:(m + 1) * P], hy01T[a][:, m, c * P:(c + 1) * P], ident)
                    last.then_inc(s["tok_mm"], 1)
            pe.wait_ge(s["cache_ld"], 32)
            for m in range(4):
                last = nc.tensor.transpose(ps[:, 6, m * P:(m + 1) * P], ck[:, m * P:(m + 1) * P], ident)
            last.then_inc(s["cv_mm"], 1)
            for m in range(4):
                last = nc.tensor.transpose(ps[:, 7, m * P:(m + 1) * P], qkT[:, 4 + m, 0:P], ident)
            last.then_inc(s["cv_mm"], 1)
            pe.wait_ge(s["tok_ev"], 6)
            pe.wait_ge(s["cv_ev"], 2)
            pe.wait_ge(s["spec_fix"], 2)
            for n in range(2):
                if n == 1:
                    pe.wait_ge(s["inv_ev"], 3)
                for a in range(2):
                    for c in range(TC):
                        if c == 0:
                            pairs = [(dft_p[:, a * 128:a * 128 + 128], hy_tok[:, 0, 0, :])]
                        else:
                            col = 256 * a + 128 * (c - 1)
                            pairs = [(dft_s[:, k, col:col + 128], hy_tok[:, 1 + k, 0, :]) for k in range(2)]
                        mm(ps[:, 3 * a + c, :], pairs).then_inc(s["u_mm"], 1)
                pe.wait_ge(s["spec_y"], n + 1)
                if n == 0:
                    for c in range(TC):
                        if c == 0:
                            pairs = [(idft_p[:, a, :], prod[:, a, 0, :]) for a in range(2)]
                        else:
                            pairs = [(idft_s[:, 2 * a + k, (c - 1) * P:c * P], prod[:, a, 1 + k, :])
                                     for a in range(2) for k in range(2)]
                        mm(ps[:, c, :], pairs).then_inc(s["inv_mm"], 1)
                else:
                    for m in range(4):
                        ch = slice(m * P, (m + 1) * P)
                        mm(ps[:, m, 0:LP], [(prod[:, a, 0, ch], idft_p[:, a, :]) for a in range(2)])
                        mm(ps[:, m, LP:T], [(prod[:, a, 1 + k, ch], idft_s[:, 2 * a + k, :])
                                            for a in range(2) for k in range(2)]).then_inc(s["inv_mm"], 1)
            pe.wait_ge(s["inv_ev"], 7)
            for hh in range(H):
                r0 = 64 * (hh % 2)
                rows = slice(r0, r0 + 64)
                for q in range(3):
                    t = 3 * hh + q
                    if t >= 8:
                        pe.wait_ge(s["sc_ev"], t - 7)
                    lhs = qkT[rows, hh // 2, q * P:(q + 1) * P]
                    if q == 0:
                        last = mm(ps[:, t % 8, 0:P], [(lhs, qkT[rows, 4 + hh // 2, 0:P])])
                    else:
                        mm(ps[:, t % 8, 0:LS], [(lhs, qkT[rows, 4 + hh // 2, LP:T])])
                        last = mm(ps[:, t % 8, LS:T], [(lhs, ckT[rows, hh // 2, :])])
                    last.then_inc(s["sc_mm"], 1)
            pe.wait_ge(s["sc_ev"], 24)
            pe.wait_ge(s["at_nrm"], 3)
            for j in range(14):
                if j >= 8:
                    pe.wait_ge(s["pt_ev"], j - 7)
                for k in range(4):
                    hh, i = divmod(4 * j + k, 7)
                    src = (sc_p[:, hh, :] if i == 0 else
                           sc_s[:, (i - 1) // 3, hh, ((i - 1) % 3) * P:((i - 1) % 3 + 1) * P])
                    last = nc.tensor.transpose(ps[:, j % 8, k * P:(k + 1) * P], src, ident)
                last.then_inc(s["pt_mm"], 1)
            pe.wait_ge(s["pt_ev"], 14)

            def pt(hh, i):
                j, k = divmod(7 * hh + i, 4)
                return ptT[:, j, k * P:(k + 1) * P]

            for hh in range(H):
                r0 = 64 * (hh % 2)
                cols = slice(hh * DH, (hh + 1) * DH)
                for q in range(3):
                    t = 3 * hh + q
                    if t >= 8:
                        pe.wait_ge(s["pv_ev"], t - 7)
                    if q == 0:
                        pairs = [(v_tok[:, 0, cols], pt(hh, 0))]
                    else:
                        pairs = [(v_tok[:, 1, cols], pt(hh, 3 * q - 2)), (v_tok[:, 2, cols], pt(hh, 3 * q - 1)),
                                 (cv[:, cols], pt(hh, 3 * q))]
                    mm(ps[r0:r0 + 64, t % 8, 0:P], pairs).then_inc(s["pv_mm"], 1)
            pe.wait_ge(s["pv_ev"], 24)
            out_proj(0)
            pe.wait_ge(s["out_ev"], 6)
            transposes(1)
            moe(0)
            pe.wait_ge(s["moe_x"], 1)
            ada(1)
            pe.wait_ge(s["ada_mod"], 4 * N_SLICE)
            transposes(2)
            t = 0
            for i, nb in enumerate(ODD_ORDER):
                pe.wait_ge(odd_ld[i % 2], 16 * (i // 2 + 1))
                for m in range(4):
                    if t >= 8:
                        pe.wait_ge(s["odd_dve"], t - 7)
                    mm(ps[:, t % 8, 0:T], [(wblk[:, i % 2, k, m * P:(m + 1) * P], hT[:, k, :]) for k in range(KD)]).then_inc(s["odd_mm"], 1)
                    t += 1
            pe.wait_ge(s["odd_act"], 16)
            pe.wait_ge(s["bd_ld"], 8 * 16)
            t = 0
            for d in range(2):
                for g in range(2):
                    for m in range(8):
                        if t >= 8:
                            pe.wait_ge(s["rg_sig"], t - 7)
                        mm(ps[:, t % 8, 0:T], [(bd[d][:, g, m, :], xrT[:, m, :])]).then_inc(s["rg_mm"], 1)
                        t += 1
            pe.wait_ge(s["rg_sig"], 32)
            pe.wait_ge(s["odd_y"], 1)
            nc.tensor.transpose(ps[0:16, 6, 0:P], fin_col.rearrange("p d m -> p (d m)"), ident).then_inc(s["fin_mm"], 1)
            out_proj(1)
            pe.wait_ge(s["out_ev"], 12)
            transposes(3)
            moe(1)

        @block.scalar
        def _(act):
            A = nc.scalar.activation
            act.wait_ge(s["params_ld"], 10 * 16)
            A(rows_s, rows_c, ACT.Silu).then_inc(s["silu_c"], 1)
            act.wait_ge(s["f1_arg"], 1)
            A(hid[:, 3, :], hid[:, 0, :], ACT.Sin).then_inc(s["f1_sin"], 1)
            act.wait_ge(s["f2_arg"], 1)
            A(hid[:, 4, :], hid[:, 0, :], ACT.Sin).then_inc(s["f2_sin"], 1)
            t = 0
            for n in range(2):
                for dst in (spec[:, n, 0, 1, :], spec[:, n, 0, 2, :], spec[:, n, 0, 0, :],
                            spec[:, n, 1, 1, :], spec[:, n, 1, 2, :], spec[:, n, 1, 0, :],
                            c0[:, n, 1, :], c0[:, n, 0, :]):
                    act.wait_ge(s["spec_mm"], t + 1)
                    A(dst, ps[0:dst.shape[0], t % 8, :], ACT.Copy).then_inc(s["spec_ev"], 1)
                    t += 1

            def modulation(l):
                t = 0
                for c in range(2):
                    for n in range(N_SLICE):
                        act.wait_ge(s["ada_bc"], 2 * N_SLICE * l + t + 1)
                        A(mods_t[:, c * 6 * D + n * 512:c * 6 * D + (n + 1) * 512], ps[:, 3 + t % 5, :], ACT.Copy).then_inc(s["ada_mod"], 1)
                        t += 1

            def sumsq(i):
                for c in range(TC):
                    A(h[:, c, :], x[:, c, :], ACT.Square, accum_out=ss[:, c:c + 1])
                act.drain()
                A(rstd, ss, ACT.Sqrt, bias=eps_c, scale=1.0 / D).then_inc(s["norm_ss"], 1)

            def transposed(i):
                for c in range(TC):
                    act.wait_ge(s["tr_mm"], 6 * i + 2 * c + 1)
                    A(hT[:, 0:4, c * P:(c + 1) * P], ps[:, 2 * c, :].rearrange("p (k t) -> p k t", k=4), ACT.Copy).then_inc(s["tr_act"], 1)

            def moe(l):
                act.wait_ge(s["rt_mm"], l + 1)
                A(R["sc"], ps[:, 0:TC, 0:NE], ACT.Sigmoid).then_inc(s["rt_sig"], 1)
                q = layer_s[l]
                for a in range(2):
                    act.wait_ge(s["rows_mm"], 2 * l + a + 1)
                    A(rows_T[:, a, :], ps[0:NE, 4 + a, 0:T], ACT.Copy).then_inc(s["rows_ev"], 1)
                with act.If(act.value_load(counts[0:1, NE:NE + 1]) > 2 * CAP):
                    with act.Fori(0, NBODY) as i:
                        base = i * BT

                        def silu(t):
                            act.wait_ge(q["de_mm"], base + (t + 1))
                            act.wait_ge(q["de_act"], base + (t + 1))
                            A(silu_b[:, t % 2, :], ps[:, 2 * (t % 2), :], ACT.Silu).then_inc(q["de_silu"], 1)

                        def down(t):
                            act.wait_ge(q["de_tr"], base + (t + 3))
                            act.wait_ge(q["de_dn"], base + (t + 1))
                            A(actT_b[:, t % 2, :], ps[:, 4 + t % 2, :], ACT.Copy).then_inc(q["de_actT"], 1)

                        for t in range(BT):
                            silu(t)
                            if t:
                                down(t - 1)
                        down(BT - 1)

                with act.Else():
                    def count(e):
                        return act.value_load(counts[0:1, bass.ds(e, 1)])

                    def gathered(e):
                        n = count(e)

                        def ready():
                            act.wait_ge(q["g_mm"], e + 3)
                            act.wait_ge(q["gu_mm"], e + 1)

                        def half(r):
                            return A(hTg[:, r], ps[:, B_G[r], :].rearrange("p (k n) -> p k n", k=KD), ACT.Copy)
                        with act.If(n > CAP):
                            ready()
                            half(1)
                        ready()
                        half(0).then_inc(q["g_ev"], 1)

                    def silu(e):
                        n = count(e)

                        def ready():
                            act.wait_ge(q["gu_mm"], e + 2)
                            act.wait_ge(q["act_ready"], e + 1)
                        with act.If(n > CAP):
                            ready()
                            A(silu_h[:, 1, :], ps[:, B_GU[1], 0:256], ACT.Silu)
                        ready()
                        A(silu_h[:, 0, :], ps[:, B_GU[0], 0:256], ACT.Silu).then_inc(q["silu_ev"], 1)

                    def transposed_act(e):
                        n = count(e)

                        def ready():
                            act.wait_ge(q["tr_mm"], e + 2)
                            act.wait_ge(q["dn_mm"], e + 1)

                        def half(r):
                            return A(actT_h[:, r], ps[:, B_TR, 256 * r:256 * r + 256].rearrange("p (j n) -> p j n", j=2), ACT.Copy)
                        with act.If(n > CAP):
                            ready()
                            half(1)
                        ready()
                        half(0).then_inc(q["tr_ev"], 1)

                    def y_out(e):
                        n = count(e)

                        def ready():
                            act.wait_ge(q["dn_mm"], e + 2)
                            act.wait_ge(q["sc_mm"], e * 3 + 4)
                        with act.If(n > CAP):
                            ready()
                            A(y_h[:, 1, :], ps[:, B_DN[1], :], ACT.Copy)
                        ready()
                        A(y_h[:, 0, :], ps[:, B_DN[0], :], ACT.Copy).then_inc(q["y_ev"], 1)

                    def body(i, last=False):
                        for b in range(2):
                            e = i * 2 + b
                            silu(e)
                            if not (last and b == 1):
                                gathered(e + 1)
                            transposed_act(e)
                            y_out(e)

                    gathered(0)
                    with act.Fori(0, NBODY - 1) as i:
                        body(i)
                    body(NBODY - 1, last=True)

            for q in layer_s:
                act.sem_inc(q["de_actT"], 2)
                act.sem_inc(q["g_ev"], 1)
                act.sem_inc(q["tr_ev"], 1)
                act.sem_inc(q["y_ev"], 1)
            modulation(0)
            act.wait_ge(s["x_ld"], 32)
            act.wait_ge(s["spec_mm"], 16)
            act.wait_ge(s["par_ev"], 2)
            sumsq(0)
            transposed(0)
            for t in range(23):
                act.wait_ge(s["in_mm"], t + 1)
                if t < 12:
                    dst = hy01T[t // 4][:, t % 4, :] if t < 8 else hy2T[:, t - 8, :]
                    A(dst, ps[:, t % 8, 0:T], ACT.Identity, bias=parH[:, 36 + t:37 + t], scale=parH[:, 12 + t:13 + t]).then_inc(s["in_act"], 1)
                elif t < 20:
                    A(qkT[:, t - 12, :], ps[:, t % 8, 0:T], ACT.Copy).then_inc(s["in_act"], 1)
                else:
                    A(v_tok[:, t - 20, :], ps[:, t % 8, :], ACT.Copy).then_inc(s["in_act"], 1)
            act.wait_ge(s["in_act"], 23)
            act.dma_start(io["new_v"][0, 0].rearrange("h t d -> t h d"), v_tok[:, 0, :].rearrange("p (h d) -> p h d", h=H)).then_inc(s["kv_out"], 16)
            act.wait_ge(s["cv_mm"], 1)
            A(ckT, ps[:, 6, :].rearrange("p (m t) -> p m t", m=4), ACT.Copy).then_inc(s["cv_ev"], 1)
            act.wait_ge(s["cv_mm"], 2)
            A(k_tok, ps[:, 7, :], ACT.Copy).then_inc(s["cv_ev"], 1)
            act.wait_ge(s["cv_ev"], 2)
            act.dma_start(io["new_k"][0, 0].rearrange("h t d -> t h d"), k_tok.rearrange("p (h d) -> p h d", h=H)).then_inc(s["kv_out"], 16)
            for q in range(3):
                act.wait_ge(s["at_max"], q + 1)
                for hh in range(H):
                    buf = sc_p[:, hh, :] if q == 0 else sc_s[:, q - 1, hh, :]
                    last = A(buf, buf, ACT.Exp, bias=amax[:, q, hh:hh + 1], accum_out=asum[:, q, hh:hh + 1])
                act.drain().then_inc(s["at_exp"], 1)
            for j in range(14):
                act.wait_ge(s["pt_mm"], j + 1)
                A(ptT[:, j, :], ps[:, j % 8, :], ACT.Copy).then_inc(s["pt_ev"], 1)
            act.wait_ge(s["out_x"], 1)
            sumsq(1)
            transposed(1)
            moe(0)
            modulation(1)
            act.wait_ge(s["moe_x"], 1)
            sumsq(2)
            transposed(2)
            act.wait_ge(s["rg_lamok"], 1)
            A(spt[:, 1, :], spt[:, 0, :], ACT.Exp, scale=-1.0).then_inc(s["sp_e"], 1)
            act.wait_ge(s["rg_lamok"], 2)
            A(spt[:, 3, :], spt[:, 2, :], ACT.Ln).then_inc(s["sp_ln"], 1)
            for t in range(16):
                act.wait_ge(s["odd_mm"], t + 1)
                if t < 8:
                    A(xrT[:, t, :], ps[:, t % 8, 0:T], ACT.Identity, bias=parR[:, 32 + t:33 + t], scale=parR[:, 16 + t:17 + t]).then_inc(s["odd_act"], 1)
                else:
                    A(geluT[:, t - 8, :], ps[:, t % 8, 0:T], ACT.Gelu_apprx_tanh).then_inc(s["odd_act"], 1)
            for d in range(2):
                for g in range(2):
                    for m in range(8):
                        t = (2 * d + g) * 8 + m
                        act.wait_ge(s["rg_mm"], t + 1)
                        if d == 1 and m == 0 and g == 0:
                            act.wait_ge(s["rg_th"], 1)
                            act.wait_ge(s["rg_scan"], 1)
                        dst = (rr if g == 0 else ri)[:, m, :]
                        A(dst, ps[:, t % 8, 0:T], ACT.Sigmoid, bias=parR[:, 40 + 16 * g + 8 * d + m:41 + 16 * g + 8 * d + m]).then_inc(s["rg_sig"], 1)
                act.wait_ge(s["rg_lamok"], 3)
                act.wait_ge(s["rg_sig"], 16 * d + 16)
                for m in range(8):
                    A(ra[:, m, :], rr[:, m, :], ACT.Exp, scale=s_rg[:, 8 * d + m:8 * d + m + 1]).then_inc(s["rg_a"], 1)
                for m in range(8):
                    A(rt[:, m, :], rr[:, m, :], ACT.Tanh, scale=s_rg[:, 8 * d + m:8 * d + m + 1]).then_inc(s["rg_th"], 1)
                act.wait_ge(s["rg_b"], 2 * d + 1)
                A(rt, rt, ACT.Sqrt).then_inc(s["rg_th"], 1)
            act.wait_ge(s["fin_mm"], 1)
            A(fin_row, ps[0:16, 6, 0:P], ACT.Copy).then_inc(s["fin_ev"], 1)
            act.wait_ge(s["fin_ev"], 1)
            act.dma_start(io["new_h"][0, 0].rearrange("d (m p) -> (d m) p", p=P), fin_row).then_inc(s["fin_out"], 16)
            act.wait_ge(s["out_x"], 2)
            sumsq(3)
            transposed(3)
            act.wait_ge(s["fin_out"], 16)
            moe(1)
            act.wait_ge(s["moe_x"], 2)
            sumsq(4)

        @block.vector
        def _(v):
            V = nc.vector
            V.memset(eps_c, EPS)
            for q in layer_s:
                v.sem_inc(q["de_act"], 2)
                v.sem_inc(q["de_acc"], 1)
                v.sem_inc(q["act_ready"], 1)
                v.sem_inc(q["pt_ready"], 1)
                v.sem_inc(q["acc_done"], 1)
            v.wait_ge(s["par_tr"], 1)
            V.tensor_copy(parH[:, :], ps[:, 0, 0:48])
            V.tensor_copy(parR[:, :], ps[:, 0, 64:168])
            V.tensor_copy(scT[:, :], ps[:, 0, 192:208]).then_inc(s["par_ev"], 2)
            v.wait_ge(s["hyp_ld"], 7 * 16)
            for i, (mm_, done, bank) in enumerate(((s["f1_mm"], s["f1_arg"], 1), (s["f2_mm"], s["f2_arg"], 2))):
                v.wait_ge(mm_, 1)
                a, b, k = hid[:, 0, :], hid[:, 1, :], hid[:, 2, :]
                if i == 1:
                    v.wait_ge(s["f1_sin"], 1)
                V.tensor_scalar(a, ps[0:FFN, bank, 0:T], hyp[:, i:i + 1], hyp[:, 2 + i:3 + i], ALU.add, ALU.mult)
                v.drain()
                V.tensor_scalar(b, a, 1.0 / TWO_PI, ROUND, ALU.mult, ALU.add)
                v.drain()
                V.tensor_scalar(k, b, ROUND, None, ALU.subtract)
                v.drain()
                V.scalar_tensor_tensor(b, k, -PI1, a, ALU.mult, ALU.add)
                v.drain()
                V.scalar_tensor_tensor(a, k, -PI2, b, ALU.mult, ALU.add)
                v.drain()
                V.tensor_scalar(a, a, 3.1415925, -3.1415925, ALU.min, ALU.max).then_inc(done, 1)
            v.wait_ge(s["decay_ld"], 16)
            for c in range(TC):
                if c == 2:
                    v.wait_ge(s["filt_sd"], 2)
                for f in range(4):
                    t = 4 * c + f
                    v.wait_ge(s["filt_mm"], t + 1)
                    V.tensor_tensor(ftmp[:, c % 2, f, :], ps[:, t % 8, :], decay[:, c, :], ALU.mult).then_inc(s["filt_dec"], 1)

            def ada_rows(l):
                v.wait_ge(s["ada_aux"], 256 * (l + 1))
                v.wait_ge(s["ada_mm"], KD * (l + 1))
                for j in range(4):
                    r = slice(32 * j, 32 * j + 2)
                    last = V.tensor_tensor(mrow[r], ps[r, 0:3, :], adab[r], ALU.add)
                last.then_inc(s["ada_row"], 1)
                v.drain()
                for j, b in ((2, 0), (3, 0), (0, 2), (1, 2)):
                    r = slice(32 * j, 32 * j + 2)
                    last = V.scalar_tensor_tensor(mrow[r, b, :], mrow[r, b, :], 1.0, gt[r, :], ALU.add, ALU.mult)
                last.then_inc(s["ada_row"], 2)

            def norm(i, row):
                v.wait_ge(s["norm_ss"], i + 1)
                V.reciprocal(rstd, rstd)
                v.drain()
                for cond, c0_, c1_ in SUBS:
                    for c in range(c0_, c1_):
                        V.scalar_tensor_tensor(h[:, c, :], x[:, c, :], rstd[:, c:c + 1], mods[:, cond, row, :],
                                               ALU.mult, ALU.mult).then_inc(s["norm_h"], 1)

            def transposed(i):
                for c in range(TC):
                    v.wait_ge(s["tr_mm"], 6 * i + 2 * c + 2)
                    V.tensor_copy(hT[:, 4:8, c * P:(c + 1) * P], ps[:, 2 * c + 1, :].rearrange("p (k t) -> p k t", k=4)).then_inc(s["tr_dve"], 1)

            def gated(l):
                for t in range(6):
                    c, half = divmod(t, 2)
                    v.wait_ge(s["out_mm"], 6 * l + t + 1)
                    V.tensor_tensor(otmp[:, c, half * 512:(half + 1) * 512], ps[:, t, :],
                                    mods[:, min(c, 1), 2, half * 512:(half + 1) * 512], ALU.mult).then_inc(s["out_ev"], 1)

            def first_max(dst, vals, mx, rank, n):
                V.tensor_reduce(mx, vals, AX.X, ALU.max)
                v.drain()
                V.tensor_tensor(dst, vals, mx.broadcast_to([P, TC, n]), ALU.is_equal)
                v.drain()
                V.tensor_tensor(dst, dst, rank, ALU.mult)
                v.drain()
                V.tensor_reduce(mx, dst, AX.X, ALU.max)
                v.drain()
                V.tensor_tensor(dst, dst, mx.broadcast_to([P, TC, n]), ALU.is_equal)
                v.drain()

            def router(l):
                v.wait_ge(s["rt_sig"], l + 1)
                v.wait_ge(s["moe_zero"], l + 1)
                rk = rank16[:, None, :].broadcast_to([P, TC, NE])
                V.tensor_tensor(R["sel"], R["sc"], rbias[:, None, :].broadcast_to([P, TC, NE]), ALU.add)
                v.drain()
                g4 = R["sel"].rearrange("p c (g o) -> p c g o", g=NG)
                for i, (a, b) in enumerate(((0, 1), (0, 2), (0, 3), (1, 2), (1, 3), (2, 3))):
                    V.tensor_tensor(pr6[:, :, :, i], g4[:, :, :, a], g4[:, :, :, b], ALU.add)
                v.drain()
                V.tensor_reduce(gsc, pr6, AX.X, ALU.max)
                v.drain()
                first_max(gin, gsc, r1, rk[:, :, 0:NG], NG)
                V.tensor_scalar(geq, gin, 1.0, BIG, ALU.subtract, ALU.mult)
                v.drain()
                m4 = R["msk"].rearrange("p c (g o) -> p c g o", g=NG)
                for o in range(EPG):
                    V.tensor_tensor(m4[:, :, :, o], g4[:, :, :, o], gin, ALU.mult)
                v.drain()
                for o in range(EPG):
                    V.tensor_tensor(m4[:, :, :, o], m4[:, :, :, o], geq, ALU.add)
                v.drain()
                first_max(R["t1"], R["msk"], r1, rk, NE)
                V.scalar_tensor_tensor(R["m2"], R["t1"], -2 * BIG, R["msk"], ALU.mult, ALU.add)
                v.drain()
                first_max(R["t2"], R["m2"], r1, rk, NE)
                V.tensor_tensor(R["t1"], R["t1"], R["t2"], ALU.add)
                v.drain()
                V.tensor_tensor(R["sm"], R["t1"], R["sc"], ALU.mult)
                v.drain()
                V.tensor_reduce(r2, R["sm"], AX.X, ALU.add)
                v.drain()
                V.reciprocal(r2, r2)
                v.drain()
                V.tensor_tensor(gates, R["sm"], r2.broadcast_to([P, TC, NE]), ALU.mult).then_inc(s["rt_gates"], 1)
                v.drain()

            def moe(l):
                router(l)
                gates_e = gates.rearrange("p c e -> p (c e)")
                q = layer_s[l]
                v.wait_ge(s["pos_mm"], l + 1)
                V.tensor_tensor(posm, R["t1"], ps[:, 0:TC, 0:NE], ALU.mult)
                V.tensor_copy(cnt_f[:, 0:NE], ps[0:1, 3, 0:NE])
                v.drain()
                V.tensor_scalar(posm, posm, -1.0, None, ALU.add)
                V.tensor_reduce(cnt_f[:, NE:NE + 1], cnt_f[:, 0:NE], AX.X, ALU.max)
                v.drain()
                V.tensor_copy(counts[:, :], cnt_f)
                v.drain().then_inc(s["pos_ready"], 1)
                posm_e = posm.rearrange("p c e -> p (c e)")
                with v.If(v.value_load(counts[0:1, NE:NE + 1]) > 2 * CAP):
                    with v.Fori(0, NBODY) as i:
                        base = i * BT

                        def act_(t):
                            b, c = divmod(t, TC)
                            v.wait_ge(q["de_silu"], base + (t + 1))
                            v.wait_ge(q["de_tr"], base + (t + 1))
                            V.scalar_tensor_tensor(act_b[:, t % 2, :], silu_b[:, t % 2, :], gates_e[:, bass.ds(i * 2 + (NE * c + b), 1)],
                                                   ps[:, 2 * (t % 2) + 1, :], ALU.mult, ALU.mult).then_inc(q["de_act"], 1)

                        def sum_(t):
                            c = t % TC
                            v.wait_ge(q["de_dn"], base + (t + 3))
                            a = acc[:, c, :].rearrange("p (a n) -> p a n", a=2)
                            V.tensor_tensor(a, a, ps[:, 6:8, :], ALU.add).then_inc(q["de_acc"], 1)

                        for t in range(BT):
                            act_(t)
                            if t:
                                sum_(t - 1)
                        sum_(BT - 1)
                with v.Else():
                    def count(e):
                        return v.value_load(counts[0:1, bass.ds(e, 1)])

                    def places(e, b):
                        v.wait_ge(q["g_mm"], e + 1)
                        for c in range(TC):
                            last = V.tensor_scalar(place[:, b, c, :], slot_row, posm_e[:, bass.ds(e + NE * c, 1)], None, ALU.is_equal)
                        last.then_inc(q["p_ready"], 1)

                    def places_T(e, b):
                        n = count(e)

                        def ready():
                            v.wait_ge(q["bc_ld"], e * 16 + 16)
                            v.wait_ge(q["sc_mm"], e * 3 + 1)

                        def half(r):
                            return V.scalar_tensor_tensor(place_T[:, b, r, :], row_bc[:, 0, :], slot_col[:, r:r + 1], row_bc[:, 1, :],
                                                          ALU.is_equal, ALU.mult)
                        with v.If(n > CAP):
                            ready()
                            half(1)
                        ready()
                        half(0).then_inc(q["pt_ready"], 1)

                    def act_(e):
                        n = count(e)

                        def ready():
                            v.wait_ge(q["silu_ev"], e + 1)
                            v.wait_ge(q["tr_mm"], e + 1)

                        def half(r):
                            return V.tensor_tensor(act_h[:, r, :], silu_h[:, r, :], ps[:, B_GU[r], 256:512], ALU.mult)
                        with v.If(n > CAP):
                            ready()
                            half(1)
                        ready()
                        half(0).then_inc(q["act_ready"], 1)

                    def sums(e):
                        for c in range(TC):
                            v.wait_ge(q["sc_mm"], e * 3 + (c + 5))
                            a = acc[:, c, :].rearrange("p (a n) -> p a n", a=2)
                            V.tensor_tensor(a, a, ps[:, B_SC:B_SC + 2, :], ALU.add).then_inc(q["acc_done"], 1)

                    def body(i, first=False, last=False):
                        for b in range(2):
                            e = i * 2 + b
                            if not (last and b == 1):
                                places(e + 1, 1 - b)
                            places_T(e, b)
                            act_(e)
                            if not (first and b == 0):
                                sums(e - 1)

                    places(0, 0)
                    body(0, first=True)
                    with v.Fori(1, NBODY - 1) as i:
                        body(i)
                    body(NBODY - 1, last=True)
                    sums(NE - 1)
                v.drain()
                for c in range(TC):
                    V.tensor_tensor(acc[:, c, :], acc[:, c, :], mods[:, min(c, 1), 5, :], ALU.mult)
                v.drain()
                V.tensor_tensor(x, x, acc, ALU.add).then_inc(s["moe_x"], 1)

            ada_rows(0)
            v.wait_ge(s["ada_mod"], 2 * N_SLICE)
            norm(0, 1)
            transposed(0)
            for t in range(12):
                dst = hy01T[t // 4][:, t % 4, :] if t < 8 else hy2T[:, t - 8, :]
                v.wait_ge(s["in_act"], t + 1)
                for lo, hi in SEGS:
                    V.scalar_tensor_tensor(dst[:, lo + 1:hi], ps[:, t % 8, lo:hi - 1], parH[:, t:t + 1],
                                           dst[:, lo + 1:hi], ALU.mult, ALU.add)
                v.drain()
                for lo, hi in SEGS:
                    last = V.scalar_tensor_tensor(dst[:, lo:hi - 1], ps[:, t % 8, lo + 1:hi], parH[:, 24 + t:25 + t],
                                                  dst[:, lo:hi - 1], ALU.mult, ALU.add)
                last.then_inc(s["in_dve"], 1)
            for t in range(6):
                v.wait_ge(s["tok_mm"], t + 1)
                V.tensor_copy(hy_tok[:, t // 2, t % 2, :], ps[:, t, :]).then_inc(s["tok_ev"], 1)
            for n in range(2):
                v.wait_ge(s["u_mm"], 6 * n + 6)
                v.wait_ge(s["spec_fix"], 2)
                Ur, Ui = ps[:, 0:3, :], ps[:, 3:6, :]
                A_, B_ = spec[:, n, 0], spec[:, n, 1]
                V.tensor_tensor(ptmp[:, 0], Ur, A_, ALU.mult)
                V.tensor_tensor(ptmp[:, 1], Ui, B_, ALU.mult)
                v.drain()
                V.tensor_tensor(prod[:, 0], ptmp[:, 0], ptmp[:, 1], ALU.subtract)
                v.drain()
                V.tensor_tensor(ptmp[:, 0], Ur, B_, ALU.mult)
                V.tensor_tensor(ptmp[:, 1], Ui, A_, ALU.mult)
                v.drain()
                V.tensor_tensor(prod[:, 1], ptmp[:, 0], ptmp[:, 1], ALU.add)
                v.drain()
                V.tensor_tensor(prod[0:1, 1, 0:2, :], ps[0:1, 3:5, :], c0[:, n], ALU.mult).then_inc(s["spec_y"], 1)
                if n == 0:
                    for c in range(TC):
                        v.wait_ge(s["inv_mm"], c + 1)
                        V.tensor_tensor(hy_tok[:, c, 0, :], ps[:, c, :], hy_tok[:, c, 1, :], ALU.mult).then_inc(s["inv_ev"], 1)
                else:
                    for m in range(4):
                        v.wait_ge(s["inv_mm"], 4 + m)
                        V.tensor_tensor(catT[:, 4 + m, :], ps[:, m, 0:T], hy2T[:, m, :], ALU.mult).then_inc(s["inv_ev"], 1)
            v.wait_ge(s["bias_ok"], H)
            for hh in range(H):
                for q in range(3):
                    t = 3 * hh + q
                    v.wait_ge(s["sc_mm"], t + 1)
                    if q == 0:
                        V.tensor_scalar(sc_p[:, hh, :], ps[:, t % 8, 0:P], SCALE, None, ALU.mult).then_inc(s["sc_ev"], 1)
                    else:
                        b0 = 3 - 2 * (q - 1)
                        V.scalar_tensor_tensor(sc_s[:, q - 1, hh, 0:LS].rearrange("p (r k) -> p r k", r=4),
                                               ps[:, t % 8, 0:LS].rearrange("p (r k) -> p r k", r=4), SCALE,
                                               bias[:, hh, b0:b0 + 4, ::-1], ALU.mult, ALU.add)
                        V.tensor_scalar(sc_s[:, q - 1, hh, LS:T], ps[:, t % 8, LS:T], SCALE, None, ALU.mult).then_inc(s["sc_ev"], 1)
            v.drain()
            for q in range(3):
                V.tensor_reduce(amax[:, q, :], sc_p if q == 0 else sc_s[:, q - 1], AX.X, ALU.max)
                v.drain()
                V.tensor_scalar(amax[:, q, :], amax[:, q, :], -1.0, None, ALU.mult).then_inc(s["at_max"], 1)
            for q in range(3):
                v.wait_ge(s["at_exp"], q + 1)
                V.reciprocal(arcp[:, q, :], asum[:, q, :])
                v.drain()
                buf = sc_p if q == 0 else sc_s[:, q - 1]
                V.tensor_tensor(buf, buf, arcp[:, q, :, None].broadcast_to([P, H, P if q == 0 else T]), ALU.mult).then_inc(s["at_nrm"], 1)
            for hh in range(H):
                r0 = 64 * (hh % 2)
                for q in range(3):
                    t = 3 * hh + q
                    v.wait_ge(s["pv_mm"], t + 1)
                    V.tensor_copy(catT[r0:r0 + 64, hh // 2, q * P:(q + 1) * P], ps[r0:r0 + 64, t % 8, 0:P]).then_inc(s["pv_ev"], 1)
            gated(0)
            norm(1, 4)
            transposed(1)
            moe(0)
            ada_rows(1)
            v.wait_ge(s["ada_mod"], 4 * N_SLICE)
            norm(2, 1)
            transposed(2)
            lam = parR[:, 72:88]
            V.tensor_scalar(spt[:, 4, :], lam, -1.0, None, ALU.mult)
            v.drain()
            V.tensor_tensor(spt[:, 0, :], lam, spt[:, 4, :], ALU.max).then_inc(s["rg_lamok"], 1)
            v.wait_ge(s["sp_e"], 1)
            V.tensor_scalar(spt[:, 2, :], spt[:, 1, :], 1.0, None, ALU.add).then_inc(s["rg_lamok"], 1)
            for t in range(8):
                dst = xrT[:, t, :]
                v.wait_ge(s["odd_act"], t + 1)
                for tap, sh in ((0, -2), (1, -1), (3, 1)):
                    for lo, hi in SEGS:
                        a, b = max(lo, lo - sh), min(hi, hi - sh)
                        last = V.scalar_tensor_tensor(dst[:, a:b], ps[:, t % 8, a + sh:b + sh], parR[:, 8 * tap + t:8 * tap + t + 1],
                                                      dst[:, a:b], ALU.mult, ALU.add)
                    if tap != 3:
                        v.drain()
                last.then_inc(s["odd_dve"], 1)
            v.wait_ge(s["sp_ln"], 1)
            V.tensor_scalar(spt[:, 5, :], spt[:, 2, :], -1.0, 1e-30, ALU.add, ALU.max)
            v.drain()
            V.reciprocal(spt[:, 6, :], spt[:, 5, :])
            V.tensor_tensor(spt[:, 3, :], spt[:, 3, :], spt[:, 1, :], ALU.mult)
            v.drain()
            V.tensor_tensor(spt[:, 3, :], spt[:, 3, :], spt[:, 6, :], ALU.mult)
            V.tensor_scalar(spt[:, 7, :], spt[:, 2, :], 1.0, None, ALU.is_equal)
            v.drain()
            V.tensor_tensor(spt[:, 7, :], spt[:, 7, :], spt[:, 1, :], ALU.mult)
            v.drain()
            V.tensor_tensor(spt[:, 3, :], spt[:, 3, :], spt[:, 7, :], ALU.add)
            V.tensor_scalar(spt[:, 4, :], spt[:, 4, :], 0.0, None, ALU.max)
            v.drain()
            V.tensor_tensor(spt[:, 3, :], spt[:, 3, :], spt[:, 4, :], ALU.add)
            v.drain()
            V.tensor_scalar(s_rg, spt[:, 3, :], -8.0, None, ALU.mult).then_inc(s["rg_lamok"], 1)
            for d in range(2):
                v.wait_ge(s["rg_sig"], 16 * d + 16)
                V.tensor_tensor(ri, ri, xrT, ALU.mult)
                v.wait_ge(s["rg_a"], 8 * d + 8)
                v.wait_ge(s["rg_th"], 9 * d + 8)
                V.tensor_tensor(rr, ra, ra, ALU.mult)
                v.drain()
                V.scalar_tensor_tensor(rt, rr, 1.0, rt, ALU.add, ALU.mult)
                v.drain()
                V.tensor_scalar(rt, rt, -1.0, 0.0, ALU.mult, ALU.max).then_inc(s["rg_b"], 1)
                v.wait_ge(s["rg_th"], 9 * d + 9)
                V.tensor_tensor(ri, ri, rt, ALU.mult).then_inc(s["rg_b"], 1)
                v.drain()
                out = catT if d == 0 else rr
                for m in range(8):
                    for lo, hi in SEGS:
                        init = 0.0 if lo == 0 else parR[:, 88 + 8 * d + m:89 + 8 * d + m]
                        o_, a_, b_ = out[:, m, lo:hi], ra[:, m, lo:hi], ri[:, m, lo:hi]
                        if d == 1:
                            o_, a_, b_ = o_[:, ::-1], a_[:, ::-1], b_[:, ::-1]
                        V.tensor_tensor_scan(o_, a_, b_, init, ALU.mult, ALU.add)
                v.drain()
                V.tensor_copy(fin_col[:, d, :], out[:, :, LP - 1] if d == 0 else out[:, :, 0])
                v.drain().then_inc(s["rg_scan"], 1)
            v.wait_ge(s["odd_act"], 16)
            V.tensor_tensor(catT, catT, rr, ALU.add)
            v.drain()
            V.tensor_tensor(catT, catT, geluT, ALU.mult)
            v.drain().then_inc(s["odd_y"], 1)
            gated(1)
            norm(3, 4)
            transposed(3)
            moe(1)
            v.wait_ge(s["norm_ss"], 5)
            V.reciprocal(rstd, rstd)
            v.drain()
            v.wait_ge(s["norm_gl"], 16)
            for c in range(TC):
                V.scalar_tensor_tensor(h[:, c, :], x[:, c, :], rstd[:, c:c + 1], fing, ALU.mult, ALU.mult).then_inc(s["y_ready"], 1)


_INS = ["x_prompt", "x_sample", "cache_k", "cache_v", "state_h", "c", "c_ctx", "norm_g", "ada_w", "ada_b",
        "final_g", "a_in_w", "a_out_w", "na_rpb", "hy_short_w", "hy_short_b", "hy_w1", "hy_b1", "hy_w2",
        "hy_b2", "hy_w3", "hy_freq", "hy_d", "c_in_w", "c_out_w", "rg_conv_w", "rg_conv_b", "rg_wa", "rg_ba",
        "rg_wx", "rg_bx", "rg_lam", "router_w", "router_b", "moe_w_gate", "moe_w_up", "moe_w_down"]
_OUTS = [("y_prompt", (1, LP, D)), ("y_sample", (1, LS, D)), ("new_k", (1, 1, H, LP, DH)),
         ("new_v", (1, 1, H, LP, DH)), ("new_h", (1, 1, 2, D))]


def kernel(**inputs):
    import concourse.bacc as bacc
    from concourse.bass_utils import run_bass_kernel_spmd

    nc = bacc.Bacc("TRN2", target_bir_lowering=False, num_devices=1)
    arrays, io = {}, {}
    for name in _INS:
        a = np.asarray(inputs[name])
        if name == "na_rpb":
            a = a[..., ::-1]
        a = np.ascontiguousarray(a)
        arrays["in_" + name] = a
        io[name] = nc.dram_tensor("in_" + name, a.shape, mybir.dt.from_np(a.dtype), kind="ExternalInput").ap()
    for name, a in shape_constants().items():
        a = np.ascontiguousarray(a)
        arrays[name] = a
        io[name] = nc.dram_tensor(name, a.shape, FP, kind="ExternalInput").ap()
    for name, shape in _OUTS:
        io[name] = nc.dram_tensor("out_" + name, shape, FP, kind="ExternalOutput").ap()
    build(nc, io)
    r = run_bass_kernel_spmd(nc, [arrays], core_ids=[0])
    return tuple(r.results[0]["out_" + name] for name, _ in _OUTS)
```

```python
import math
from contextlib import ExitStack

import numpy as np
import concourse.bass as bass
from concourse import mybir

FP = mybir.dt.float32
ALU = mybir.AluOpType
ACT = mybir.ActivationFunctionType
AX = mybir.AxisListType

P = 128
D = 1024
KD = D // P
LP, LS = 128, 256
T = LP + LS
TC = T // P
DEPTH = 2
H, DH = 8, 64
DA = H * DH
DB = D - DA
GRID_W, ROWS = 64, 4
WIN_COLS, WIN_ROWS = 16, 8
RPB_C = 2 * WIN_COLS - 1
RPB_R = 2 * WIN_ROWS - 1
EMB, FFN = 33, 64
NE, NG, EPG = 16, 4, 4
F = 512
KF = F // P
CAP = 64
EPS = 1e-6
BIG = 1e30
SCALE = DH ** -0.5
TWO_PI = 2 * math.pi
PI1 = 6.28125
PI2 = float(np.float32(TWO_PI - PI1))
ROUND = 12582912.0
SEGS = ((0, LP), (LP, T))
SUBS = ((0, 0, 1), (1, 1, 3))
N_SLICE = 6 * D // 512


def shape_constants():
    c = {}
    ident = np.eye(P, dtype=np.float32)
    cols = np.arange(GRID_W)
    start = np.clip(cols - WIN_COLS // 2, 0, GRID_W - WIN_COLS)
    inside = (cols[None, :] >= start[:, None]) & (cols[None, :] < start[:, None] + WIN_COLS)
    mask = np.where(inside, 0.0, -BIG).astype(np.float32)[:, ::-1]
    c["k_const"] = np.concatenate([ident, np.concatenate([mask, mask]),
                                   np.triu(np.ones((P, P), np.float32)), np.ones((P, P), np.float32),
                                   np.tile(np.arange(P, dtype=np.float32), (P, 1)),
                                   np.tile(NE - np.arange(NE, dtype=np.float32), (P, 1))], axis=1)
    zs, decs = [], []
    for L in (LP, LS):
        t = np.linspace(0.0, 1.0, L, dtype=np.float32)[:, None]
        w = (2.0 * math.pi * np.arange(L, dtype=np.float32)[:, None] / L).astype(np.float32)
        f = np.linspace(1e-4, 15, 16, dtype=np.float32)[None, :]
        zs.append(np.concatenate([t, np.cos(f * w), -np.sin(f * w)], axis=-1))
        lo, hi = math.log(1e-2) / 1.5, math.log(1e-2) / 0.3
        deltas = np.linspace(lo, hi, DB, dtype=np.float32)
        decs.append(np.exp(-t * np.abs(deltas)))
    c["k_z"] = np.ascontiguousarray(np.concatenate(zs).T.astype(np.float32))
    c["k_decay"] = np.concatenate(decs).astype(np.float32)
    for tag, L in (("p", LP), ("s", LS)):
        n = 2 * L
        t, k = np.arange(L)[:, None], np.arange(L)[None, :]
        ang = 2 * np.pi * ((t * k) % n) / n
        re, im = np.cos(ang), -np.sin(ang)
        im[:, 0] = (-1.0) ** np.arange(L)
        c["k_dft_" + tag] = np.concatenate([re, im], axis=1).astype(np.float32)
        wt = np.full((L, 1), 2.0 / n)
        wt[0] = 1.0 / n
        c["k_idft_" + tag] = np.concatenate([re.T * wt, im.T * wt], axis=0).astype(np.float32)
    return c


SEM_NAMES = """consts_ld x_ld tables_ld hyp_ld w3_ld decay_ld params_ld rw_ld
silu_c pad_z par_tr par_ev
net_mm net_arg net_sin filt_mm filt_dec filt_sd
spec_mm spec_ev spec_fix
ada_ld0 ada_ld1 ada_aux ada_mm ada_row ada_bc ada_mod mod_dma
norm_ss norm_h tr_mm tr_act tr_dve
in_ld0 in_ld1 in_mm in_act in_dve
tok_mm tok_ev
cache_ld bias_ld bias_ok cv_mm cv_ev
u_mm spec_y inv_mm inv_ev
sc_mm sc_ev at_max at_exp at_nrm pt_mm pt_ev pv_mm pv_ev
out_ld0 out_ld1 half_mm half_ev out_mm out_ev out_x
rt_mm rt_sig rt_gates
gu_ld0 gu_ld1 dn_ld0 dn_ld1 g_used0 g_used1 gu_used0 gu_used1 dn_used0 dn_used1
moe_x mrow_z zeros_ok zero_st pos_mm pos_ready
kv_out
odd_mm odd_act odd_dve bd_zero bd_ld rg_mm rg_sig rg_a rg_sq rg_b rg_scan sp_exp rg_lamok
fin_mm fin_ev fin_out odd_y
norm_gl y_ready y_out""".split()
LAYER_SEMS = """de_mm de_silu de_act de_tr de_actT de_dn de_acc
g_mm rows_ev gt_mm g_ev p_ready gu_mm silu_ev act_ready tr_mm tr_ev dn_mm y_ev y_st0 y_st1 back_ld0 back_ld1 back_ld2 back_w""".split()


def build(nc, io):
    ctx = ExitStack()
    with ctx:
        def sb(name, cols, rows=P):
            return ctx.enter_context(nc.sbuf_tensor(name, [rows, cols], FP))

        s = {n: ctx.enter_context(nc.semaphore(n)) for n in SEM_NAMES}
        layer_s = [{n: ctx.enter_context(nc.semaphore(f"{n}_l{l}")) for n in LAYER_SEMS} for l in range(DEPTH)]
        ada_ld, in_ld = (s["ada_ld0"], s["ada_ld1"]), (s["in_ld0"], s["in_ld1"])
        gu_ld, dn_ld = (s["gu_ld0"], s["gu_ld1"]), (s["dn_ld0"], s["dn_ld1"])
        g_used = (s["g_used0"], s["g_used1"])
        gu_used, dn_used = (s["gu_used0"], s["gu_used1"]), (s["dn_used0"], s["dn_used1"])

        const = sb("const", 128 + 64 + 3 * 128 + NE)
        ident, cmask = const[:, 0:128], const[:, 128:192]
        tri, ones = const[:, 192:320], const[:, 320:448]
        slot_row = const[:, 448:576]
        rank16 = const[:, 576:576 + NE]
        rbias = sb("rbias", NE)[:, :]
        x = sb("x", TC * D)[:, :].rearrange("p (c d) -> p c d", c=TC)
        h_t = sb("h", TC * D)
        h = h_t[:, :].rearrange("p (c d) -> p c d", c=TC)
        hT_t = sb("hT", KD * T)
        hT = hT_t[:, :].rearrange("p (k t) -> p k t", k=KD)
        catT = hT
        mods_t = sb("mods", 2 * 6 * D)
        mods = mods_t[:, :].rearrange("p (c v d) -> p c v d", c=2, v=6)
        W = sb("W", 24576)
        E = sb("E", 3584)
        c0_t = sb("c0", 2048)
        c0 = c0_t[0:1, :].rearrange("p (n s f) -> p n s f", n=2, s=2)
        parH = sb("parH", 48)
        parR = sb("parR", 104)
        scT = sb("scT", 16)
        rw = sb("rw", KD * NE)[:, :].rearrange("p (k e) -> p k e", k=KD)
        small = sb("small", 64)
        hyp = sb("hyp", 4, FFN)
        ss, rstd = small[:, 0:3], small[:, 3:6]
        eps_c = small[:, 6:7]
        s_rg = small[:, 8:24]
        gates = sb("gates", TC * NE)[:, :].rearrange("p (c e) -> p c e", c=TC)
        ps = ctx.enter_context(nc.psum_tensor("ps", [P, 8, 512], FP))

        rows_h, rows_r, rows_c = mods_t[0:48, 0:128], mods_t[0:104, 128:256], mods_t[0:16, 256:384]
        rows_s = mods_t[0:16, 384:512]
        ftmp = mods_t[:, 1024:5120].rearrange("p (b f n) -> p b f n", b=2, f=4)
        d_row = mods_t[0:1, 5120:6144].rearrange("p (n f) -> p n f", n=2)
        hid = mods_t[0:FFN, 6144:6144 + 6 * T].rearrange("p (b t) -> p b t", b=6)
        filt_s = h_t[:, :].rearrange("p (c n f) -> p c n f", c=TC, n=2)
        filt_d = hT_t[:, :].rearrange("p (c n f) -> p c n f", c=TC, n=2)
        hid2 = mods_t[:, 7680:7680 + T]
        w3 = E[:, 0:2048]
        decay = E[:, 2048:3584].rearrange("p (c f) -> p c f", c=TC)
        ada_w = W[:, 0:12288].rearrange("p (b n) -> p b n", b=2)
        mrow = W[:, 12288:13824].rearrange("p (b n) -> p b n", b=3)
        adab = W[:, 13824:15360].rearrange("p (b n) -> p b n", b=3)
        gt = W[:, 15360:15872]
        ada_w1 = [mods_t[:, 6144 * b:6144 * b + 2048] for b in range(2)]
        mrow1 = c0_t[:, 0:1536].rearrange("p (b n) -> p b n", b=3)
        gt1 = c0_t[:, 1536:2048]
        z_sb = mods_t[0:EMB, 8448:8448 + T]
        wblk = W[:, 0:8192].rearrange("p (b k n) -> p b k n", b=2, k=KD)
        qkT = W[:, 8192:11264].rearrange("p (m t) -> p m t", m=8)
        v_tok = W[:, 11264:12800].rearrange("p (c n) -> p c n", c=TC)
        hy2T = W[:, 12800:14336].rearrange("p (m t) -> p m t", m=4)
        ck = W[:, 14336:14848]
        cv = W[:, 14848:15360]
        ckT = W[:, 15360:15872].rearrange("p (m t) -> p m t", m=4)
        dft_s = W[:, 15872:16896].rearrange("p (k f) -> p k f", k=2)
        idft_s = W[:, 16896:17920].rearrange("p (k t) -> p k t", k=4)
        dft_p = W[:, 17920:18176]
        idft_p = W[:, 18176:18432].rearrange("p (k t) -> p k t", k=2)
        spec = W[:, 18432:24576].rearrange("p (n a c f) -> p n a c f", n=2, a=2, c=TC)
        hy01T = [mods_t[:, 6144 * b:6144 * b + 4 * T].rearrange("p (m t) -> p m t", m=4) for b in range(2)]
        hy_tok = h_t[:, :].rearrange("p (c a n) -> p c a n", c=TC, a=2)
        prod = W[:, 0:3072].rearrange("p (a c n) -> p a c n", a=2, c=TC)
        ptmp = W[:, 3072:6144].rearrange("p (a c n) -> p a c n", a=2, c=TC)
        bias = E[:, :].rearrange("p (h r k) -> p h r k", h=H, r=7)
        sc_p = W[:, 15872:16896].rearrange("p (h k) -> p h k", h=H)
        sc_s = W[:, 16896:23040].rearrange("p (q h k) -> p q h k", q=2, h=H)
        ptT = ([h_t[:, 512 * j:512 * j + 512] for j in range(6)] + [W[:, 12800 + 512 * j:13312 + 512 * j] for j in range(4)]
               + [E[:, 512 * j:512 * j + 512] for j in range(4)])
        amax = W[:, 23040:23064].rearrange("p (q h) -> p q h", q=3)
        asum = W[:, 23064:23088].rearrange("p (q h) -> p q h", q=3)
        arcp = W[:, 23088:23112].rearrange("p (q h) -> p q h", q=3)
        k_tok = ck
        wout = W[:, 0:8192].rearrange("p (k n) -> p k n", k=KD)
        otmp = W[:, 8192:11264].rearrange("p (c d) -> p c d", c=TC)
        geluT = W[:, 8192:11264].rearrange("p (m t) -> p m t", m=8)
        xrT = W[:, 11264:14336].rearrange("p (m t) -> p m t", m=8)
        rr = h_t[:, :].rearrange("p (m t) -> p m t", m=8)
        ri = W[:, 14336:17408].rearrange("p (m t) -> p m t", m=8)
        ra = W[:, 17408:20480].rearrange("p (m t) -> p m t", m=8)
        rt = W[:, 20480:23552].rearrange("p (m t) -> p m t", m=8)
        bd = [mods_t[:, 6144 * d:6144 * d + 2048].rearrange("p (g m n) -> p g m n", g=2, m=8) for d in range(2)]
        fwd = E[:, 0:8 * T].rearrange("p (m t) -> p m t", m=8)
        spt = W[:, 23552:23552 + 128].rearrange("p (a m) -> p a m", a=8)
        fin_col = W[:, 23680:23696].rearrange("p (d m) -> p d m", d=2)
        fin_row = W[0:16, 23712:23840]
        wg = [W[:, 12288 * b:12288 * b + 4096].rearrange("p (k f) -> p k f", k=KD) for b in range(2)]
        wu = [W[:, 12288 * b + 4096:12288 * b + 8192].rearrange("p (k f) -> p k f", k=KD) for b in range(2)]
        wd = [W[:, 12288 * b + 8192:12288 * b + 12288].rearrange("p (k d) -> p k d", k=KF) for b in range(2)]
        acc = mods[:, 0, 0:3, :]
        mr = mods_t[:, 6144:6144 + 3072]
        silu_h, act_h = (mr[:, 512 * i:512 * i + 512].rearrange("p (r n) -> p r n", r=2) for i in range(2))
        actT_h = mr[:, 1024:1536].rearrange("p (r j n) -> p r j n", r=2, j=2)
        rows_g = mr[:, 1536:2560].rearrange("p (r n) -> p r n", r=2)
        y_h = mods_t[:, 9216:9216 + 2048].rearrange("p (b r n) -> p b r n", b=2, r=2)
        hTg = mods_t[:, 3072:4096].rearrange("p (r k n) -> p r k n", r=2, k=KD)
        place = E[:, 1024:1792].rearrange("p (b c n) -> p b c n", b=2, c=TC)
        posm = E[:, 2560:2608].rearrange("p (c e) -> p c e", c=TC)
        row_f = E[:, 2640:2646].rearrange("p (a c) -> p a c", a=2)
        gate2 = E[:, 2648:2654].rearrange("p (a c) -> p a c", a=2)
        row_i = ctx.enter_context(nc.sbuf_tensor("row_i", [P, 2 * TC], mybir.dt.uint32))
        counts = ctx.enter_context(nc.sbuf_tensor("counts", [1, NE + 1], mybir.dt.int32))
        cnt_f = E[0:1, 2608:2608 + NE + 1]
        y_d = nc.dram_tensor("y_rows", (NE * 2 * CAP, D), FP, kind="Internal").ap()
        zeros = sb("zeros", P)
        mod_d = nc.dram_tensor("mod_rows", (2, 6 * D), FP, kind="Internal").ap()
        back = W[:, 18432:24576].rearrange("p (a c d) -> p a c d", a=2, c=TC)
        total = back[:, 1]
        B_G, B_GU, B_TR, B_DN = (0, 1), (2, 3), 4, (5, 6)
        mt = mods_t[:, 6144:6144 + 3072].rearrange("p (a b n) -> p a b n", a=3, b=2)
        silu_b, act_b, actT_b = mt[:, 0], mt[:, 1], mt[:, 2]
        R = {n: E[:, 48 * i:48 * i + 48].rearrange("p (c e) -> p c e", c=TC)
                   for i, n in enumerate(["sc", "sel", "msk", "eq", "w", "t1", "t2", "m2", "sm"])}
        pr6 = E[:, 512:512 + 72].rearrange("p (c g o) -> p c g o", c=TC, g=NG)
        gsc, geq, gw, gin = (E[:, 600 + 16 * i:612 + 16 * i].rearrange("p (c g) -> p c g", c=TC) for i in range(4))
        r1, r2 = (E[:, 680 + 8 * i:683 + 8 * i].rearrange("p (c o) -> p c o", c=TC) for i in range(2))
        fing = W[:, 0:D]

        block = ctx.enter_context(nc.Block())
        w_in = io["a_in_w"][0].rearrange("(k p) n -> p k n", p=P)
        w_cin = io["c_in_w"][0].rearrange("(k p) n -> p k n", p=P)
        w_aout = io["a_out_w"][0].rearrange("(k p) n -> p k n", p=P)
        w_cout = io["c_out_w"][0].rearrange("(k p) n -> p k n", p=P)
        wg_d = io["moe_w_gate"].rearrange("l e (k p) f -> (l e) p k f", p=P)
        wu_d = io["moe_w_up"].rearrange("l e (k p) f -> (l e) p k f", p=P)
        wd_d = io["moe_w_down"].rearrange("l e (k p) d -> (l e) p k d", p=P)
        IN_ORDER = (3, 4, 5, 0, 1, 2)
        ODD_ORDER = (2, 3, 0, 1)
        MOD0 = 8
        UNITS = ((0, 0), (0, 1), (1, 0), (1, 1))
        NBODY = NE // 2
        BT = 2 * TC

        @block.sync
        def _(sp):
            sp.dma_start(const[:, :], io["k_const"]).then_inc(s["consts_ld"], 16)
            sp.dma_start(rows_c[0:8, :], io["c_ctx"].rearrange("(k p) -> k p", p=P)).then_inc(s["params_ld"], 16)
            sp.dma_start(rows_c[8:16, :], io["c"][0].rearrange("(k p) -> k p", p=P)).then_inc(s["params_ld"], 16)
            sp.dma_start(rows_h[0:36, :], io["hy_short_w"][0].rearrange("j (c p) -> (j c) p", p=P)).then_inc(s["params_ld"], 16)
            sp.dma_start(rows_h[36:48, :], io["hy_short_b"][0].rearrange("(c p) -> c p", p=P)).then_inc(s["params_ld"], 16)
            sp.dma_start(rows_r[0:32, :], io["rg_conv_w"][0].rearrange("j (c p) -> (j c) p", p=P)).then_inc(s["params_ld"], 16)
            sp.dma_start(rows_r[32:40, :], io["rg_conv_b"][0].rearrange("(c p) -> c p", p=P)).then_inc(s["params_ld"], 16)
            for i, n in enumerate(("rg_ba", "rg_bx", "rg_lam", "state_h")):
                sp.dma_start(rows_r[40 + 16 * i:56 + 16 * i, :],
                             io[n][0].rearrange("d (c p) -> (d c) p", p=P) if n != "state_h"
                             else io[n][0, 0].rearrange("d (c p) -> (d c) p", p=P)).then_inc(s["params_ld"], 16)

            def ada0():
                for k in range(KD):
                    if k >= 2:
                        sp.wait_ge(s["ada_mm"], k - 1)
                    sp.dma_start(ada_w[:, k % 2, :], io["ada_w"][0, k * P:(k + 1) * P, :]).then_inc(ada_ld[k % 2], 16)
                    if k == 1:
                        sp.dma_start(x[:, 0, :], io["x_prompt"][0]).then_inc(s["x_ld"], 16)
                        sp.dma_start(x[:, 1:3, :], io["x_sample"][0].rearrange("(c p) d -> p c d", p=P)).then_inc(s["x_ld"], 16)

            def ada1(pieces):
                for p in pieces:
                    b, k = divmod(p, KD)
                    if p >= 2:
                        sp.wait_ge(s["ada_mm"], KD + p - 1)
                    sp.dma_start(ada_w1[p % 2], io["ada_w"][1, k * P:(k + 1) * P, 2048 * b:2048 * b + 2048]).then_inc(ada_ld[p % 2], 16)

            def in_blocks(l, src, order, sems, mm, per):
                for i, nb in enumerate(order):
                    if l == 0 and i < 2:
                        sp.wait_ge(s["ada_mm"], KD - 1 + i)
                    if i >= 2:
                        sp.wait_ge(mm, per[i - 2])
                    sp.dma_start(wblk[:, i % 2], src[:, :, nb * 512:(nb + 1) * 512]).then_inc(sems[i % 2], 16)

            def experts(l):
                sp.wait_ge(s["out_mm"], 6 * (l + 1))
                sp.wait_ge(s["out_x"], TC * (l + 1))
                if l == 1:
                    sp.wait_ge(s["fin_out"], 16)
                with sp.Fori(0, NBODY) as i:
                    for b in range(2):
                        e = i * 2 + (NE * l + b)
                        sp.wait_ge(g_used[b], i + (NBODY * l + 1))
                        sp.dma_start(wg[b], wg_d[e]).then_inc(gu_ld[b], 16)
                        sp.wait_ge(gu_used[b], i + (NBODY * l + 1))
                        sp.dma_start(wu[b], wu_d[e]).then_inc(gu_ld[b], 16)
                        sp.wait_ge(dn_used[b], i + (NBODY * l + 1))
                        sp.dma_start(wd[b], wd_d[e]).then_inc(dn_ld[b], 16)

            ada0()
            in_blocks(0, w_in, IN_ORDER, in_ld, s["in_mm"], (4, 8, 12, 16, 20, 23))
            sp.wait_ge(s["zeros_ok"], 1)
            y_half = y_d.rearrange("(e r a b) d -> e r a (b d)", r=2, a=8, b=CAP // 8)
            for e in range(NE):
                sp.dma_start(y_half[e, 1].rearrange("a (m n) -> a m n", n=P),
                             zeros[0:8, None, :].broadcast_to([8, CAP // 8 * D // P, P])).then_inc(s["zero_st"], 16)
            sp.wait_ge(s["tok_mm"], 6)
            ada1(range(0, 10))
            sp.wait_ge(s["inv_mm"], 7)
            for k, pieces in ((1, range(10, 15)), (0, range(15, 24))):
                sp.dma_start(wout[:, 4 * k:4 * k + 4, :], w_aout[:, 4 * k:4 * k + 4, :]).then_inc(s[f"out_ld{k}"], 16)
                ada1(pieces)
            experts(0)
            sp.wait_ge(gu_used[0], NBODY + 1)
            in_blocks(1, w_cin, ODD_ORDER, in_ld, s["odd_mm"], (4, 8, 12, 16))
            for k in range(2):
                sp.wait_ge(s["odd_mm"], 12 + 4 * k)
                sp.dma_start(wout[:, 4 * k:4 * k + 4, :], w_cout[:, 4 * k:4 * k + 4, :]).then_inc(s[f"out_ld{k}"], 16)
            experts(1)
            sp.wait_ge(gu_used[0], 2 * NBODY + 1)
            sp.dma_start(fing, io["final_g"].rearrange("(o d) -> o d", o=1).broadcast_to([P, D])).then_inc(s["norm_gl"], 16)
            for c in range(TC):
                sp.wait_ge(s["y_ready"], c + 1)
                dst = io["y_prompt"][0] if c == 0 else io["y_sample"][0, (c - 1) * P:c * P]
                sp.dma_start(dst, h[:, c, :]).then_inc(s["y_out"], 16)
            sp.wait_ge(s["y_out"], 16 * TC)
            sp.wait_ge(s["kv_out"], 32)
            sp.wait_ge(s["fin_out"], 16)

        @block.gpsimd
        def _(pool):
            gp = nc.gpsimd
            gp.memset(zeros[:, :], 0.0).then_inc(s["zeros_ok"], 1)
            pool.dma_start(rw, io["router_w"].rearrange("(k p) e -> p k e", p=P)).then_inc(s["rw_ld"], 16)
            pool.dma_start(rbias, io["router_b"].rearrange("(o e) -> o e", o=1).broadcast_to([P, NE])).then_inc(s["rw_ld"], 16)

            def ada_aux(l, rows, bias_rows, g_rows):
                gp.memset(rows, 0.0).then_inc(s["mrow_z"], 1)
                pool.wait_ge(s["mrow_z"], l + 1)
                for c in range(2):
                    for j in range(4):
                        pool.dma_start(bias_rows[32 * j + c:32 * j + c + 1], io["ada_b"][l:l + 1].rearrange(
                            "o (b j n) -> o j b n", b=3, j=4)[:, j]).then_inc(s["ada_aux"], 16)
                    for j, (v, half) in enumerate(((1, 0), (1, 1), (0, 0), (0, 1))):
                        pool.dma_start(g_rows[32 * j + c:32 * j + c + 1, :],
                                       io["norm_g"][l, v:v + 1, half * 512:half * 512 + 512]).then_inc(s["ada_aux"], 16)

            ada_aux(0, mrow, adab, gt)
            pool.wait_ge(s["spec_ev"], 16)
            for n in range(2):
                gp.memset(spec[0:1, n, 1, 0:2, :], 0.0).then_inc(s["spec_fix"], 1)

            pool.wait_ge(s["ada_row"], 3)
            for c in range(2):
                for j in range(4):
                    pool.dma_start(mod_d[c:c + 1].rearrange("o (b j n) -> o j b n", b=3, j=4)[:, j],
                                   mrow[32 * j + c:32 * j + c + 1]).then_inc(s["mod_dma"], 16)
            pool.wait_ge(s["mod_dma"], 16 * 8)
            for c in range(2):
                pool.dma_start(mods[:, c, 2:6, :], mod_d[c:c + 1, 2 * D:6 * D].rearrange("o (v d) -> o v d", v=4)
                               .broadcast_to([P, 4, D])).then_inc(s["mod_dma"], 16)

            pool.wait_ge(s["filt_dec"], 12)
            pool.wait_ge(s["in_mm"], 4)
            rpb = io["na_rpb"]
            for up in range(2):
                for hh in range(H):
                    off = hh * RPB_R * RPB_C + (WIN_ROWS - 4 - up) * RPB_C + WIN_COLS - GRID_W
                    src = bass.AP(tensor=rpb.tensor, offset=off, ap=[[1, GRID_W], [RPB_C, 7], [1, GRID_W]])
                    pool.dma_start(bias[64 * up:64 * up + 64, hh], src).then_inc(s["bias_ld"], 16)
            pool.wait_ge(s["ada_bc"], MOD0)
            pool.dma_start(ck.rearrange("p (h d) -> p h d", h=H), io["cache_k"][0, 0].rearrange("h t d -> t h d")).then_inc(s["cache_ld"], 16)
            pool.dma_start(cv.rearrange("p (h d) -> p h d", h=H), io["cache_v"][0, 0].rearrange("h t d -> t h d")).then_inc(s["cache_ld"], 16)
            pool.wait_ge(s["bias_ld"], 16 * 16)
            for hh in range(H):
                b3 = bias[:, hh]
                gp.tensor_tensor(b3, b3, cmask[:, None, :].broadcast_to([P, 7, GRID_W]), ALU.add).then_inc(s["bias_ok"], 1)

            pool.wait_ge(s["spec_y"], 6)
            ada_aux(1, mrow1, mrow1, gt1)

            def moe_pool(l):
                q = layer_s[l]
                pool.wait_ge(s["zero_st"], 16 * NE)
                pool.wait_ge(s["pos_ready"], l + 1)
                with pool.If(pool.value_load(counts[0:1, NE:NE + 1]) <= 2 * CAP):
                    with pool.Fori(0, NBODY) as i:
                        for b in range(2):
                            e = i * 2 + b
                            n = pool.value_load(counts[0:1, bass.ds(e, 1)])
                            dst = y_d.rearrange("(e r s) (a n) -> e a s r n", r=2, s=CAP, a=2)[bass.ds(e, 1)]
                            with pool.If(n > CAP):
                                pool.wait_ge(q["y_ev"], e + 2)
                                for a in range(2):
                                    pool.dma_start(dst[0, a], y_h[64 * a:64 * a + 64, b]).then_inc(q[f"y_st{b}"], 16)
                            with pool.Else():
                                pool.wait_ge(q["y_ev"], e + 2)
                                for a in range(2):
                                    pool.dma_start(dst[0, a, :, 0:1, :], y_h[64 * a:64 * a + 64, b, 0:1]).then_inc(q[f"y_st{b}"], 16)
                    for b in range(2):
                        pool.wait_ge(q[f"y_st{b}"], 32 * NBODY)
                    for c in range(TC):
                        for a in range(2):
                            gp.indirect_dma_start(back[:, a, c, :], None, y_d,
                                                  bass.IndirectOffsetOnAxis(ap=row_i[:, TC * a + c:TC * a + c + 1], axis=0))\
                              .then_inc(q[f"back_ld{c}"], 16)

            moe_pool(0)
            pool.wait_ge(s["norm_h"], 3 * 3)
            for d in range(2):
                gp.memset(bd[d], 0.0).then_inc(s["bd_zero"], 1)
            pool.wait_ge(s["bd_zero"], 2)
            for d in range(2):
                for g, n in enumerate(("rg_wa", "rg_wx")):
                    src = io[n][0, d].rearrange("(m u) i j -> u i m j", u=2)
                    for u in range(2):
                        pool.dma_start(bd[d][64 * u:64 * u + 64, g, :, 64 * u:64 * u + 64], src[u]).then_inc(s["bd_ld"], 16)
            moe_pool(1)

        @block.tensor
        def _(pe):
            def mm(out, pairs):
                for i, (a, b) in enumerate(pairs):
                    last = nc.tensor.matmul(out, a, b, start=(i == 0), stop=(i == len(pairs) - 1))
                return last

            pe.wait_ge(s["consts_ld"], 16)
            pe.wait_ge(s["params_ld"], 10 * 16)
            nc.tensor.transpose(ps[:, 7, 0:48], rows_h, ident[0:48, 0:48])
            nc.tensor.transpose(ps[:, 7, 64:168], rows_r, ident[0:104, 0:104])
            pe.wait_ge(s["silu_c"], 1)
            nc.tensor.transpose(ps[:, 7, 192:208], rows_s, ident[0:16, 0:16]).then_inc(s["par_tr"], 1)
            pe.wait_ge(s["hyp_ld"], 7 * 16)
            nc.tensor.matmul(ps[0:FFN, 5, 0:T], hid[0:EMB, 5, 0:FFN], z_sb, start=True, stop=True).then_inc(s["net_mm"], 1)
            pe.wait_ge(s["net_sin"], 1)
            nc.tensor.matmul(ps[0:FFN, 6, 0:T], hid[:, 5, 64:128], hid[:, 3, :], start=True, stop=True).then_inc(s["net_mm"], 1)

            def ada0(ks):
                for k in ks:
                    pe.wait_ge(ada_ld[k % 2], 16 * (k // 2 + 1))
                    lhs = scT[:, :].rearrange("p (c k) -> p k c", c=2)[:, k, :]
                    for n in range(N_SLICE):
                        b, j = divmod(n, 4)
                        last = nc.tensor.matmul(ps[32 * j:32 * j + 2, b, :], lhs, ada_w[:, k % 2, n * 512:(n + 1) * 512],
                                                start=(k == 0), stop=(k == KD - 1))
                    last.then_inc(s["ada_mm"], 1)

            def ada1(pieces):
                for p in pieces:
                    b, k = divmod(p, KD)
                    if p == 2 * KD:
                        pe.wait_ge(s["ada_row"], 4)
                    pe.wait_ge(ada_ld[p % 2], 16 * (KD // 2 + p // 2 + 1))
                    lhs = scT[:, :].rearrange("p (c k) -> p k c", c=2)[:, k, :]
                    for j in range(4):
                        last = nc.tensor.matmul(ps[32 * j:32 * j + 2, 7 - b % 2, :], lhs, ada_w1[p % 2][:, j * 512:(j + 1) * 512],
                                                start=(k == 0), stop=(k == KD - 1))
                    last.then_inc(s["ada_mm"], 1)

            def filters(c):
                for f in range(4):
                    t = 4 * c + f
                    if t >= 5:
                        pe.wait_ge(s["filt_dec"], t - 4)
                    mm(ps[:, 3 + t % 5, :], [(hid2[:, c * P:(c + 1) * P], w3[:, f * 512:(f + 1) * 512])]).then_inc(s["filt_mm"], 1)

            def spectra(ts):
                for t in ts:
                    n, i = divmod(t, 8)
                    src, col, c = ((0, 0, 1), (0, 128, 2), (0, 0, 0), (1, 256, 1), (1, 384, 2), (1, 128, 0), (2, 256, 1), (2, 128, 0))[i]
                    filt = filt_d if src == 1 else filt_s
                    m = 1 if src == 2 else P
                    if t >= 5:
                        pe.wait_ge(s["spec_ev"], t - 4)
                    pairs = ([(dft_p[:, col:col + m], filt[:, 0, n, :])] if c == 0 else
                             [(dft_s[:, k, col:col + m], filt[:, 1 + k, n, :]) for k in range(2)])
                    mm(ps[0:m, 3 + t % 5, :], pairs).then_inc(s["spec_mm"], 1)

            pe.wait_ge(s["par_ev"], 1)
            ada0(range(0, 2))
            pe.wait_ge(s["net_sin"], 2)
            pe.wait_ge(s["w3_ld"], 16)
            pe.wait_ge(s["pad_z"], 2)
            for c in range(TC):
                filters(c)
                ada0([2 + c])
            pe.wait_ge(s["tables_ld"], 4 * 16)
            pe.wait_ge(s["filt_dec"], 12)
            pe.wait_ge(s["filt_sd"], 8)
            spectra(range(0, 8))
            ada0(range(5, 7))
            spectra(range(8, 11))
            ada0([7])
            spectra(range(11, 16))

            def broadcast(l, ns, t):
                src = mrow1 if l else mrow
                for n in ns:
                    for c in range(2):
                        b, j = divmod(n, 4)
                        if t >= 5:
                            pe.wait_ge(s["ada_mod"], MOD0 * l + t - 4)
                        nc.tensor.matmul(ps[:, 3 + t % 5, :], ident[:, 32 * j + c:32 * j + c + 1].broadcast_to([P, P]), src[:, b, :],
                                         start=True, stop=True).then_inc(s["ada_bc"], 1)
                        t += 1

            def keep_clock(n, bank):
                for _ in range(n):
                    nc.tensor.matmul(ps[:, bank, :], ident, const[:, 0:512], start=True, stop=True)

            def router(i, c):
                pe.wait_ge(s["rw_ld"], 32)
                pe.wait_ge(s["tr_act"], 3 * i + c + 1)
                pe.wait_ge(s["tr_dve"], 3 * i + c + 1)
                last = mm(ps[:, c, 0:NE], [(hT[:, k, c * P:(c + 1) * P], rw[:, k, :]) for k in range(KD)])
                if c == TC - 1:
                    last.then_inc(s["rt_mm"], 1)

            def transposes(i):
                if i == 1:
                    pe.wait_ge(s["ada_row"], 5)
                keep_clock(5, (2, 6, 2, 7)[i])
                for c in range(TC):
                    pe.wait_ge(s["norm_h"], 3 * i + c + 1)
                    for half in range(2):
                        for k in range(4):
                            last = nc.tensor.transpose(ps[:, 2 * c + half, k * P:(k + 1) * P],
                                                       h[:, c, (4 * half + k) * P:(4 * half + k + 1) * P], ident)
                        last.then_inc(s["tr_mm"], 1)
                    if i % 2 and c:
                        router(i, c - 1)
                if i % 2:
                    router(i, TC - 1)
                pe.wait_ge(s["tr_act"], 3 * i + 3)
                pe.wait_ge(s["tr_dve"], 3 * i + 3)

            def out_proj(t, ks, first, last):
                c, half = divmod(t, 2)
                for k in ks:
                    m_ = nc.tensor.matmul(ps[:, t, :], catT[:, k, c * P:(c + 1) * P], wout[:, k, half * 512:(half + 1) * 512],
                                          start=first and k == ks[0], stop=last and k == ks[-1])
                return m_

            def moe(l):
                pe.wait_ge(s["ada_row"], 6)
                keep_clock(7, 7)
                pe.wait_ge(s["rt_sig"], l + 1)
                q = layer_s[l]
                pe.wait_ge(s["rt_gates"], l + 1)
                for c in range(TC):
                    mm(ps[:, c, 0:NE], [(ones, R["t1"][:, a, :]) for a in range(c)] + [(tri, R["t1"][:, c, :])])
                mm(ps[0:1, 3, 0:NE], [(ones[:, 0:1], R["t1"][:, a, :]) for a in range(TC)]).then_inc(s["pos_mm"], 1)
                keep_clock(3, 7)
                pe.wait_ge(s["pos_ready"], l + 1)
                with pe.If(pe.value_load(counts[0:1, NE:NE + 1]) > 2 * CAP):
                    with pe.Fori(0, NBODY) as i:
                        base = i * BT

                        def gate_up(t):
                            b, c = divmod(t, TC)
                            if c == 0:
                                pe.wait_ge(gu_ld[b], i * 32 + (32 * (NBODY * l + 1)))
                            pe.wait_ge(q["de_act"], base + (t + 1))
                            for w, bank in ((wg[b], 2 * (t % 2)), (wu[b], 2 * (t % 2) + 1)):
                                last = mm(ps[:, bank, :], [(hT[:, k, c * P:(c + 1) * P], w[:, k, :]) for k in range(KD)])
                            last.then_inc(q["de_mm"], 1)
                            if c == TC - 1:
                                pe.drain().then_inc(g_used[b], 1)
                                pe.drain().then_inc(gu_used[b], 1)

                        def down(t):
                            b, c = divmod(t, TC)
                            pe.wait_ge(q["de_act"], base + (t + 3))
                            pe.wait_ge(q["de_actT"], base + (t + 1))
                            for k in range(KF):
                                last = nc.tensor.transpose(ps[:, 4 + t % 2, k * P:(k + 1) * P],
                                                           act_b[:, t % 2, k * P:(k + 1) * P], ident)
                            last.then_inc(q["de_tr"], 1)
                            if c == 0:
                                pe.wait_ge(dn_ld[b], i * 16 + (16 * (NBODY * l + 1)))
                            pe.wait_ge(q["de_actT"], base + (t + 3))
                            pe.wait_ge(q["de_acc"], base + (t + 1))
                            for half in range(2):
                                last = mm(ps[:, 6 + half, :], [(actT_b[:, t % 2, k * P:(k + 1) * P],
                                                                wd[b][:, k, half * 512:(half + 1) * 512]) for k in range(KF)])
                            last.then_inc(q["de_dn"], 1)
                            if c == TC - 1:
                                pe.drain().then_inc(dn_used[b], 1)

                        for t in range(BT):
                            gate_up(t)
                            if t:
                                down(t - 1)
                        down(BT - 1)
                    pe.wait_ge(q["de_acc"], BT * NBODY + 1)

                with pe.Else():
                    def count(e):
                        return pe.value_load(counts[0:1, bass.ds(e, 1)])

                    def gather(e, b, n):
                        pe.wait_ge(q["p_ready"], e + 1)
                        pe.wait_ge(q["g_ev"], e + 1)

                        def half(r):
                            for c in range(TC):
                                for dh in range(2):
                                    last = nc.tensor.matmul(ps[64 * dh:64 * dh + 64, B_G[r], :], place[:, b, c, r * CAP:(r + 1) * CAP],
                                                            h[:, c, 512 * dh:512 * dh + 512], start=(c == 0), stop=(c == TC - 1))
                            return last
                        with pe.If(n > CAP):
                            half(1)
                        half(0).then_inc(q["g_mm"], 1)

                    def gather_transposes(e, n):
                        pe.wait_ge(q["rows_ev"], e + 1)

                        def half(r):
                            for j in range(4):
                                last = nc.tensor.transpose(ps[:, B_G[r], P * j:P * j + P], rows_g[:, r, P * j:P * j + P], ident)
                            return last
                        with pe.If(n > CAP):
                            half(1)
                        half(0).then_inc(q["gt_mm"], 1)

                    def gate_up(i, b, n):
                        e = i * 2 + b
                        pe.wait_ge(gu_ld[b], i * 32 + (32 * (NBODY * l + 1)))
                        pe.wait_ge(q["g_ev"], e + 2)
                        pe.wait_ge(q["act_ready"], e + 1)

                        def half(r):
                            for w, col in ((wg[b], 0), (wu[b], 256)):
                                for k in range(KD):
                                    for fh in range(2):
                                        last = nc.tensor.matmul(ps[64 * fh:64 * fh + 64, B_GU[r], col:col + 256], hTg[:, r, 2 * (k % 4) + k // 4, :],
                                                                w[:, k, 256 * fh:256 * fh + 256], start=(k == 0), stop=(k == KD - 1))
                                if r == 0 and col == 0:
                                    last.then_inc(g_used[b], 1)
                            return last
                        with pe.If(n > CAP):
                            half(1)
                        half(0).then_inc(q["gu_mm"], 1)

                    def act_transposes(e, n):
                        pe.wait_ge(q["act_ready"], e + 2)
                        pe.wait_ge(q["tr_ev"], e + 1)

                        def half(r):
                            for j in range(2):
                                last = nc.tensor.transpose(ps[:, B_TR, 256 * r + 128 * j:256 * r + 128 * j + 128],
                                                           act_h[:, r, 128 * j:128 * j + 128], ident)
                            return last
                        with pe.If(n > CAP):
                            half(1)
                        half(0).then_inc(q["tr_mm"], 1)

                    def down(i, b, n):
                        e = i * 2 + b
                        pe.wait_ge(dn_ld[b], i * 16 + (16 * (NBODY * l + 1)))
                        pe.wait_ge(q["tr_ev"], e + 2)
                        pe.wait_ge(q["y_ev"], e + 1)

                        def half(r):
                            for k in range(KF):
                                for dh in range(2):
                                    last = nc.tensor.matmul(ps[64 * dh:64 * dh + 64, B_DN[r], :],
                                                            actT_h[:, r, k % 2, 64 * (k // 2):64 * (k // 2) + 64],
                                                            wd[b][:, k, 512 * dh:512 * dh + 512], start=(k == 0), stop=(k == KF - 1))
                            return last
                        with pe.If(n > CAP):
                            half(1)
                        half(0).then_inc(q["dn_mm"], 1)

                    def body(i, last=False):
                        n = [count(i * 2), count(i * 2 + 1)]
                        for b in range(2):
                            e = i * 2 + b
                            more = not (last and b == 1)
                            n_next = n[1] if b == 0 else count(e + 1) if more else None
                            gate_up(i, b, n[b])
                            if more:
                                gather(e + 1, 1 - b, n_next)
                            act_transposes(e, n[b])
                            if more:
                                gather_transposes(e + 1, n_next)
                            down(i, b, n[b])

                    n_first = count(0)
                    gather(0, 0, n_first)
                    gather_transposes(0, n_first)
                    with pe.Fori(0, NBODY - 1) as i:
                        body(i)
                    body(NBODY - 1, last=True)
                    pe.wait_ge(q["y_ev"], NE + 1)

            for b in range(2):
                pe.sem_inc(g_used[b], 1)
                pe.sem_inc(gu_used[b], 1)
                pe.sem_inc(dn_used[b], 1)
            for q in layer_s:
                pe.sem_inc(q["de_tr"], 2)
                pe.sem_inc(q["de_dn"], 2)
                pe.sem_inc(q["g_mm"], 2)
                pe.sem_inc(q["gu_mm"], 1)
                pe.sem_inc(q["tr_mm"], 1)
                pe.sem_inc(q["dn_mm"], 1)

            pe.wait_ge(s["spec_ev"], 16)
            pe.wait_ge(s["ada_row"], 3)
            broadcast(0, range(0, MOD0 // 2), 0)
            pe.wait_ge(s["ada_mod"], MOD0)
            transposes(0)
            t = 0
            for i, nb in enumerate(IN_ORDER):
                pe.wait_ge(in_ld[i % 2], 16 * (i // 2 + 1))
                for m in range(3 if nb == 2 else 4):
                    if t >= 8:
                        u = t - 8
                        if u < 12:
                            pe.wait_ge(s["in_dve"], u + 1)
                        else:
                            pe.wait_ge(s["in_act"], u + 1)
                    if nb == 2:
                        mm(ps[:, t % 8, :], [(hT[:, k, m * P:(m + 1) * P], wblk[:, i % 2, k, :]) for k in range(KD)]).then_inc(s["in_mm"], 1)
                    else:
                        mm(ps[:, t % 8, 0:T], [(wblk[:, i % 2, k, m * P:(m + 1) * P], hT[:, k, :]) for k in range(KD)]).then_inc(s["in_mm"], 1)
                    t += 1
            pe.wait_ge(s["in_act"], 23)
            for c in range(TC):
                for a in range(2):
                    for m in range(4):
                        last = nc.tensor.transpose(ps[:, 2 * c + a, m * P:(m + 1) * P], hy01T[a][:, m, c * P:(c + 1) * P], ident)
                    last.then_inc(s["tok_mm"], 1)
            pe.wait_ge(s["cache_ld"], 32)
            for m in range(4):
                last = nc.tensor.transpose(ps[:, 6, m * P:(m + 1) * P], ck[:, m * P:(m + 1) * P], ident)
            last.then_inc(s["cv_mm"], 1)
            for m in range(4):
                last = nc.tensor.transpose(ps[:, 7, m * P:(m + 1) * P], qkT[:, 4 + m, 0:P], ident)
            last.then_inc(s["cv_mm"], 1)
            pe.wait_ge(s["tok_ev"], 6)
            pe.wait_ge(s["cv_ev"], 2)
            pe.wait_ge(s["spec_fix"], 2)
            for n in range(2):
                for c in range(TC):
                    if n == 1:
                        pe.wait_ge(s["inv_ev"], 1 if c == 0 else 3)
                    for a in range(2):
                        if c == 0:
                            pairs = [(dft_p[:, a * 128:a * 128 + 128], hy_tok[:, 0, 0, :])]
                        else:
                            col = 256 * a + 128 * (c - 1)
                            pairs = [(dft_s[:, k, col:col + 128], hy_tok[:, 1 + k, 0, :]) for k in range(2)]
                        mm(ps[:, 3 * a + c, :], pairs).then_inc(s["u_mm"], 1)
                if n == 1:
                    ada1(range(3, 6))
                    pe.wait_ge(s["spec_y"], 6)
                if n == 0:
                    for c in range(TC):
                        pe.wait_ge(s["spec_y"], 1 if c == 0 else 3)
                        if c == 0:
                            pairs = [(idft_p[:, a, :], prod[:, a, 0, :]) for a in range(2)]
                        else:
                            pairs = [(idft_s[:, 2 * a + k, (c - 1) * P:c * P], prod[:, a, 1 + k, :])
                                     for a in range(2) for k in range(2)]
                        mm(ps[:, c, :], pairs).then_inc(s["inv_mm"], 1)
                        if c == 0:
                            ada1(range(0, 2))
                    ada1([2])
                else:
                    for m in range(4):
                        ch = slice(m * P, (m + 1) * P)
                        mm(ps[:, m, 0:LP], [(prod[:, a, 0, ch], idft_p[:, a, :]) for a in range(2)])
                        mm(ps[:, m, LP:T], [(prod[:, a, 1 + k, ch], idft_s[:, 2 * a + k, :])
                                            for a in range(2) for k in range(2)]).then_inc(s["inv_mm"], 1)
                        if m == 1:
                            ada1([6])
            ada1([7])
            pe.wait_ge(s["inv_ev"], 7)
            for hh in range(H):
                r0 = 64 * (hh % 2)
                rows = slice(r0, r0 + 64)
                for q in range(3):
                    t = 3 * hh + q
                    if t % 6 == 5:
                        ada1([8 + t // 6])
                    if t >= 6:
                        pe.wait_ge(s["sc_ev"], t - 5)
                    lhs = qkT[rows, hh // 2, q * P:(q + 1) * P]
                    if q == 0:
                        last = mm(ps[:, t % 6, 0:P], [(lhs, qkT[rows, 4 + hh // 2, 0:P])])
                    else:
                        mm(ps[:, t % 6, 0:LS], [(lhs, qkT[rows, 4 + hh // 2, LP:T])])
                        last = mm(ps[:, t % 6, LS:T], [(lhs, ckT[rows, hh // 2, :])])
                    last.then_inc(s["sc_mm"], 1)
            pe.wait_ge(s["sc_ev"], 24)
            pe.wait_ge(s["out_ld1"], 16)
            for t in range(6):
                out_proj(t, range(4, 8), True, True).then_inc(s["half_mm"], 1)
                if t % 2:
                    ada1([12 + t // 2])
            pe.wait_ge(s["at_nrm"], 3)
            for j in range(14):
                if j >= 6:
                    pe.wait_ge(s["pt_ev"], j - 5)
                else:
                    pe.wait_ge(s["half_ev"], j + 1)
                if j % 4 == 1 and j > 1:
                    ada1([14 + j // 4])
                for k in range(4):
                    hh, i = divmod(4 * j + k, 7)
                    src = (sc_p[:, hh, :] if i == 0 else
                           sc_s[:, (i - 1) // 3, hh, ((i - 1) % 3) * P:((i - 1) % 3 + 1) * P])
                    last = nc.tensor.transpose(ps[:, j % 6, k * P:(k + 1) * P], src, ident)
                last.then_inc(s["pt_mm"], 1)
            pe.wait_ge(s["pt_ev"], 14)

            def pt(hh, i):
                j, k = divmod(7 * hh + i, 4)
                return ptT[j][:, k * P:(k + 1) * P]

            for hh in range(H):
                r0 = 64 * (hh % 2)
                cols = slice(hh * DH, (hh + 1) * DH)
                for q in range(3):
                    t = 3 * hh + q
                    if t >= 6:
                        pe.wait_ge(s["pv_ev"], t - 5)
                    if t % 6 == 5:
                        ada1([18 + t // 6])
                    if q == 0:
                        pairs = [(v_tok[:, 0, cols], pt(hh, 0))]
                    else:
                        pairs = [(v_tok[:, 1, cols], pt(hh, 3 * q - 2)), (v_tok[:, 2, cols], pt(hh, 3 * q - 1)),
                                 (cv[:, cols], pt(hh, 3 * q))]
                    mm(ps[r0:r0 + 64, t % 6, 0:P], pairs).then_inc(s["pv_mm"], 1)
            pe.wait_ge(s["pv_ev"], 24)
            pe.wait_ge(s["out_ld0"], 16)
            for t in range(6):
                out_proj(t, range(0, 4), True, True).then_inc(s["out_mm"], 1)
                if t < 2:
                    ada1([22 + t])
            pe.wait_ge(s["out_ev"], 6)
            transposes(1)
            moe(0)
            broadcast(1, range(0, N_SLICE), 0)
            pe.wait_ge(s["ada_mod"], MOD0 + 2 * N_SLICE)
            transposes(2)

            def odd_tile(t):
                i, m = divmod(t, 4)
                if m == 0:
                    pe.wait_ge(in_ld[i % 2], 16 * (len(IN_ORDER) // 2 + i // 2 + 1))
                if 8 <= t < 12:
                    pe.wait_ge(s["odd_dve"], t - 7)
                elif t >= 12:
                    pe.wait_ge(s["odd_act"], t - 3)
                bank = t if t < 8 else t % 4
                mm(ps[:, bank, 0:T], [(wblk[:, i % 2, k, m * P:(m + 1) * P], hT[:, k, :]) for k in range(KD)]).then_inc(s["odd_mm"], 1)

            def gates_unit(u):
                d, hf = UNITS[u]
                t = 8 * u
                for g in range(2):
                    for m in range(4 * hf, 4 * hf + 4):
                        if t >= 4:
                            pe.wait_ge(s["rg_sig"], t - 3)
                        mm(ps[:, 4 + t % 4, 0:T], [(bd[d][:, g, m, :], xrT[:, m, :])]).then_inc(s["rg_mm"], 1)
                        t += 1

            for t in range(9):
                odd_tile(t)
            pe.wait_ge(s["odd_dve"], 8)
            pe.wait_ge(s["bd_ld"], 8 * 16)
            gates_unit(0)
            odd_tile(9)
            gates_unit(1)
            odd_tile(10)
            odd_tile(11)
            gates_unit(2)
            odd_tile(12)
            odd_tile(13)
            gates_unit(3)
            odd_tile(14)
            odd_tile(15)
            pe.wait_ge(s["odd_act"], 16)
            pe.wait_ge(s["rg_sig"], 32)
            for k in range(2):
                pe.wait_ge(s[f"out_ld{k}"], 32)
                pe.wait_ge(s["odd_y"], k + 1)
                if k == 1:
                    nc.tensor.transpose(ps[0:16, 6, 0:P], fin_col.rearrange("p d m -> p (d m)"), ident).then_inc(s["fin_mm"], 1)
                for t in range(6):
                    m_ = out_proj(t, range(4 * k, 4 * k + 4), k == 0, k == 1)
                    if k == 1:
                        m_.then_inc(s["out_mm"], 1)
            pe.wait_ge(s["out_ev"], 12)
            transposes(3)
            moe(1)

        @block.scalar
        def _(act):
            A = nc.scalar.activation
            act.dma_start(z_sb, io["k_z"]).then_inc(s["hyp_ld"], 16)
            for i, src in enumerate((io["hy_b1"][0], io["hy_b2"][0], io["hy_freq"][0, 0], io["hy_freq"][0, 1])):
                act.dma_start(hyp[:, i:i + 1], src.rearrange("(p o) -> p o", o=1)).then_inc(s["hyp_ld"], 16)
            act.dma_start(hid[0:EMB, 5, 0:FFN], io["hy_w1"][0]).then_inc(s["hyp_ld"], 16)
            act.dma_start(hid[:, 5, 64:128], io["hy_w2"][0]).then_inc(s["hyp_ld"], 16)
            act.dma_start(d_row, io["hy_d"][0:1]).then_inc(s["decay_ld"], 16)
            act.dma_start(decay, io["k_decay"].rearrange("(c p) f -> p c f", p=P)).then_inc(s["decay_ld"], 16)
            act.dma_start(w3[0:FFN, :], io["hy_w3"][0]).then_inc(s["w3_ld"], 16)
            act.dma_start(dft_s, io["k_dft_s"].rearrange("(k p) f -> p k f", p=P)).then_inc(s["tables_ld"], 16)
            act.dma_start(dft_p, io["k_dft_p"]).then_inc(s["tables_ld"], 16)
            act.dma_start(idft_s, io["k_idft_s"].rearrange("(k p) f -> p k f", p=P)).then_inc(s["tables_ld"], 16)
            act.dma_start(idft_p, io["k_idft_p"].rearrange("(k p) f -> p k f", p=P)).then_inc(s["tables_ld"], 16)
            act.wait_ge(s["params_ld"], 10 * 16)
            A(rows_s, rows_c, ACT.Silu).then_inc(s["silu_c"], 1)
            act.wait_ge(s["net_arg"], 1)
            A(hid[:, 3, :], hid[:, 0, :], ACT.Sin).then_inc(s["net_sin"], 1)
            act.wait_ge(s["net_arg"], 2)
            A(hid[:, 4, :], hid[:, 0, :], ACT.Sin).then_inc(s["net_sin"], 1)
            t = 0
            for n in range(2):
                for dst in (spec[:, n, 0, 1, :], spec[:, n, 0, 2, :], spec[:, n, 0, 0, :],
                            spec[:, n, 1, 1, :], spec[:, n, 1, 2, :], spec[:, n, 1, 0, :],
                            c0[:, n, 1, :], c0[:, n, 0, :]):
                    act.wait_ge(s["spec_mm"], t + 1)
                    A(dst, ps[0:dst.shape[0], 3 + t % 5, :], ACT.Copy).then_inc(s["spec_ev"], 1)
                    t += 1

            def modulation(l, ns, t):
                for n in ns:
                    for c in range(2):
                        act.wait_ge(s["ada_bc"], MOD0 * l + t + 1)
                        A(mods_t[:, c * 6 * D + n * 512:c * 6 * D + (n + 1) * 512], ps[:, 3 + t % 5, :], ACT.Copy).then_inc(s["ada_mod"], 1)
                        t += 1

            def sumsq(i, given=None, base=0):
                for c in range(TC):
                    if given is not None:
                        act.wait_ge(given, base + c + 1)
                    A(h[:, c, :], x[:, c, :], ACT.Square, accum_out=ss[:, c:c + 1])
                    act.drain()
                    A(rstd[:, c:c + 1], ss[:, c:c + 1], ACT.Sqrt, bias=eps_c, scale=1.0 / D).then_inc(s["norm_ss"], 1)

            def transposed(i):
                for c in range(TC):
                    act.wait_ge(s["tr_mm"], 6 * i + 2 * c + 1)
                    A(hT[:, 0:4, c * P:(c + 1) * P], ps[:, 2 * c, :].rearrange("p (k t) -> p k t", k=4), ACT.Copy).then_inc(s["tr_act"], 1)

            def moe(l):
                act.wait_ge(s["rt_mm"], l + 1)
                A(R["sc"], ps[:, 0:TC, 0:NE], ACT.Sigmoid).then_inc(s["rt_sig"], 1)
                q = layer_s[l]
                act.wait_ge(s["pos_ready"], l + 1)
                with act.If(act.value_load(counts[0:1, NE:NE + 1]) > 2 * CAP):
                    with act.Fori(0, NBODY) as i:
                        base = i * BT

                        def silu(t):
                            act.wait_ge(q["de_mm"], base + (t + 1))
                            act.wait_ge(q["de_act"], base + (t + 1))
                            A(silu_b[:, t % 2, :], ps[:, 2 * (t % 2), :], ACT.Silu).then_inc(q["de_silu"], 1)

                        def down(t):
                            act.wait_ge(q["de_tr"], base + (t + 3))
                            act.wait_ge(q["de_dn"], base + (t + 1))
                            A(actT_b[:, t % 2, :], ps[:, 4 + t % 2, :], ACT.Copy).then_inc(q["de_actT"], 1)

                        for t in range(BT):
                            silu(t)
                            if t:
                                down(t - 1)
                        down(BT - 1)
                    if l + 1 < DEPTH:
                        act.wait_ge(s["moe_x"], 3)
                        modulation(1, range(0, 10), 0)

                with act.Else():
                    def count(e):
                        return act.value_load(counts[0:1, bass.ds(e, 1)])

                    def rows(e):
                        n = count(e)

                        def half(r):
                            return A(rows_g[:, r, :], ps[:, B_G[r], :], ACT.Copy)
                        with act.If(n > CAP):
                            act.wait_ge(q["g_mm"], e + 3)
                            half(1)
                        act.wait_ge(q["g_mm"], e + 3)
                        half(0).then_inc(q["rows_ev"], 1)

                    def gathered(e):
                        n = count(e)

                        def ready():
                            act.wait_ge(q["gt_mm"], e + 1)
                            act.wait_ge(q["gu_mm"], e + 1)

                        def half(r):
                            return A(hTg[:, r], ps[:, B_G[r], :].rearrange("p (k n) -> p k n", k=KD), ACT.Copy)
                        with act.If(n > CAP):
                            ready()
                            half(1)
                        ready()
                        half(0).then_inc(q["g_ev"], 1)

                    def silu(e, b):
                        n = count(e)
                        act.wait_ge(q["gu_mm"], e + 2)
                        act.sem_inc(gu_used[b], 1)

                        def ready():
                            act.wait_ge(q["gu_mm"], e + 2)
                            act.wait_ge(q["act_ready"], e + 1)
                        with act.If(n > CAP):
                            ready()
                            A(silu_h[:, 1, :], ps[:, B_GU[1], 0:256], ACT.Silu)
                        ready()
                        A(silu_h[:, 0, :], ps[:, B_GU[0], 0:256], ACT.Silu).then_inc(q["silu_ev"], 1)

                    def transposed_act(e):
                        n = count(e)

                        def ready():
                            act.wait_ge(q["tr_mm"], e + 2)
                            act.wait_ge(q["dn_mm"], e + 1)

                        def half(r):
                            return A(actT_h[:, r], ps[:, B_TR, 256 * r:256 * r + 256].rearrange("p (j n) -> p j n", j=2), ACT.Copy)
                        with act.If(n > CAP):
                            ready()
                            half(1)
                        ready()
                        half(0).then_inc(q["tr_ev"], 1)

                    def y_out(i, b, first):
                        e = i * 2 + b
                        n = count(e)
                        act.wait_ge(q["dn_mm"], e + 2)
                        act.sem_inc(dn_used[b], 1)

                        def ready():
                            act.wait_ge(q["dn_mm"], e + 2)
                            if not first:
                                act.wait_ge(q[f"y_st{b}"], i * 32)
                        with act.If(n > CAP):
                            ready()
                            A(y_h[:, b, 1, :], ps[:, B_DN[1], :], ACT.Copy)
                        ready()
                        A(y_h[:, b, 0, :], ps[:, B_DN[0], :], ACT.Copy).then_inc(q["y_ev"], 1)

                    def body(i, first=False, last=False):
                        for b in range(2):
                            e = i * 2 + b
                            silu(e, b)
                            if not (last and b == 1):
                                rows(e + 1)
                            transposed_act(e)
                            if not (last and b == 1):
                                gathered(e + 1)
                            y_out(i, b, first)

                    rows(0)
                    gathered(0)
                    body(0, first=True)
                    with act.Fori(1, NBODY - 1) as i:
                        body(i)
                    body(NBODY - 1, last=True)
                    if l + 1 < DEPTH:
                        modulation(1, range(0, 6), 0)
                    for c in range(TC):
                        act.wait_ge(q[f"back_ld{c}"], 32)
                        A(back[:, 0, c, :], back[:, 0, c, :], ACT.Copy, scale=gate2[:, 0, c:c + 1]).then_inc(q["back_w"], 1)
                        if l + 1 < DEPTH and c < 2:
                            modulation(1, range(6 + 2 * c, 8 + 2 * c), 12 + 4 * c)

            for q in layer_s:
                act.sem_inc(q["de_actT"], 2)
                act.sem_inc(q["g_ev"], 1)
                act.sem_inc(q["tr_ev"], 1)
                act.sem_inc(q["y_ev"], 1)
            act.wait_ge(s["x_ld"], 32)
            act.wait_ge(s["spec_mm"], 16)
            act.wait_ge(s["par_ev"], 2)
            sumsq(0)
            modulation(0, range(0, MOD0 // 2), 0)
            transposed(0)
            for t in range(23):
                act.wait_ge(s["in_mm"], t + 1)
                if t == 8:
                    act.wait_ge(s["mod_dma"], 16 * 8)
                if t < 12:
                    dst = hy01T[t // 4][:, t % 4, :] if t < 8 else hy2T[:, t - 8, :]
                    A(dst, ps[:, t % 8, 0:T], ACT.Identity, bias=parH[:, 36 + t:37 + t], scale=parH[:, 12 + t:13 + t]).then_inc(s["in_act"], 1)
                elif t < 20:
                    A(qkT[:, t - 12, :], ps[:, t % 8, 0:T], ACT.Copy).then_inc(s["in_act"], 1)
                else:
                    A(v_tok[:, t - 20, :], ps[:, t % 8, :], ACT.Copy).then_inc(s["in_act"], 1)
            act.wait_ge(s["in_act"], 23)
            act.dma_start(io["new_v"][0, 0].rearrange("h t d -> t h d"), v_tok[:, 0, :].rearrange("p (h d) -> p h d", h=H)).then_inc(s["kv_out"], 16)
            act.wait_ge(s["cv_mm"], 1)
            A(ckT, ps[:, 6, :].rearrange("p (m t) -> p m t", m=4), ACT.Copy).then_inc(s["cv_ev"], 1)
            act.wait_ge(s["cv_mm"], 2)
            A(k_tok, ps[:, 7, :], ACT.Copy).then_inc(s["cv_ev"], 1)
            act.wait_ge(s["cv_ev"], 2)
            act.dma_start(io["new_k"][0, 0].rearrange("h t d -> t h d"), k_tok.rearrange("p (h d) -> p h d", h=H)).then_inc(s["kv_out"], 16)
            for q in range(3):
                act.wait_ge(s["at_max"], q + 1)
                for hh in range(H):
                    buf = sc_p[:, hh, :] if q == 0 else sc_s[:, q - 1, hh, :]
                    last = A(buf, buf, ACT.Exp, bias=amax[:, q, hh:hh + 1], accum_out=asum[:, q, hh:hh + 1])
                act.drain().then_inc(s["at_exp"], 1)
            act.wait_ge(s["kv_out"], 32)
            for j in range(14):
                act.wait_ge(s["pt_mm"], j + 1)
                A(ptT[j], ps[:, j % 6, :], ACT.Copy).then_inc(s["pt_ev"], 1)
            sumsq(1, s["out_x"], 0)
            transposed(1)
            moe(0)
            sumsq(2, s["moe_x"], 0)
            modulation(1, range(10, N_SLICE), 20)
            transposed(2)
            act.wait_ge(s["rg_lamok"], 1)
            A(spt[:, 1, :], spt[:, 0, :], ACT.Exp, scale=-1.0).then_inc(s["sp_exp"], 1)
            act.wait_ge(s["rg_lamok"], 2)
            A(spt[:, 3, :], spt[:, 2, :], ACT.Ln).then_inc(s["sp_exp"], 1)
            for t in range(8):
                act.wait_ge(s["odd_mm"], t + 1)
                A(xrT[:, t, :], ps[:, t, 0:T], ACT.Identity, bias=parR[:, 32 + t:33 + t], scale=parR[:, 16 + t:17 + t]).then_inc(s["odd_act"], 1)

            def gelu(ts):
                for t in ts:
                    act.wait_ge(s["odd_mm"], t + 9)
                    A(geluT[:, t, :], ps[:, t % 4, 0:T], ACT.Gelu_apprx_tanh).then_inc(s["odd_act"], 1)

            def sigmoids(u):
                d, hf = UNITS[u]
                if u >= 2:
                    act.wait_ge(s["rg_scan"], u - 1)
                for g in range(2):
                    for m in range(4 * hf, 4 * hf + 4):
                        t = 8 * u + 4 * g + m - 4 * hf
                        act.wait_ge(s["rg_mm"], t + 1)
                        dst = (rr if g == 0 else ri)[:, m, :]
                        A(dst, ps[:, 4 + t % 4, 0:T], ACT.Sigmoid, bias=parR[:, 40 + 16 * g + 8 * d + m:41 + 16 * g + 8 * d + m]).then_inc(s["rg_sig"], 1)

            def decays(u):
                d, hf = UNITS[u]
                act.wait_ge(s["rg_lamok"], 3)
                act.wait_ge(s["rg_sig"], 8 * u + 8)
                for m in range(4 * hf, 4 * hf + 4):
                    A(ra[:, m, :], rr[:, m, :], ACT.Exp, scale=s_rg[:, 8 * d + m:8 * d + m + 1]).then_inc(s["rg_a"], 1)
                for m in range(4 * hf, 4 * hf + 4):
                    A(rt[:, m, :], rr[:, m, :], ACT.Tanh, scale=s_rg[:, 8 * d + m:8 * d + m + 1]).then_inc(s["rg_a"], 1)

            def root(u):
                hf = UNITS[u][1]
                act.wait_ge(s["rg_b"], u + 1)
                A(rt[:, 4 * hf:4 * hf + 4, :], rt[:, 4 * hf:4 * hf + 4, :], ACT.Sqrt).then_inc(s["rg_sq"], 1)

            sigmoids(0)
            decays(0)
            sigmoids(1)
            root(0)
            decays(1)
            gelu(range(0, 3))
            sigmoids(2)
            root(1)
            decays(2)
            gelu(range(3, 6))
            sigmoids(3)
            root(2)
            decays(3)
            gelu(range(6, 8))
            root(3)
            act.wait_ge(s["fin_mm"], 1)
            A(fin_row, ps[0:16, 6, 0:P], ACT.Copy).then_inc(s["fin_ev"], 1)
            act.wait_ge(s["fin_ev"], 1)
            act.dma_start(io["new_h"][0, 0].rearrange("d (m p) -> (d m) p", p=P), fin_row).then_inc(s["fin_out"], 16)
            sumsq(3, s["out_x"], TC)
            transposed(3)
            act.wait_ge(s["fin_out"], 16)
            moe(1)
            sumsq(4, s["moe_x"], TC)

        @block.vector
        def _(v):
            V = nc.vector
            V.memset(eps_c, EPS)
            V.memset(hid2[FFN:P, :], 0.0).then_inc(s["pad_z"], 1)
            V.memset(w3[FFN:P, :], 0.0).then_inc(s["pad_z"], 1)
            for q in layer_s:
                v.sem_inc(q["de_act"], 2)
                v.sem_inc(q["de_acc"], 1)
                v.sem_inc(q["act_ready"], 1)
            v.wait_ge(s["par_tr"], 1)
            V.tensor_copy(parH[:, :], ps[:, 7, 0:48])
            V.tensor_copy(parR[:, :], ps[:, 7, 64:168])
            V.tensor_copy(scT[:, :], ps[:, 7, 192:208]).then_inc(s["par_ev"], 2)
            v.wait_ge(s["hyp_ld"], 7 * 16)
            for i, bank in enumerate((5, 6)):
                v.wait_ge(s["net_mm"], i + 1)
                a, b, k = hid[:, 0, :], hid[:, 1, :], hid[:, 2, :]
                if i == 1:
                    v.wait_ge(s["net_sin"], 1)
                V.tensor_scalar(a, ps[0:FFN, bank, 0:T], hyp[:, i:i + 1], hyp[:, 2 + i:3 + i], ALU.add, ALU.mult)
                v.drain()
                V.tensor_scalar(b, a, 1.0 / TWO_PI, ROUND, ALU.mult, ALU.add)
                v.drain()
                V.tensor_scalar(k, b, ROUND, None, ALU.subtract)
                v.drain()
                V.scalar_tensor_tensor(b, k, -PI1, a, ALU.mult, ALU.add)
                v.drain()
                V.scalar_tensor_tensor(a, k, -PI2, b, ALU.mult, ALU.add)
                v.drain()
                V.tensor_scalar(a, a, 3.1415925, -3.1415925, ALU.min, ALU.max).then_inc(s["net_arg"], 1)
            v.wait_ge(s["decay_ld"], 32)
            for c in range(TC):
                for f in range(4):
                    t = 4 * c + f
                    v.wait_ge(s["filt_mm"], t + 1)
                    V.tensor_tensor(ftmp[:, c % 2, f, :], ps[:, 3 + t % 5, :], decay[:, c, :], ALU.mult).then_inc(s["filt_dec"], 1)
                v.drain()
                for n in range(2):
                    f0, f1 = ftmp[:, c % 2, 2 * n, :], ftmp[:, c % 2, 2 * n + 1, :]
                    V.tensor_tensor(filt_s[:, c, n, :], f0, f1, ALU.add)
                    V.tensor_tensor(filt_d[:, c, n, :], f0, f1, ALU.subtract).then_inc(s["filt_sd"], 1)
            v.drain()
            for c in range(2):
                V.tensor_tensor(filt_s[0:1, c, :, :], filt_s[0:1, c, :, :], d_row, ALU.add).then_inc(s["filt_sd"], 1)

            def ada_rows(l, b, rows, bias_rows, g_rows):
                v.wait_ge(s["mrow_z"], l + 1)
                v.wait_ge(s["ada_aux"], 256 * (l + 1))
                v.wait_ge(s["ada_mm"], KD if l == 0 else KD + KD * (b + 1))
                bank = 7 - b % 2 if l else b
                for j in range(4):
                    r = slice(32 * j, 32 * j + 2)
                    V.tensor_tensor(rows[r, b, :], ps[r, bank, :], bias_rows[r, b, :], ALU.add)
                v.drain()
                for j in {0: (2, 3), 1: (), 2: (0, 1)}[b]:
                    r = slice(32 * j, 32 * j + 2)
                    V.scalar_tensor_tensor(rows[r, b, :], rows[r, b, :], 1.0, g_rows[r, :], ALU.add, ALU.mult)
                v.drain().then_inc(s["ada_row"], 1)

            def norm(i, lo):
                for cond, c0_, c1_ in SUBS:
                    for c in range(c0_, c1_):
                        v.wait_ge(s["norm_ss"], 3 * i + c + 1)
                        V.reciprocal(rstd[:, c:c + 1], rstd[:, c:c + 1])
                        v.drain()
                        V.scalar_tensor_tensor(h[:, c, :], x[:, c, :], rstd[:, c:c + 1], mods[:, cond, lo + 1, :], ALU.mult, ALU.mult)
                        v.drain()
                        V.tensor_tensor(h[:, c, :], h[:, c, :], mods[:, cond, lo, :], ALU.add).then_inc(s["norm_h"], 1)

            def transposed(i):
                for c in range(TC):
                    v.wait_ge(s["tr_mm"], 6 * i + 2 * c + 2)
                    V.tensor_copy(hT[:, 4:8, c * P:(c + 1) * P], ps[:, 2 * c + 1, :].rearrange("p (k t) -> p k t", k=4)).then_inc(s["tr_dve"], 1)

            def gated(l):
                for c in range(TC):
                    for half in range(2):
                        cols = slice(half * 512, (half + 1) * 512)
                        v.wait_ge(s["out_mm"], 6 * l + 2 * c + half + 1)
                        src = ps[:, 2 * c + half, :]
                        if l == 0:
                            V.tensor_tensor(otmp[:, c, cols], src, otmp[:, c, cols], ALU.add).then_inc(s["out_ev"], 1)
                            v.drain()
                            V.tensor_tensor(otmp[:, c, cols], otmp[:, c, cols], mods[:, min(c, 1), 2, cols], ALU.mult)
                        else:
                            V.tensor_tensor(otmp[:, c, cols], src, mods[:, min(c, 1), 2, cols], ALU.mult).then_inc(s["out_ev"], 1)
                    v.drain()
                    V.tensor_tensor(x[:, c, :], x[:, c, :], otmp[:, c, :], ALU.add).then_inc(s["out_x"], 1)

            def first_max(dst, vals, mx, rank, n):
                V.tensor_reduce(mx, vals, AX.X, ALU.max)
                v.drain()
                V.tensor_tensor(dst, vals, mx.broadcast_to([P, TC, n]), ALU.is_equal)
                v.drain()
                V.tensor_tensor(dst, dst, rank, ALU.mult)
                v.drain()
                V.tensor_reduce(mx, dst, AX.X, ALU.max)
                v.drain()
                V.tensor_tensor(dst, dst, mx.broadcast_to([P, TC, n]), ALU.is_equal)
                v.drain()

            def router(l):
                v.wait_ge(s["rt_sig"], l + 1)
                v.wait_ge(s["rw_ld"], 32)
                rk = rank16[:, None, :].broadcast_to([P, TC, NE])
                V.tensor_tensor(R["sel"], R["sc"], rbias[:, None, :].broadcast_to([P, TC, NE]), ALU.add)
                v.drain()
                g4 = R["sel"].rearrange("p c (g o) -> p c g o", g=NG)
                for i, (a, b) in enumerate(((0, 1), (0, 2), (0, 3), (1, 2), (1, 3), (2, 3))):
                    V.tensor_tensor(pr6[:, :, :, i], g4[:, :, :, a], g4[:, :, :, b], ALU.add)
                v.drain()
                V.tensor_reduce(gsc, pr6, AX.X, ALU.max)
                v.drain()
                first_max(gin, gsc, r1, rk[:, :, 0:NG], NG)
                V.tensor_scalar(geq, gin, 1.0, BIG, ALU.subtract, ALU.mult)
                v.drain()
                m4 = R["msk"].rearrange("p c (g o) -> p c g o", g=NG)
                for o in range(EPG):
                    V.tensor_tensor(m4[:, :, :, o], g4[:, :, :, o], gin, ALU.mult)
                v.drain()
                for o in range(EPG):
                    V.tensor_tensor(m4[:, :, :, o], m4[:, :, :, o], geq, ALU.add)
                v.drain()
                first_max(R["t1"], R["msk"], r1, rk, NE)
                V.scalar_tensor_tensor(R["m2"], R["t1"], -2 * BIG, R["msk"], ALU.mult, ALU.add)
                v.drain()
                first_max(R["t2"], R["m2"], r1, rk, NE)
                V.tensor_copy(R["w"], R["t1"])
                v.drain()
                V.tensor_tensor(R["t1"], R["t1"], R["t2"], ALU.add)
                v.drain()
                V.tensor_tensor(R["sm"], R["t1"], R["sc"], ALU.mult)
                v.drain()
                V.tensor_reduce(r2, R["sm"], AX.X, ALU.add)
                v.drain()
                V.reciprocal(r2, r2)
                v.drain()
                V.tensor_tensor(gates, R["sm"], r2.broadcast_to([P, TC, NE]), ALU.mult).then_inc(s["rt_gates"], 1)
                v.drain()

            def moe(l):
                router(l)
                gates_e = gates.rearrange("p c e -> p (c e)")
                q = layer_s[l]
                v.wait_ge(s["pos_mm"], l + 1)
                rk_ = rank16[:, None, :].broadcast_to([P, TC, NE])
                V.tensor_tensor(posm, R["t1"], ps[:, 0:TC, 0:NE], ALU.mult)
                V.tensor_copy(cnt_f[:, 0:NE], ps[0:1, 3, 0:NE])
                v.drain()
                V.tensor_scalar(posm, posm, -1.0, None, ALU.add)
                V.tensor_reduce(cnt_f[:, NE:NE + 1], cnt_f[:, 0:NE], AX.X, ALU.max)
                v.drain()
                V.tensor_copy(counts[:, :], cnt_f)
                v.drain().then_inc(s["pos_ready"], 1)
                posm_e = posm.rearrange("p c e -> p (c e)")

                def gated_sum(c):
                    v.drain()
                    V.tensor_tensor(total[:, c, :], total[:, c, :], mods[:, min(c, 1), 5, :], ALU.mult)
                    v.drain()
                    V.tensor_tensor(x[:, c, :], x[:, c, :], total[:, c, :], ALU.add).then_inc(s["moe_x"], 1)

                with v.If(v.value_load(counts[0:1, NE:NE + 1]) > 2 * CAP):
                    V.memset(acc, 0.0)
                    v.drain()
                    with v.Fori(0, NBODY) as i:
                        base = i * BT

                        def act_(t):
                            b, c = divmod(t, TC)
                            v.wait_ge(q["de_silu"], base + (t + 1))
                            v.wait_ge(q["de_tr"], base + (t + 1))
                            V.scalar_tensor_tensor(act_b[:, t % 2, :], silu_b[:, t % 2, :], gates_e[:, bass.ds(i * 2 + (NE * c + b), 1)],
                                                   ps[:, 2 * (t % 2) + 1, :], ALU.mult, ALU.mult).then_inc(q["de_act"], 1)

                        def sum_(t):
                            c = t % TC
                            v.wait_ge(q["de_dn"], base + (t + 3))
                            a = acc[:, c, :].rearrange("p (a n) -> p a n", a=2)
                            V.tensor_tensor(a, a, ps[:, 6:8, :], ALU.add).then_inc(q["de_acc"], 1)

                        for t in range(BT):
                            act_(t)
                            if t:
                                sum_(t - 1)
                        sum_(BT - 1)
                    v.drain()
                    V.tensor_copy(total, acc)
                    for c in range(TC):
                        gated_sum(c)
                with v.Else():
                    def count(e):
                        return v.value_load(counts[0:1, bass.ds(e, 1)])

                    def places(e, b):
                        v.wait_ge(q["g_mm"], e + 1)
                        for c in range(TC):
                            last = V.tensor_scalar(place[:, b, c, :], slot_row, posm_e[:, bass.ds(e + NE * c, 1)], None, ALU.is_equal)
                        last.then_inc(q["p_ready"], 1)

                    def act_(e):
                        n = count(e)

                        def ready():
                            v.wait_ge(q["silu_ev"], e + 1)
                            v.wait_ge(q["tr_mm"], e + 1)

                        def half(r):
                            return V.tensor_tensor(act_h[:, r, :], silu_h[:, r, :], ps[:, B_GU[r], 256:512], ALU.mult)
                        with v.If(n > CAP):
                            ready()
                            half(1)
                        ready()
                        half(0).then_inc(q["act_ready"], 1)

                    def body(i, last=False):
                        for b in range(2):
                            e = i * 2 + b
                            if not (last and b == 1):
                                places(e + 1, 1 - b)
                            act_(e)

                    places(0, 0)
                    V.tensor_scalar(R["sm"], rk_, -2.0 * CAP, 2.0 * CAP * NE, ALU.mult, ALU.add)
                    v.drain()
                    V.tensor_tensor(R["sm"], R["sm"], posm, ALU.add)
                    v.drain()
                    for a, hot in enumerate((R["w"], R["t2"])):
                        V.tensor_tensor(R["eq"], R["sm"], hot, ALU.mult)
                        V.tensor_tensor(R["msk"], gates, hot, ALU.mult)
                        v.drain()
                        V.tensor_reduce(row_f[:, a, :], R["eq"], AX.X, ALU.add)
                        V.tensor_reduce(gate2[:, a, :], R["msk"], AX.X, ALU.add)
                        v.drain()
                    V.tensor_copy(row_i[:, :], row_f.rearrange("p a c -> p (a c)"))
                    v.drain()
                    with v.Fori(0, NBODY - 1) as i:
                        body(i)
                    body(NBODY - 1, last=True)
                    for c in range(TC):
                        v.wait_ge(q["back_w"], c + 1)
                        V.scalar_tensor_tensor(total[:, c, :], back[:, 1, c, :], gate2[:, 1, c:c + 1], back[:, 0, c, :], ALU.mult, ALU.add)
                        gated_sum(c)

            for b in range(3):
                ada_rows(0, b, mrow, adab, gt)
            v.wait_ge(s["ada_mod"], 8)
            norm(0, 0)
            transposed(0)
            for t in range(12):
                dst = hy01T[t // 4][:, t % 4, :] if t < 8 else hy2T[:, t - 8, :]
                v.wait_ge(s["in_act"], t + 1)
                for lo, hi in SEGS:
                    V.scalar_tensor_tensor(dst[:, lo + 1:hi], ps[:, t % 8, lo:hi - 1], parH[:, t:t + 1],
                                           dst[:, lo + 1:hi], ALU.mult, ALU.add)
                v.drain()
                for lo, hi in SEGS:
                    last = V.scalar_tensor_tensor(dst[:, lo:hi - 1], ps[:, t % 8, lo + 1:hi], parH[:, 24 + t:25 + t],
                                                  dst[:, lo:hi - 1], ALU.mult, ALU.add)
                last.then_inc(s["in_dve"], 1)
            for t in range(6):
                v.wait_ge(s["tok_mm"], t + 1)
                V.tensor_copy(hy_tok[:, t // 2, t % 2, :], ps[:, t, :]).then_inc(s["tok_ev"], 1)
            for n in range(2):
                v.wait_ge(s["spec_fix"], 2)
                for c in range(TC):
                    v.wait_ge(s["u_mm"], 6 * n + 2 * c + 2)
                    if n == 1:
                        v.wait_ge(s["inv_mm"], 3)
                    Ur, Ui = ps[:, c, :], ps[:, 3 + c, :]
                    A_, B_ = spec[:, n, 0, c], spec[:, n, 1, c]
                    V.tensor_tensor(ptmp[:, 0, c], Ur, A_, ALU.mult)
                    V.tensor_tensor(ptmp[:, 1, c], Ui, B_, ALU.mult)
                    v.drain()
                    V.tensor_tensor(prod[:, 0, c], ptmp[:, 0, c], ptmp[:, 1, c], ALU.subtract)
                    v.drain()
                    V.tensor_tensor(ptmp[:, 0, c], Ur, B_, ALU.mult)
                    V.tensor_tensor(ptmp[:, 1, c], Ui, A_, ALU.mult)
                    v.drain()
                    last = V.tensor_tensor(prod[:, 1, c], ptmp[:, 0, c], ptmp[:, 1, c], ALU.add)
                    if c < 2:
                        v.drain()
                        last = V.tensor_tensor(prod[0:1, 1, c], ps[0:1, 3 + c], c0[:, n, c], ALU.mult)
                    last.then_inc(s["spec_y"], 1)
                if n == 0:
                    for c in range(TC):
                        v.wait_ge(s["inv_mm"], c + 1)
                        V.tensor_tensor(hy_tok[:, c, 0, :], ps[:, c, :], hy_tok[:, c, 1, :], ALU.mult).then_inc(s["inv_ev"], 1)
                else:
                    for m in range(4):
                        v.wait_ge(s["inv_mm"], 4 + m)
                        V.tensor_tensor(catT[:, 4 + m, :], ps[:, m, 0:T], hy2T[:, m, :], ALU.mult).then_inc(s["inv_ev"], 1)
            v.wait_ge(s["bias_ok"], H)
            for hh in range(H):
                for q in range(3):
                    t = 3 * hh + q
                    v.wait_ge(s["sc_mm"], t + 1)
                    if q == 0:
                        V.tensor_scalar(sc_p[:, hh, :], ps[:, t % 6, 0:P], SCALE, None, ALU.mult).then_inc(s["sc_ev"], 1)
                    else:
                        b0 = 3 - 2 * (q - 1)
                        V.scalar_tensor_tensor(sc_s[:, q - 1, hh, 0:LS].rearrange("p (r k) -> p r k", r=4),
                                               ps[:, t % 6, 0:LS].rearrange("p (r k) -> p r k", r=4), SCALE,
                                               bias[:, hh, b0:b0 + 4, ::-1], ALU.mult, ALU.add)
                        V.tensor_scalar(sc_s[:, q - 1, hh, LS:T], ps[:, t % 6, LS:T], SCALE, None, ALU.mult).then_inc(s["sc_ev"], 1)
            v.drain()
            for q in range(3):
                V.tensor_reduce(amax[:, q, :], sc_p if q == 0 else sc_s[:, q - 1], AX.X, ALU.max)
                v.drain()
                V.tensor_scalar(amax[:, q, :], amax[:, q, :], -1.0, None, ALU.mult).then_inc(s["at_max"], 1)
            for q in range(3):
                v.wait_ge(s["at_exp"], q + 1)
                V.reciprocal(arcp[:, q, :], asum[:, q, :])
                v.drain()
                buf = sc_p if q == 0 else sc_s[:, q - 1]
                V.tensor_tensor(buf, buf, arcp[:, q, :, None].broadcast_to([P, H, P if q == 0 else T]), ALU.mult).then_inc(s["at_nrm"], 1)
            for t in range(6):
                v.wait_ge(s["half_mm"], t + 1)
                V.tensor_copy(otmp[:, t // 2, (t % 2) * 512:(t % 2) * 512 + 512], ps[:, t, :]).then_inc(s["half_ev"], 1)
            ada_rows(1, 0, mrow1, mrow1, gt1)
            for hh in range(H):
                r0 = 64 * (hh % 2)
                for q in range(3):
                    t = 3 * hh + q
                    v.wait_ge(s["pv_mm"], t + 1)
                    V.tensor_copy(catT[r0:r0 + 64, hh // 2, q * P:(q + 1) * P], ps[r0:r0 + 64, t % 6, 0:P]).then_inc(s["pv_ev"], 1)
            ada_rows(1, 1, mrow1, mrow1, gt1)
            v.wait_ge(s["mod_dma"], 16 * 10)
            gated(0)
            norm(1, 3)
            transposed(1)
            ada_rows(1, 2, mrow1, mrow1, gt1)
            moe(0)
            v.wait_ge(s["ada_mod"], MOD0 + 8)
            norm(2, 0)
            transposed(2)
            lam = parR[:, 72:88]
            V.tensor_scalar(spt[:, 4, :], lam, -1.0, None, ALU.mult)
            v.drain()
            V.tensor_tensor(spt[:, 0, :], lam, spt[:, 4, :], ALU.max).then_inc(s["rg_lamok"], 1)
            v.wait_ge(s["sp_exp"], 1)
            V.tensor_scalar(spt[:, 2, :], spt[:, 1, :], 1.0, None, ALU.add).then_inc(s["rg_lamok"], 1)
            v.wait_ge(s["sp_exp"], 2)
            V.tensor_scalar(spt[:, 5, :], spt[:, 2, :], -1.0, 1e-30, ALU.add, ALU.max)
            v.drain()
            V.reciprocal(spt[:, 6, :], spt[:, 5, :])
            V.tensor_tensor(spt[:, 3, :], spt[:, 3, :], spt[:, 1, :], ALU.mult)
            v.drain()
            V.tensor_tensor(spt[:, 3, :], spt[:, 3, :], spt[:, 6, :], ALU.mult)
            V.tensor_scalar(spt[:, 7, :], spt[:, 2, :], 1.0, None, ALU.is_equal)
            v.drain()
            V.tensor_tensor(spt[:, 7, :], spt[:, 7, :], spt[:, 1, :], ALU.mult)
            v.drain()
            V.tensor_tensor(spt[:, 3, :], spt[:, 3, :], spt[:, 7, :], ALU.add)
            V.tensor_scalar(spt[:, 4, :], spt[:, 4, :], 0.0, None, ALU.max)
            v.drain()
            V.tensor_tensor(spt[:, 3, :], spt[:, 3, :], spt[:, 4, :], ALU.add)
            v.drain()
            V.tensor_scalar(s_rg, spt[:, 3, :], -8.0, None, ALU.mult).then_inc(s["rg_lamok"], 1)
            for t in range(8):
                dst = xrT[:, t, :]
                v.wait_ge(s["odd_act"], t + 1)
                for tap, sh in ((0, -2), (1, -1), (3, 1)):
                    for lo, hi in SEGS:
                        a, b = max(lo, lo - sh), min(hi, hi - sh)
                        last = V.scalar_tensor_tensor(dst[:, a:b], ps[:, t, a + sh:b + sh], parR[:, 8 * tap + t:8 * tap + t + 1],
                                                      dst[:, a:b], ALU.mult, ALU.add)
                    if tap != 3:
                        v.drain()
                last.then_inc(s["odd_dve"], 1)

            def unit_mul(u):
                ms = slice(4 * UNITS[u][1], 4 * UNITS[u][1] + 4)
                v.wait_ge(s["rg_sig"], 8 * u + 8)
                V.tensor_tensor(ri[:, ms], ri[:, ms], xrT[:, ms], ALU.mult)

            def unit_square(u):
                ms = slice(4 * UNITS[u][1], 4 * UNITS[u][1] + 4)
                v.wait_ge(s["rg_a"], 8 * u + 8)
                V.tensor_tensor(rr[:, ms], ra[:, ms], ra[:, ms], ALU.mult)
                v.drain()
                V.scalar_tensor_tensor(rt[:, ms], rr[:, ms], 1.0, rt[:, ms], ALU.add, ALU.mult)
                v.drain()
                V.tensor_scalar(rt[:, ms], rt[:, ms], -1.0, 0.0, ALU.mult, ALU.max).then_inc(s["rg_b"], 1)

            def unit_scan(u):
                d, hf = UNITS[u]
                ms = slice(4 * hf, 4 * hf + 4)
                v.wait_ge(s["rg_sq"], u + 1)
                V.tensor_tensor(ri[:, ms], ri[:, ms], rt[:, ms], ALU.mult)
                v.drain()
                out = fwd if d == 0 else rr
                for m in range(4 * hf, 4 * hf + 4):
                    for lo, hi in SEGS:
                        init = 0.0 if lo == 0 else parR[:, 88 + 8 * d + m:89 + 8 * d + m]
                        o_, a_, b_ = out[:, m, lo:hi], ra[:, m, lo:hi], ri[:, m, lo:hi]
                        if d == 1:
                            o_, a_, b_ = o_[:, ::-1], a_[:, ::-1], b_[:, ::-1]
                        V.tensor_tensor_scan(o_, a_, b_, init, ALU.mult, ALU.add)
                v.drain()
                V.tensor_copy(fin_col[:, d, ms], out[:, ms, LP - 1] if d == 0 else out[:, ms, 0])
                v.drain().then_inc(s["rg_scan"], 1)

            def joined(hf):
                ms = slice(4 * hf, 4 * hf + 4)
                V.tensor_tensor(fwd[:, ms], fwd[:, ms], rr[:, ms], ALU.add)
                v.wait_ge(s["odd_mm"], 16)
                v.wait_ge(s["odd_act"], 12 + 4 * hf)
                v.drain()
                V.tensor_tensor(catT[:, ms], fwd[:, ms], geluT[:, ms], ALU.mult).then_inc(s["odd_y"], 1)

            unit_mul(0)
            unit_square(0)
            for u in range(3):
                unit_scan(u)
                unit_mul(u + 1)
                unit_square(u + 1)
            joined(0)
            unit_scan(3)
            joined(1)
            gated(1)
            norm(3, 3)
            transposed(3)
            moe(1)
            v.wait_ge(s["norm_gl"], 16)
            for c in range(TC):
                v.wait_ge(s["norm_ss"], 3 * 4 + c + 1)
                V.reciprocal(rstd[:, c:c + 1], rstd[:, c:c + 1])
                v.drain()
                V.scalar_tensor_tensor(h[:, c, :], x[:, c, :], rstd[:, c:c + 1], fing, ALU.mult, ALU.mult).then_inc(s["y_ready"], 1)


_INS = ["x_prompt", "x_sample", "cache_k", "cache_v", "state_h", "c", "c_ctx", "norm_g", "ada_w", "ada_b",
        "final_g", "a_in_w", "a_out_w", "na_rpb", "hy_short_w", "hy_short_b", "hy_w1", "hy_b1", "hy_w2",
        "hy_b2", "hy_w3", "hy_freq", "hy_d", "c_in_w", "c_out_w", "rg_conv_w", "rg_conv_b", "rg_wa", "rg_ba",
        "rg_wx", "rg_bx", "rg_lam", "router_w", "router_b", "moe_w_gate", "moe_w_up", "moe_w_down"]
_OUTS = [("y_prompt", (1, LP, D)), ("y_sample", (1, LS, D)), ("new_k", (1, 1, H, LP, DH)),
         ("new_v", (1, 1, H, LP, DH)), ("new_h", (1, 1, 2, D))]


def kernel(**inputs):
    import concourse.bacc as bacc
    from concourse.bass_utils import run_bass_kernel_spmd

    nc = bacc.Bacc("TRN2", target_bir_lowering=False, num_devices=1)
    arrays, io = {}, {}
    for name in _INS:
        a = np.asarray(inputs[name])
        if name == "na_rpb":
            a = a[..., ::-1]
        a = np.ascontiguousarray(a)
        arrays["in_" + name] = a
        io[name] = nc.dram_tensor("in_" + name, a.shape, mybir.dt.from_np(a.dtype), kind="ExternalInput").ap()
    for name, a in shape_constants().items():
        a = np.ascontiguousarray(a)
        arrays[name] = a
        io[name] = nc.dram_tensor(name, a.shape, FP, kind="ExternalInput").ap()
    for name, shape in _OUTS:
        io[name] = nc.dram_tensor("out_" + name, shape, FP, kind="ExternalOutput").ap()
    build(nc, io)
    r = run_bass_kernel_spmd(nc, [arrays], core_ids=[0])
    return tuple(r.results[0]["out_" + name] for name, _ in _OUTS)
```
